# Optimizing a Trainium2 kernel written in Bass

```python
import math
import jax, jax.numpy as jnp
from jax import lax
import numpy as np

D_MODEL = 1024
BATCH = 1
SEQ = 256
DEPTH = 2

F32 = jnp.float32
EPS = 1e-6
MEM_LEN = 256
MAX_POS_OFFSET = 1024
SSM_WIDTH = 512
SSM_GROUP = 16
SSM_GROUPS = SSM_WIDTH // SSM_GROUP
SSM_STATE = 64
DT_MIN = 1e-3
DT_MAX = 1e-1
ATT_HEAD_DIM = 64
ATT_SLOTS = 4
DIL_PAIRS = ((128, 1), (512, 4), (2048, 16))
N_DIL = len(DIL_PAIRS)
ATT_HEADS = ATT_SLOTS * N_DIL
ATT_WIDTH = ATT_HEADS * ATT_HEAD_DIM
ATT_OUT = ATT_SLOTS * ATT_HEAD_DIM
BLOCK = 128
ROPE_THETA = 10000.0
X_HEADS = 4
X_HEAD_DIM = 128
X_WIDTH = X_HEADS * X_HEAD_DIM
N_BRANCH = 3
IN_COLS = SSM_WIDTH + 3 * ATT_WIDTH + X_WIDTH + N_BRANCH * D_MODEL
D_FF = 2816
N_EXPERTS = 8
TOP_K = 2
D_FF_EXPERT = 3584
N_DENSE = (DEPTH + 1) // 2
N_MOE = DEPTH // 2

kernel_name = 'hybrid_s5_dilated_memory_moe_block'

def rmsnorm(x, g):
    xf = x.astype(F32)
    y = xf * lax.rsqrt(jnp.mean(xf * xf, axis=-1, keepdims=True) + EPS)
    return (y * g.astype(F32)).astype(x.dtype)

def rope(x, pos):
    half = x.shape[-1] // 2
    inv = ROPE_THETA ** (-jnp.arange(half, dtype=F32) / half)
    ang = pos.astype(F32)[:, None, :, None] * inv
    cos, sin = jnp.cos(ang), jnp.sin(ang)
    xf = x.astype(F32)
    x1, x2 = xf[..., :half], xf[..., half:]
    return jnp.concatenate([x1 * cos - x2 * sin, x1 * sin + x2 * cos], axis=-1).astype(x.dtype)

def ssm_branch(u, a_re, a_im, log_dt, b_re, b_im, c_re, c_im, d_skip, w_glu):
    bsz, L, _ = u.shape
    uf = u.astype(F32).reshape(bsz, L, SSM_GROUPS, SSM_GROUP)
    lam = lax.complex(a_re.astype(F32), a_im.astype(F32))
    dt = jnp.exp(log_dt.astype(F32))[:, None]
    lam_bar = jnp.exp(lam * dt)
    b = lax.complex(b_re.astype(F32), b_im.astype(F32))
    b_bar = ((lam_bar - 1.0) / lam)[..., None] * b
    bu = jnp.einsum('blgc,gpc->blgp', uf.astype(jnp.complex64), b_bar)
    a_el = jnp.broadcast_to(lam_bar, bu.shape)

    def combine(left, right):
        a1, s1 = left
        a2, s2 = right
        return a2 * a1, a2 * s1 + s2

    _, states = lax.associative_scan(combine, (a_el, bu), axis=1)
    c = lax.complex(c_re.astype(F32), c_im.astype(F32))
    y = jnp.einsum('blgp,gcp->blgc', states, c).real \
        + d_skip.astype(F32).reshape(SSM_GROUPS, SSM_GROUP) * uf
    y = jax.nn.gelu(y.reshape(bsz, L, SSM_WIDTH))
    ga = y @ w_glu.astype(F32)
    out = ga[..., :SSM_WIDTH] * jax.nn.sigmoid(ga[..., SSM_WIDTH:])
    return out.astype(u.dtype)

def dilated_group(q, k, v, dilation, span):
    bsz, H, L, hd = q.shape
    n = L // dilation
    nb = -(-n // BLOCK)
    npad = nb * BLOCK

    def stride(t):
        t = t.reshape(bsz, H, n, dilation, hd).transpose(0, 1, 3, 2, 4)
        return jnp.pad(t, ((0, 0), (0, 0), (0, 0), (0, npad - n), (0, 0)))

    def band(t):
        tb = t.reshape(bsz, H, dilation, nb, BLOCK, hd)
        prev = jnp.pad(tb, ((0, 0), (0, 0), (0, 0), (1, 0), (0, 0), (0, 0)))[:, :, :, :nb]
        return jnp.concatenate([prev, tb], axis=4)

    qb = stride(q).reshape(bsz, H, dilation, nb, BLOCK, hd)
    kb = band(stride(k))
    vb = band(stride(v))
    s = jnp.einsum('bhrnqd,bhrnkd->bhrnqk', qb, kb).astype(F32) * (hd ** -0.5)
    qi = jnp.arange(BLOCK)[:, None] + BLOCK
    ki = jnp.arange(2 * BLOCK)[None, :]
    off = qi - ki
    blk = jnp.arange(nb)[:, None, None]
    valid = (off >= 0) & (off <= span) & (blk * BLOCK + ki - BLOCK >= 0)
    s = jnp.where(valid, s, -1e30)
    m = jnp.max(s, axis=-1, keepdims=True)
    p = jnp.exp(s - m)
    den = jnp.sum(p, axis=-1, keepdims=True)
    o = jnp.einsum('bhrnqk,bhrnkd->bhrnqd', p, vb.astype(F32)) / den
    lse = (m + jnp.log(den))[..., 0]
    o = o.reshape(bsz, H, dilation, npad, hd)[:, :, :, :n].transpose(0, 1, 3, 2, 4).reshape(bsz, H, L, hd)
    lse = lse.reshape(bsz, H, dilation, npad)[:, :, :, :n].transpose(0, 1, 3, 2).reshape(bsz, H, L)
    return o, lse

def dilated_attention(q, k, v, pos, g_q, g_k):
    bsz, L, _ = q.shape

    def heads(t):
        return t.reshape(bsz, L, ATT_HEADS, ATT_HEAD_DIM).transpose(0, 2, 1, 3)

    qh = rope(rmsnorm(heads(q), g_q), pos)
    kh = rope(rmsnorm(heads(k), g_k), pos)
    vh = heads(v)
    outs, lses = [], []
    for gi, (window, dil) in enumerate(DIL_PAIRS):
        sl = slice(gi * ATT_SLOTS, (gi + 1) * ATT_SLOTS)
        o, lse = dilated_group(qh[:, sl], kh[:, sl], vh[:, sl], dil, window // dil)
        outs.append(o)
        lses.append(lse)
    alpha = jax.nn.softmax(jnp.stack(lses), axis=0)
    out = jnp.sum(alpha[..., None] * jnp.stack(outs), axis=0)
    return out.transpose(0, 2, 1, 3).reshape(bsz, L, ATT_OUT).astype(q.dtype)

def memory_attention(q, mem_n, w_kv, g_q, g_k):
    bsz, L, _ = q.shape
    M = mem_n.shape[1]
    kv = mem_n @ w_kv
    k = kv[..., :X_WIDTH].reshape(bsz, M, X_HEADS, X_HEAD_DIM).transpose(0, 2, 1, 3)
    v = kv[..., X_WIDTH:].reshape(bsz, M, X_HEADS, X_HEAD_DIM).transpose(0, 2, 1, 3)
    qh = q.reshape(bsz, L, X_HEADS, X_HEAD_DIM).transpose(0, 2, 1, 3)
    qh = rmsnorm(qh, g_q)
    k = rmsnorm(k, g_k)
    s = jnp.einsum('bhld,bhmd->bhlm', qh, k).astype(F32) * (X_HEAD_DIM ** -0.5)
    p = jax.nn.softmax(s, axis=-1)
    o = jnp.einsum('bhlm,bhmd->bhld', p, v.astype(F32))
    return o.transpose(0, 2, 1, 3).reshape(bsz, L, X_WIDTH).astype(q.dtype)

def swiglu(h, w_gate, w_up, w_down):
    return (jax.nn.silu(h @ w_gate) * (h @ w_up)) @ w_down

def moe_swiglu(h, w_router, w_gate, w_up, w_down):
    bsz, L, D = h.shape
    t = h.reshape(bsz * L, D)
    logits = (t @ w_router).astype(F32)
    top_v, top_i = lax.top_k(logits, TOP_K)
    wts = jax.nn.softmax(top_v, axis=-1)
    gate = jnp.sum(jax.nn.one_hot(top_i, N_EXPERTS, dtype=F32) * wts[..., None], axis=1)
    out = jnp.zeros((bsz * L, D), F32)
    for e in range(N_EXPERTS):
        ye = swiglu(t, w_gate[e], w_up[e], w_down[e]).astype(F32)
        out = out + gate[:, e:e + 1] * ye
    return out.reshape(bsz, L, D).astype(h.dtype)

def setup_inputs(seed: int = 0) -> dict:
    key = jax.random.key(seed)
    ks = iter(jax.random.split(key, 48))

    def nrm(shape, scale):
        return jax.random.normal(next(ks), shape, F32) * scale

    def gain(shape):
        return 1.0 + 0.02 * jax.random.normal(next(ks), shape, F32)

    x = nrm((BATCH, SEQ, D_MODEL), 1.0)
    mem = nrm((BATCH, MEM_LEN, D_MODEL), 1.0)
    positions = jnp.arange(SEQ, dtype=jnp.int32)[None, :] + jax.random.randint(
        next(ks), (BATCH, 1), 0, MAX_POS_OFFSET, dtype=jnp.int32)
    norm_mix = gain((DEPTH, D_MODEL))
    w_in = nrm((DEPTH, D_MODEL, IN_COLS), D_MODEL ** -0.5)
    n_idx = jnp.arange(SSM_STATE, dtype=F32)
    ssm_a_re = -0.5 + 0.01 * jax.random.normal(next(ks), (DEPTH, SSM_GROUPS, SSM_STATE), F32)
    ssm_a_im = math.pi * n_idx + 0.01 * jax.random.normal(next(ks), (DEPTH, SSM_GROUPS, SSM_STATE), F32)
    ssm_log_dt = jax.random.uniform(next(ks), (DEPTH, SSM_GROUPS), F32,
                                    math.log(DT_MIN), math.log(DT_MAX))
    b_scale = (2 * SSM_GROUP) ** -0.5
    c_scale = (2 * SSM_STATE) ** -0.5
    ssm_b_re = nrm((DEPTH, SSM_GROUPS, SSM_STATE, SSM_GROUP), b_scale)
    ssm_b_im = nrm((DEPTH, SSM_GROUPS, SSM_STATE, SSM_GROUP), b_scale)
    ssm_c_re = nrm((DEPTH, SSM_GROUPS, SSM_GROUP, SSM_STATE), c_scale)
    ssm_c_im = nrm((DEPTH, SSM_GROUPS, SSM_GROUP, SSM_STATE), c_scale)
    ssm_d = nrm((DEPTH, SSM_WIDTH), 1.0)
    ssm_w_glu = nrm((DEPTH, SSM_WIDTH, 2 * SSM_WIDTH), SSM_WIDTH ** -0.5)
    w_ssm_out = nrm((DEPTH, SSM_WIDTH, D_MODEL), SSM_WIDTH ** -0.5)
    att_q_norm = gain((DEPTH, ATT_HEAD_DIM))
    att_k_norm = gain((DEPTH, ATT_HEAD_DIM))
    w_att_out = nrm((DEPTH, ATT_OUT, D_MODEL), ATT_OUT ** -0.5)
    norm_mem = gain((DEPTH, D_MODEL))
    w_mem_kv = nrm((DEPTH, D_MODEL, 2 * X_WIDTH), D_MODEL ** -0.5)
    mem_q_norm = gain((DEPTH, X_HEAD_DIM))
    mem_k_norm = gain((DEPTH, X_HEAD_DIM))
    w_mem_out = nrm((DEPTH, X_WIDTH, D_MODEL), X_WIDTH ** -0.5)
    w_o = nrm((DEPTH, D_MODEL, D_MODEL), D_MODEL ** -0.5)
    norm_ffn = gain((DEPTH, D_MODEL))
    ffn_w_gate = nrm((N_DENSE, D_MODEL, D_FF), D_MODEL ** -0.5)
    ffn_w_up = nrm((N_DENSE, D_MODEL, D_FF), D_MODEL ** -0.5)
    ffn_w_down = nrm((N_DENSE, D_FF, D_MODEL), D_FF ** -0.5)
    moe_w_router = nrm((N_MOE, D_MODEL, N_EXPERTS), D_MODEL ** -0.5)
    moe_w_gate = nrm((N_MOE, N_EXPERTS, D_MODEL, D_FF_EXPERT), D_MODEL ** -0.5)
    moe_w_up = nrm((N_MOE, N_EXPERTS, D_MODEL, D_FF_EXPERT), D_MODEL ** -0.5)
    moe_w_down = nrm((N_MOE, N_EXPERTS, D_FF_EXPERT, D_MODEL), D_FF_EXPERT ** -0.5)
    return {'x': x, 'mem': mem, 'positions': positions, 'norm_mix': norm_mix, 'w_in': w_in,
            'ssm_a_re': ssm_a_re, 'ssm_a_im': ssm_a_im, 'ssm_log_dt': ssm_log_dt,
            'ssm_b_re': ssm_b_re, 'ssm_b_im': ssm_b_im, 'ssm_c_re': ssm_c_re, 'ssm_c_im': ssm_c_im,
            'ssm_d': ssm_d, 'ssm_w_glu': ssm_w_glu, 'w_ssm_out': w_ssm_out,
            'att_q_norm': att_q_norm, 'att_k_norm': att_k_norm, 'w_att_out': w_att_out,
            'norm_mem': norm_mem, 'w_mem_kv': w_mem_kv, 'mem_q_norm': mem_q_norm,
            'mem_k_norm': mem_k_norm, 'w_mem_out': w_mem_out, 'w_o': w_o, 'norm_ffn': norm_ffn,
            'ffn_w_gate': ffn_w_gate, 'ffn_w_up': ffn_w_up, 'ffn_w_down': ffn_w_down,
            'moe_w_router': moe_w_router, 'moe_w_gate': moe_w_gate, 'moe_w_up': moe_w_up,
            'moe_w_down': moe_w_down}

def reference(x, mem, positions, norm_mix, w_in, ssm_a_re, ssm_a_im, ssm_log_dt,
              ssm_b_re, ssm_b_im, ssm_c_re, ssm_c_im, ssm_d, ssm_w_glu, w_ssm_out,
              att_q_norm, att_k_norm, w_att_out, norm_mem, w_mem_kv, mem_q_norm,
              mem_k_norm, w_mem_out, w_o, norm_ffn, ffn_w_gate, ffn_w_up, ffn_w_down,
              moe_w_router, moe_w_gate, moe_w_up, moe_w_down):
    bsz, L, D = x.shape
    c0 = SSM_WIDTH
    c1 = c0 + ATT_WIDTH
    c2 = c1 + ATT_WIDTH
    c3 = c2 + ATT_WIDTH
    c4 = c3 + X_WIDTH
    for i in range(DEPTH):
        h = rmsnorm(x, norm_mix[i])
        z = h @ w_in[i]
        y_ssm = ssm_branch(z[..., :c0], ssm_a_re[i], ssm_a_im[i], ssm_log_dt[i],
                           ssm_b_re[i], ssm_b_im[i], ssm_c_re[i], ssm_c_im[i],
                           ssm_d[i], ssm_w_glu[i]) @ w_ssm_out[i]
        y_att = dilated_attention(z[..., c0:c1], z[..., c1:c2], z[..., c2:c3], positions,
                                  att_q_norm[i], att_k_norm[i]) @ w_att_out[i]
        mem_n = rmsnorm(mem, norm_mem[i])
        y_mem = memory_attention(z[..., c3:c4], mem_n, w_mem_kv[i],
                                 mem_q_norm[i], mem_k_norm[i]) @ w_mem_out[i]
        g = jax.nn.sigmoid(z[..., c4:].astype(F32)).reshape(bsz, L, N_BRANCH, D)
        merged = (g[..., 0, :] * y_ssm + g[..., 1, :] * y_att + g[..., 2, :] * y_mem).astype(x.dtype)
        x = x + merged @ w_o[i]
        h2 = rmsnorm(x, norm_ffn[i])
        if i % 2 == 0:
            j = i // 2
            x = x + swiglu(h2, ffn_w_gate[j], ffn_w_up[j], ffn_w_down[j])
        else:
            j = i // 2
            x = x + moe_swiglu(h2, moe_w_router[j], moe_w_gate[j], moe_w_up[j], moe_w_down[j])
    return x


_drawn_inputs = setup_inputs


def setup_inputs(seed=0):
    import zlib

    import numpy as np

    out = dict(_drawn_inputs(seed))
    spreads = {}
    factors = {'norm_mix': 3.549,
     'ssm_a_re': 8.0,
     'att_q_norm': 4.681,
     'att_k_norm': 8.0,
     'norm_mem': 3.797,
     'mem_q_norm': 8.0,
     'mem_k_norm': 8.0}
    for name, (base, spread) in spreads.items():
        noise = np.random.default_rng([zlib.crc32(name.encode()), seed]).standard_normal(out[name].shape)
        drawn = base * np.exp(spread * noise) if base else spread * noise
        out[name] = __import__('jax').numpy.asarray(drawn.astype(out[name].dtype))
    for name, factor in factors.items():
        out[name] = (out[name] * factor).astype(out[name].dtype)
    return out
```

```python
import math
from contextlib import ExitStack

import numpy as np
import concourse.bass as bass
from concourse import mybir

F32 = mybir.dt.float32
F32R = mybir.dt.float32r
I32 = mybir.dt.int32
ALU = mybir.AluOpType
ACT = mybir.ActivationFunctionType
AX = mybir.AxisListType

P = 128
BANK = 512
NEG = -1e30
EPS = 1e-6
TWO_PI = 2 * math.pi
ROUND = 1.5 * 2.0 ** 23
ROUND_FINE = ROUND * 2.0 ** -14
PI_A = 6.28125
PI_B = float(np.float32(np.round((TWO_PI - PI_A) * 2 ** 22) / 2 ** 22))
PI_C = float(np.float32(TWO_PI - PI_A - PI_B))


def decoder_trunk(nc, x_in, mem_in, positions, norm_mix, w_in, a_re, a_im, log_dt, b_re, b_im,
                  c_re, c_im, ssm_d, w_glu, w_ssm_out, g_q, g_k, w_att_out, norm_mem, w_mem_kv,
                  g_mq, g_mk, w_mem_out, w_o, norm_ffn, ffn_gate, ffn_up, ffn_down, router,
                  moe_gate, moe_up, moe_down, out, dbg=None):
    _, SEQ, D = x_in.shape
    MEM = mem_in.shape[1]
    L = norm_mix.shape[0]
    C = SEQ // P
    KD = D // P
    COLS = w_in.shape[2]
    GROUPS, STATE = a_re.shape[1:]
    GCH = b_re.shape[3]
    SSM = GROUPS * GCH
    KS = SSM // P
    NJ = GROUPS * STATE // P
    HD = g_q.shape[1]
    SLOTS = w_att_out.shape[1] // HD
    DIL = (1, 4, 16)
    SPAN = 128
    NG = len(DIL)
    HEADS = NG * SLOTS
    AW = HEADS * HD
    XD = g_mq.shape[1]
    XW = w_mem_kv.shape[2] // 2
    XH = XW // XD
    Q0, K0, V0, MQ0, GATE0 = SSM, SSM + AW, SSM + 2 * AW, SSM + 3 * AW, SSM + 3 * AW + XW
    FF = ffn_gate.shape[2]
    NE = router.shape[2]
    FE = moe_gate.shape[3]
    assert SEQ == MEM == 2 * P and 2 * STATE == P and L == 2 and HD == 64 and XD == P

    TILE = 2048
    KT = TILE // BANK
    R = 3
    RM = 6
    H = 3
    KV_TILES, IN_FULL = 4, COLS // BANK
    MIX_TILES = KV_TILES + 2 * IN_FULL + 1 + 2 + 2 + 1 + 2 + 4
    NF = FF // 256
    FFN_TILES = 3 * NF
    NFE = FE // BANK
    MOE_TILES = 6 * NFE
    assert COLS == IN_FULL * BANK + 256 and FF % 256 == 0 and FE % BANK == 0 and NF % 2 == 1
    assert FFN_TILES % H == 0 and MOE_TILES % RM == 0

    ctx = ExitStack()
    sems = {}

    def sem(name):
        if name not in sems:
            sems[name] = ctx.enter_context(nc.semaphore(name))
        return sems[name]

    def buffers(stack):
        return lambda name, shape, dt=F32: stack.enter_context(nc.sbuf_tensor(name, shape, dt))

    with ctx:
        sb = buffers(ctx)
        ps = ctx.enter_context(nc.psum_tensor("ps", [P, 8, BANK], F32))

        x = sb("x", [P, C, D])
        h = sb("h", [P, C, D])
        hT = sb("hT", [P, KD, SEQ])
        ring = sb("ring", [P, R, TILE])
        ident = sb("ident", [P, P])
        ones = sb("ones", [P, P])
        before = sb("before", [P, P])
        ramp_i = sb("ramp_i", [P, SEQ], I32)
        ramp = sb("ramp", [P, SEQ])
        gains = sb("gains", [P, 3, L, KD])
        ss = sb("ss", [P, 4])
        rs = sb("rs", [P, 4])
        half_neg = sb("half_neg", [P, 64])
        half_pi = sb("half_pi", [P, 1])

        memT = sb("memT", [P, KD, MEM])
        mask = sb("mask", [P, NG * 3 * P])
        dsk = sb("dsk", [P, L, KS])
        gmq = sb("gmq", [P, L, 2])
        gqk = sb("gqk", [P, L, 2, HD])
        rope = sb("rope", [P, 2, C, HD // 2])

        mix = ExitStack()
        mb = buffers(mix)
        z = mb("z", [P, C, COLS])
        kv = mb("kv", [P, C, 2 * XW])
        uT = mb("uT", [P, KS, SEQ])
        gT = mb("gT", [P, KS, SEQ])
        qmT = mb("qmT", [P, XH, SEQ])
        kmT = mb("kmT", [P, XH, MEM])
        bT = mb("bT", [P, NJ // 4, 2, P])
        cT = mb("cT", [P, NJ, 2, 2 * GCH])
        pos_i = mb("pos_i", [P, C], I32)
        pos = mb("pos", [P, C])
        rgain = mb("rgain", [P, 2, 2, C, HD])
        spT = mb("spT", [P, 8, NJ])
        dt16 = mb("dt16", [NJ, 2])
        rqk = mb("rqk", [P, C, 2 * HEADS])
        rqk2 = mb("rqk2", [P, C, 2 * HEADS])
        rm = mb("rm", [P, 2, C, XH])
        rm2 = mb("rm2", [P, 2, C, XH])
        stat = mb("stat", [P, 8, 4])
        early = ExitStack()
        eb = buffers(early)
        costab = eb("costab", [P, NJ, SEQ])
        sintab = eb("sintab", [P, NJ, SEQ])
        wa = eb("wa", [P, 2, 2, SEQ])
        wb = eb("wb", [P, 2, 2, SEQ])
        wv = eb("wv", [P, 2, 2, SEQ])
        wp = eb("wp", [P, 2, 2, SEQ])
        early.close()
        first = ExitStack()
        sb1 = buffers(first)
        invf = sb1("invf", [P, HD // 2])
        dist_i = sb1("dist_i", [P, C, SEQ], I32)
        grid_i = sb1("grid_i", [P, 2, SEQ], I32)
        ang = sb1("ang", [P, C, HD // 2])
        turns = sb1("turns", [P, C, HD // 2])
        first.close()
        late = ExitStack()
        lb = buffers(late)
        t1 = lb("t1", [P, C, 2 * AW])
        t2 = lb("t2", [P, C, 2 * AW])
        qkT = lb("qkT", [P, 2, HEADS // 2, SEQ])
        sc = lb("sc", [P, 2, NG * 2 * P])
        pr = lb("pr", [P, 2, NG * 2 * P])
        pT = lb("pT", [P, NG * 2 * P])
        late.close()
        mix.close()

        ffn = ExitStack()
        fb = buffers(ffn)
        hi = fb("hi", [P, H, TILE], F32R)
        lo = fb("lo", [P, H, TILE], F32R)
        aT_hi = fb("aT_hi", [P, BANK], F32R)
        aT_lo = fb("aT_lo", [P, BANK], F32R)
        gate_act = fb("gate_act", [P, BANK])
        act_out = fb("act_out", [P, BANK])
        dense_only = ExitStack()
        hT_hi = buffers(dense_only)("hT_hi", [P, KD, SEQ], F32R)
        hT_lo = buffers(dense_only)("hT_lo", [P, KD, SEQ], F32R)
        dense_only.close()
        ring_e = fb("ring_e", [P, RM, TILE])
        xe = fb("xe", [P, KD, P])
        xe_hi = fb("xe_hi", [P, KD, P], F32R)
        xe_lo = fb("xe_lo", [P, KD, P], F32R)
        y_e = fb("y_e", [P, D])
        disp = fb("disp", [P, C, P])
        comb = fb("comb", [P, C, P])
        combT = fb("combT", [P, C * P])
        rt = fb("rt", [P, KD, NE])
        lg = fb("lg", [P, C, NE])
        cmp_ = fb("cmp", [P, 2, C, NE, NE])
        tie = fb("tie", [P, NE, NE])
        sel = fb("sel", [P, C, NE])
        gate = fb("gate", [P, C, NE])
        slot_of = fb("slot_of", [P, C, NE + 1])
        rstat = fb("rstat", [P, 8])
        most = fb("most", [P, 1], I32)
        ffn.close()

        def flat(t):
            names = "abcd"[:len(t.shape) - 1]
            return t[:].rearrange(f"p {' '.join(names)} -> p ({' '.join(names)})")

        def spread(a, axis, n):
            a = a.unsqueeze(axis)
            shape = list(a.shape)
            shape[axis] = n
            return a.to_broadcast(shape)

        def gmask(c, g):
            o = NG * P * c + g * (c + 1) * P
            return mask[:, o:o + (c + 1) * P]

        sout = z[:, :, 0:SSM]
        soT = uT
        oatt = z[:, :, Q0:Q0 + SLOTS * HD]
        oT = hT
        omem = z[:, :, MQ0:MQ0 + XW]
        omT = gT
        sig = z[:, :, K0:K0 + SSM]
        merged = h
        b_raw = z[:, 1, GATE0:GATE0 + 2 * NJ * GCH].rearrange("p (r j c) -> p r j c", r=2, j=NJ)
        b_bar = z[:, 1, GATE0 + 512:GATE0 + 512 + 2 * NJ * 2 * GCH].rearrange(
            "p (r j c) -> p r j c", r=2, j=NJ)
        b_tmp = z[:, 0, GATE0 + 1024:GATE0 + 1024 + NJ * GCH].rearrange("p (j c) -> p j c", j=NJ)
        b_tmp2 = z[:, 0, GATE0 + 1280:GATE0 + 1280 + NJ * GCH].rearrange("p (j c) -> p j c", j=NJ)
        sp16 = z[0:NJ, 0, GATE0 + 1536:GATE0 + 1536 + 12 * P].rearrange("j (i s) -> j i s", i=12)
        c_raw = z[:, 0, GATE0:GATE0 + 2 * 4 * P].rearrange("p (r q s) -> p r q s", r=2, q=4)

        def blocks(w, k0, k1, n0, n1):
            return w[k0 * P:k1 * P, n0:n1].rearrange("(k p) n -> p k n", p=P)

        def mix_tiles(l):
            t = [blocks(w_mem_kv[l], KT * i, KT * i + KT, BANK * n, BANK * n + BANK)
                 for n in range(2) for i in range(2)]
            t += [blocks(w_in[l], KT * i, KT * i + KT, BANK * n, BANK * n + BANK)
                  for n in range(IN_FULL) for i in range(2)]
            t += [blocks(w_in[l], 0, KD, IN_FULL * BANK, COLS)]
            t += [blocks(w_glu[l], 0, KT, BANK * n, BANK * n + BANK) for n in range(2)]
            t += [blocks(w_ssm_out[l], 0, KT, BANK * n, BANK * n + BANK) for n in range(2)]
            t += [blocks(w_att_out[l], 0, 2, 0, D)]
            t += [blocks(w_mem_out[l], 0, KT, BANK * n, BANK * n + BANK) for n in range(2)]
            t += [blocks(w_o[l], KT * i, KT * i + KT, BANK * n, BANK * n + BANK)
                  for n in range(2) for i in range(2)]
            assert len(t) == MIX_TILES
            return t

        full = [sem(f"tile_arrived_{r}") for r in range(R)]
        COL_TILES = 2 + IN_FULL + 1 + 2 + 3 * 2 + 2

        def tile_uses():
            uses, col, mid = [], 0, 0
            for count, per_column in ((KV_TILES, 2), (2 * IN_FULL, 2), (1, 1), (2, 1), (2, 1), (1, 0.5), (2, 1), (4, 2)):
                for i in range(count):
                    if per_column == 2 and i % 2 == 0:
                        mid += 1
                        uses.append(("middle_tiles_used", mid))
                    else:
                        col += 2 if per_column == 0.5 else 1
                        uses.append(("columns_done", col))
            assert col == COL_TILES and len(uses) == MIX_TILES
            return uses, mid

        USES, MIDDLE = tile_uses()

        BATCHES = (("ssm", 1), ("b", 2), ("c", 2), ("h", KD // 2), ("u", KS // 2), ("qk", HEADS // 2), ("mem_qk", XH),
                   ("ssm_out", KS // 2), ("att_out", 1), ("mem_out", XH // 2), ("merged", KD // 2), ("ffn", KD // 2))

        def batches_to(l, name):
            n = KD // 2 + l * sum(b for _, b in BATCHES)
            for key, b in BATCHES:
                n += b
                if key == name:
                    return n
        full_e = [sem(f"expert_tile_arrived_{r}") for r in range(RM)]
        params = sem("params_loaded")
        lparams = [sem(f"layer_params_loaded{l}") for l in range(L)]
        N_SMALL = 7
        BASE = [0, MIX_TILES + FFN_TILES]

        ctx.enter_context(nc.allow_non_contiguous_dma(reason="gains and skips by channel: small"))
        block = ctx.enter_context(nc.Block())

        @block.sync
        def _(sp):
            def load(n, src, shift=0):
                if n >= R:
                    i = n - R if n < BASE[1] + R else n - R - BASE[1]
                    if MIX_TILES <= i and n < BASE[1] + R:
                        sp.wait_ge(sem("lo_ready"), i - MIX_TILES + 1 + R * shift)
                    else:
                        name, count = USES[i]
                        sp.wait_ge(sem(name), count + (0 if n < BASE[1] + R else {"columns_done": COL_TILES}.get(name, MIDDLE)))
                v = ring[:, n % R, :].rearrange("p (k n) -> p k n", n=src.shape[2])
                sp.dma_start(v, src).then_inc(full[n % R], 16)

            sp.dma_start(h[:], mem_in[0].rearrange("(c p) d -> p c d", p=P)).then_inc(sem("mem_loaded"), 16)
            sp.dma_start(x[:], x_in[0].rearrange("(c p) d -> p c d", p=P)).then_inc(sem("x_loaded"), 16)
            for l in range(L):
                for i, src in enumerate(mix_tiles(l)):
                    load(BASE[l] + i, src)
                if l == 0:
                    n0 = MIX_TILES

                    def gate_tile(w, f):
                        return w[0][:, bass.ds(f * 256, 256)].rearrange("(k p) n -> p k n", p=P)

                    def down_tile(f):
                        return ffn_down[0][bass.ds(f * 256, 256), :].rearrange("(k p) n -> p k n", p=P)
                    load(n0, gate_tile(ffn_gate, 0))
                    load(n0 + 1, gate_tile(ffn_up, 0))
                    load(n0 + 2, gate_tile(ffn_gate, 1))
                    load(n0 + 3, gate_tile(ffn_up, 1))
                    load(n0 + 4, down_tile(0))
                    with sp.Fori(2, NF) as f:
                        load(n0 + 5, gate_tile(ffn_gate, f), f - 2)
                        load(n0 + 6, gate_tile(ffn_up, f), f - 2)
                        load(n0 + 7, down_tile(f - 1), f - 2)
                    load(n0 + 3 * NF - 1, down_tile(NF - 1))

            sp.wait_ge(sem("columns_used"), L * COL_TILES)

            def load_e(c, src, turn, first=False):
                if not first:
                    sp.wait_ge(sem("lo_ready"), FFN_TILES + RM * (turn - 1) + c % RM + 1)
                v = ring_e[:, c % RM, :].rearrange("p (k n) -> p k n", n=src.shape[2])
                sp.dma_start(v, src).then_inc(full_e[c % RM], 16)

            def moe_src(e, f, i):
                w = (moe_gate, moe_gate, moe_up, moe_up)[i]
                src = w[0].rearrange("e k n -> (e k) n")[
                    bass.ds(e * D + (i % 2) * KT * P, KT * P), bass.ds(f * BANK, BANK)]
                return src.rearrange("(k p) n -> p k n", p=P)

            def moe_down_src(e, f, i):
                src = moe_down[0].rearrange("e k n -> (e k) n")[
                    bass.ds(e * FE + f * BANK + i * 2 * P, 2 * P), :]
                return src.rearrange("(k p) n -> p k n", p=P)

            def expert_loads(e, turn0, first):
                for i in range(4):
                    load_e(i, moe_src(e, 0, i), turn0, first)
                for i in range(2):
                    load_e(4 + i, moe_src(e, 1, i), turn0, first)
                for i in range(2):
                    load_e(i, moe_src(e, 1, 2 + i), turn0 + 1)
                for i in range(2):
                    load_e(2 + i, moe_down_src(e, 0, i), turn0 + 1)
                with sp.Fori(2, NFE) as f:
                    for i in range(2):
                        load_e(4 + i, moe_src(e, f, i), turn0 + f - 1)
                    for i in range(2):
                        load_e(i, moe_src(e, f, 2 + i), turn0 + f)
                    for i in range(2):
                        load_e(2 + i, moe_down_src(e, f - 1, i), turn0 + f)
                for i in range(2):
                    load_e(4 + i, moe_down_src(e, NFE - 1, i), turn0 + NFE - 1)

            expert_loads(0, 0, True)
            with sp.Fori(1, NE) as e:
                expert_loads(e, NFE * e, False)
            sp.wait_ge(sem("routed"), 1)
            busiest = sp.value_load(most[0:1, 0:1])
            with sp.If(busiest > P):
                with sp.Fori(0, NE) as e:
                    expert_loads(e, NFE * NE + NFE * e, False)
            sp.wait_ge(sem("x_final"), 1)
            sp.dma_start(out[0].rearrange("(c p) d -> p c d", p=P), x[:]).then_inc(sem("stored"), 16)
            sp.wait_ge(sem("stored"), 16)

        @block.gpsimd
        def _(pool):
            built = sem("pool_chain")
            n = [0]

            def chain(ins):
                n[0] += 1
                ins.then_inc(built, 1)
                pool.wait_ge(built, n[0])

            for i, g in enumerate((norm_mix, norm_mem, norm_ffn)):
                for l in range(L):
                    pool.dma_start(gains[:, i, l, :], g[l].rearrange("(k p) -> p k", p=P)).then_inc(params, 16)
            for l in range(L):
                pool.dma_start(dsk[:, l, :], ssm_d[l].rearrange("(q p) -> p q", p=P)).then_inc(params, 16)
                pool.dma_start(gmq[:, l, 0:1], g_mq[l].rearrange("(p o) -> p o", o=1)).then_inc(params, 16)
                pool.dma_start(gmq[:, l, 1:2], g_mk[l].rearrange("(p o) -> p o", o=1)).then_inc(params, 16)
                pool.dma_start(gqk[:, l, 0, :], g_q[l:l + 1, :].to_broadcast([P, HD])).then_inc(params, 16)
                pool.dma_start(gqk[:, l, 1, :], g_k[l:l + 1, :].to_broadcast([P, HD])).then_inc(params, 16)
            pool.dma_start(pos_i[:], positions.rearrange("o (c p) -> p (o c)", p=P)).then_inc(sem("pos_loaded"), 16)

            nc.gpsimd.memset(half_neg[:], -0.5)
            nc.gpsimd.memset(half_pi[:], math.pi / 2)
            nc.gpsimd.memset(ones[:], 1.0)
            chain(nc.gpsimd.memset(ident[:], 0.0))
            nc.gpsimd.affine_select(out=ident[:], in_=ident[:], compare_op=ALU.not_equal, fill=1.0, base=0,
                                    pattern=[[-1, P]], channel_multiplier=1).then_inc(sem("ident_ready"), 1)
            nc.gpsimd.affine_select(out=before[:], in_=ones[:], compare_op=ALU.is_gt, fill=0.0, base=0,
                                    pattern=[[1, P]], channel_multiplier=-1)
            nc.gpsimd.iota(ramp_i[:], pattern=[[1, SEQ]], base=0, channel_multiplier=0)
            for i in range(HD // 2):
                nc.gpsimd.memset(invf[:, i:i + 1], float(np.float32(10000.0) ** np.float32(-i / (HD // 2))))
            for c in range(C):
                last = nc.gpsimd.iota(dist_i[:, c, :], pattern=[[-1, SEQ]], base=SEQ + c * P, channel_multiplier=1)
            last.then_inc(sem("consts_ready"), 1)
            for c in range(C):
                chain(nc.gpsimd.memset(gmask(c, 0), 0.0))
                chain(nc.gpsimd.affine_select(out=gmask(c, 0), in_=gmask(c, 0), compare_op=ALU.is_ge, fill=NEG,
                                              base=SPAN - c * P, pattern=[[1, (c + 1) * P]], channel_multiplier=-1))
            def rsqrt_mean(dst, src, count, of, done):
                pool.wait_ge(*of)
                chain(nc.gpsimd.tensor_scalar(src, src, 1.0 / count, EPS, ALU.mult, ALU.add))
                nc.gpsimd.tensor_tensor(dst, src, half_neg[:, 0:src.shape[1]], ALU.pow).then_inc(done, 1)

            def load_layer(l):
                s = lparams[l]
                pool.dma_start(sp16[:, 0, :], a_re[l].rearrange("(j g) p -> j (g p)", g=2)).then_inc(s, 16)
                pool.dma_start(sp16[:, 1, :], a_im[l].rearrange("(j g) p -> j (g p)", g=2)).then_inc(s, 16)
                pool.dma_start(dt16[:], log_dt[l].rearrange("(j g) -> j g", g=2)).then_inc(s, 16)
                for r, w in enumerate((b_re, b_im)):
                    pool.dma_start(b_raw[:, r], w[l].rearrange("(j g) p c -> (g p) j c", g=2)).then_inc(s, 16)
                for r, w in enumerate((c_re, c_im)):
                    for half in range(2):
                        pool.dma_start(c_raw[:, r, :, half * STATE:(half + 1) * STATE],
                                       w[l].rearrange("(q g) c p -> (g c) q p", q=4)).then_inc(s, 16)

            load_layer(0)
            rsqrt_mean(rs[:, 0:C], ss[:, 0:C], D, (sem("mem_squared"), 1), sem("mem_rs"))
            for l in range(L):
                if l > 0:
                    pool.wait_ge(sem("x_ready"), l)
                    load_layer(l)
                rsqrt_mean(rs[:, 2:2 + C], ss[:, 2:2 + C], D, (sem("x_squared"), 2 * l + 1), sem("x_rs"))
                if l == 0:
                    pool.wait_ge(sem("grid_ready"), 1)
                    for c in range(C):
                        for g in range(NG):
                            last = nc.gpsimd.affine_select(out=gmask(c, g), in_=gmask(c, g), compare_op=ALU.is_ge, fill=NEG,
                                                           base=c * P, pattern=[[-1, (c + 1) * P]], channel_multiplier=1)
                    last.then_inc(sem("mask_ready"), 1)
                rsqrt_mean(flat(rqk2), flat(rqk), HD, (sem("qk_squared"), l + 1), sem("qk_rs"))
                rsqrt_mean(flat(rm2), flat(rm), XD, (sem("mqk_squared"), l + 1), sem("mqk_rs"))
                rsqrt_mean(rs[:, 2:2 + C], ss[:, 2:2 + C], D, (sem("x_squared"), 2 * l + 2), sem("x_rs"))

        @block.tensor
        def _(pe):
            tr = [0]
            used = [0]

            def batch(ins, wait=None):
                if wait:
                    pe.wait_ge(*wait)
                if tr[0] >= 4:
                    pe.wait_ge(sem("transposed_used"), tr[0] - 3)
                col = 0
                for a in ins:
                    o = ps[0:a.shape[1], 4 + tr[0] % 4, col:col + a.shape[0]]
                    last = nc.tensor.transpose(o, a, ident[0:a.shape[0], 0:a.shape[0]])
                    col += a.shape[0]
                tr[0] += 1
                last.then_inc(sem("transposed"), 1)

            def tile(n, width=BANK):
                pe.wait_ge(full[n % R], 16 * (n // R + 1))
                return ring[:, n % R, :].rearrange("p (k n) -> p k n", n=width)

            acc = [0]

            def columns(n, tiles, lhs, k_tile, width=BANK):
                pair = 2 * (acc[0] % 2)
                if acc[0] >= 2:
                    pe.wait_ge(sem("columns_used"), acc[0] - 1)
                for i in range(tiles):
                    w = tile(n + i, width)
                    for c in range(C):
                        for k in range(k_tile):
                            kk = i * k_tile + k
                            last = nc.tensor.matmul(ps[:, pair + c, 0:width], lhs[:, kk, c * P:(c + 1) * P],
                                                    w[:, k, :], start=kk == 0, stop=kk == tiles * k_tile - 1)
                    if i < tiles - 1:
                        last.then_inc(sem("middle_tiles_used"), 1)
                acc[0] += 1
                last.then_inc(sem("columns_done"), 1)

            def mixer(l):
                n = BASE[l]
                if l == 0:
                    pe.wait_ge(sem("ident_ready"), 1)
                    for k in range(0, KD, 2):
                        batch([h[:, c, (k + i) * P:(k + i + 1) * P] for i in range(2) for c in range(C)],
                              (sem("h_ready"), 1))
                pe.wait_ge(sem("memT_scaled"), l + 1)
                columns(n, 2, hT, KT)
                batch([sp16[:, i, :] for i in (6, 7, 10, 11, 2, 3)], (sem("ssm_params"), l + 1))
                columns(n + 2, 2, hT, KT)
                n += KV_TILES
                for r in range(2):
                    batch([b_bar[:, r, 4 * q:4 * q + 4, :].rearrange("p j c -> p (j c)") for q in range(4)],
                          (sem("b_bar_ready"), l + 1))
                for r in range(2):
                    batch([c_raw[:, r, q, :] for q in range(4)])
                for k in range(0, KD, 2):
                    batch([h[:, c, (k + i) * P:(k + i + 1) * P] for i in range(2) for c in range(C)],
                          (sem("h_ready"), 2 * l + 2))
                pe.wait_ge(sem("transposed_used"), batches_to(l, "h"))
                columns(n, 2, hT, KT)
                columns(n + 2, 2, hT, KT)
                n += 4
                pe.wait_ge(sem("columns_used"), acc[0] - 1)
                for q in range(0, KS, 2):
                    batch([z[:, c, (q + i) * P:(q + i + 1) * P] for i in range(2) for c in range(C)])
                pe.wait_ge(sem("transposed_used"), tr[0])
                for v in range(NJ // 2):
                    if v > 0:
                        pe.wait_ge(sem("bu_used"), NJ // 2 * l + v)
                    for i in range(2):
                        j = 2 * v + i
                        o = 32 * (j % 4)
                        for r in range(2):
                            last = nc.tensor.matmul(ps[:, 4 + i, r * SEQ:(r + 1) * SEQ], bT[o:o + 32, j // 4, r, :],
                                                    uT[o:o + 32, j // 4, :], start=True, stop=True)
                    last.then_inc(sem("bu_done"), 1)
                    columns(n, 2, hT, KT)
                    n += 2
                    pe.wait_ge(sem("states_ready"), NJ // 2 * l + v + 1)
                    if v >= 4 and v % 2 == 0:
                        pe.wait_ge(sem("y_used"), KS * l + v // 2 - 1)
                    for i in range(2):
                        j = 2 * v + i
                        o = 32 * (j % 4)
                        for r in range(2):
                            last = nc.tensor.matmul(ps[o:o + 32, 6, (j // 4 % 2) * SEQ:(j // 4 % 2 + 1) * SEQ],
                                                    cT[:, j, r, :], wv[:, i, r, :], start=r == 0, stop=r == 1,
                                                    skip_group_check=True)
                    last.then_inc(sem("y_done"), 1)
                for _ in range(IN_FULL - 2 - NJ // 2):
                    columns(n, 2, hT, KT)
                    n += 2
                columns(n, 1, hT, KD, 256)
                n += 1
                pe.wait_ge(sem("gelu_ready"), l + 1)
                columns(n, 1, gT, KS)
                columns(n + 1, 1, gT, KS)
                n += 2
                for qk in range(2):
                    for i in range(0, HEADS // 2, 2):
                        o = Q0 + qk * AW + i * P
                        batch([z[:, c, o + d * P:o + (d + 1) * P] for d in range(2) for c in range(C)],
                              (sem("qk_ready"), l + 1))
                for src, o in ((z, MQ0), (kv, 0)):
                    for i in range(0, XH, 2):
                        batch([src[:, c, o + (i + d) * XD:o + (i + d + 1) * XD] for d in range(2) for c in range(C)],
                              (sem("mqk_ready"), l + 1))
                pe.wait_ge(sem("transposed_used"), tr[0])
                pe.wait_ge(sem("columns_used"), acc[0])

                def scores(u):
                    c, s = u // SLOTS, u % SLOTS
                    if u >= 2:
                        pe.wait_ge(sem("scores_used"), 2 * SLOTS * l + u - 1)
                    nk = (c + 1) * P
                    for g in range(NG):
                        hd = g * SLOTS + s
                        o = HD * (hd % 2)
                        bank, col = 2 * (u % 2) + g * nk // BANK, g * nk % BANK
                        last = nc.tensor.matmul(ps[:, bank, col:col + nk], qkT[o:o + HD, 0, hd // 2, c * P:(c + 1) * P],
                                                qkT[o:o + HD, 1, hd // 2, 0:nk], start=True, stop=True)
                    last.then_inc(sem("scores_done"), 1)

                def attend(u):
                    c, s = u // SLOTS, u % SLOTS
                    nb = NG * (c + 1)
                    pe.wait_ge(sem("probs_ready"), 2 * SLOTS * l + u + 1)
                    if u >= 1:
                        pe.wait_ge(sem("probsT_ready"), 2 * SLOTS * l + u)
                    for b in range(nb):
                        last = nc.tensor.transpose(ps[:, 4 + b // 4, b % 4 * P:(b % 4 + 1) * P],
                                                   pr[:, u % 2, b * P:(b + 1) * P], ident[:])
                    last.then_inc(sem("probsT_done"), 1)
                    pe.wait_ge(sem("probsT_ready"), 2 * SLOTS * l + u + 1)
                    if u >= 2:
                        pe.wait_ge(sem("att_out_ready"), 2 * SLOTS * l + u - 1)
                    for b in range(nb):
                        g, kc = b // (c + 1), b % (c + 1)
                        o = V0 + (g * SLOTS + s) * HD
                        last = nc.tensor.matmul(ps[:, 6 + u % 2, 0:HD],
                                                pT[:, b * P:(b + 1) * P], z[:, kc, o:o + HD],
                                                start=b == 0, stop=b == nb - 1, skip_group_check=True)
                    last.then_inc(sem("attended"), 1)

                units = C * SLOTS
                scores(0)
                for u in range(1, units):
                    scores(u)
                    attend(u - 1)
                attend(units - 1)
                for c in range(C):
                    if c == 0:
                        pe.wait_ge(sem("scores_used"), units * (l + 1))
                    for hd in range(XH):
                        last = nc.tensor.matmul(ps[:, 2 * c + hd // 2, hd % 2 * MEM:(hd % 2 + 1) * MEM],
                                                qmT[:, hd, c * P:(c + 1) * P], kmT[:, hd, :], start=True, stop=True)
                    last.then_inc(sem("mem_scores_done"), 1)
                for c in range(C):
                    pe.wait_ge(sem("mem_probs_ready"), C * l + c + 1)
                    if c > 0:
                        pe.wait_ge(sem("mem_probsT_ready"), C * l + c)
                    for b in range(2 * XH):
                        last = nc.tensor.transpose(ps[:, 4 + b // 4, b % 4 * P:(b % 4 + 1) * P],
                                                   t1[:, c, b * P:(b + 1) * P], ident[:])
                    last.then_inc(sem("mem_probsT_done"), 1)
                    pe.wait_ge(sem("mem_probsT_ready"), C * l + c + 1)
                    if c == 0:
                        pe.wait_ge(sem("att_out_ready"), units * (l + 1))
                    else:
                        pe.wait_ge(sem("mem_out_ready"), C * l + c)
                    for hd in range(XH):
                        for kc in range(2):
                            b = 2 * hd + kc
                            last = nc.tensor.matmul(ps[:, 7, hd * XD:(hd + 1) * XD], t2[:, c, b * P:(b + 1) * P],
                                                    kv[:, kc, XW + hd * XD:XW + (hd + 1) * XD],
                                                    start=kc == 0, stop=kc == 1, skip_group_check=True)
                    last.then_inc(sem("mem_attended"), 1)
                pe.wait_ge(sem("mem_out_ready"), C * (l + 1))
                pe.wait_ge(sem("att_out_ready"), units * (l + 1))
                for q in range(0, KS, 2):
                    batch([sout[:, c, (q + i) * P:(q + i + 1) * P] for i in range(2) for c in range(C)],
                          (sem("columns_used"), acc[0]))
                batch([oatt[:, c, i * P:(i + 1) * P] for i in range(2) for c in range(C)])
                for q in range(0, XH, 2):
                    batch([omem[:, c, (q + i) * P:(q + i + 1) * P] for i in range(2) for c in range(C)])
                pe.wait_ge(sem("transposed_used"), tr[0])
                for lhs, tiles in ((soT, 2), (oT, 1), (omT, 2)):
                    if tiles == 2:
                        for t in range(2):
                            columns(n, 1, lhs, KS)
                            n += 1
                    else:
                        w = tile(n, D)
                        for half in range(2):
                            pair = 2 * (acc[0] % 2)
                            pe.wait_ge(sem("columns_used"), acc[0] - 1)
                            for c in range(C):
                                for k in range(2):
                                    last = nc.tensor.matmul(ps[:, pair + c, :], lhs[:, k, c * P:(c + 1) * P],
                                                            w[:, k, half * BANK:(half + 1) * BANK],
                                                            start=k == 0, stop=k == 1)
                            acc[0] += 1
                            last.then_inc(sem("columns_done"), 1)
                        n += 1
                for k in range(0, KD, 2):
                    batch([merged[:, c, (k + i) * P:(k + i + 1) * P] for i in range(2) for c in range(C)],
                          (sem("merged_ready"), l + 1))
                pe.wait_ge(sem("transposed_used"), tr[0])
                columns(n, 2, hT, KT)
                columns(n + 2, 2, hT, KT)
                for k in range(0, KD, 2):
                    batch([h[:, c, (k + i) * P:(k + i + 1) * P] for i in range(2) for c in range(C)],
                          (sem("h_ready"), 2 * l + 3))

            def split_product(o, x_hi, x_lo, w_hi, w_lo, first, end):
                nc.tensor.matmul(o, x_hi, w_hi, start=first, stop=False, skip_group_check=True)
                nc.tensor.matmul(o, x_hi, w_lo, start=False, stop=False, skip_group_check=True)
                return nc.tensor.matmul(o, x_lo, w_hi, start=False, stop=end, skip_group_check=True)

            def split_tile(m, width, shift=0):
                pe.wait_ge(sem("lo_ready"), m + 1 + shift)
                return (hi[:, m % H, :].rearrange("p (k n) -> p k n", n=width),
                        lo[:, m % H, :].rearrange("p (k n) -> p k n", n=width))

            def dense():
                def hidden(bank, m, shift):
                    w_hi, w_lo = split_tile(m, 256, shift)
                    for c in range(C):
                        for k in range(KD):
                            last = split_product(ps[:, bank, c * 256:(c + 1) * 256], hT_hi[:, k, c * P:(c + 1) * P],
                                                 hT_lo[:, k, c * P:(c + 1) * P], w_hi[:, k, :], w_lo[:, k, :],
                                                 k == 0, k == KD - 1)
                    last.then_inc(sem("split_used"), 1)

                def act_transposes(f):
                    pe.wait_ge(sem("act_ready"), f)
                    for j in range(2):
                        for c in range(C):
                            last = nc.tensor.transpose(ps[:, 2, j * SEQ + c * P:j * SEQ + (c + 1) * P],
                                                       act_out[:, c * 256 + j * P:c * 256 + (j + 1) * P], ident[:])
                    last.then_inc(sem("actT_done"), 1)

                def down(f, m, shift, first, end):
                    pe.wait_ge(sem("actT_ready"), f)
                    w_hi, w_lo = split_tile(m, D, shift)
                    for c in range(C):
                        for half in range(2):
                            for j in range(2):
                                t = slice(j * SEQ + c * P, j * SEQ + (c + 1) * P)
                                last = split_product(ps[:, 4 + 2 * c + half, :], aT_hi[:, t], aT_lo[:, t],
                                                     w_hi[:, j, half * BANK:(half + 1) * BANK],
                                                     w_lo[:, j, half * BANK:(half + 1) * BANK],
                                                     first and j == 0, end and j == 1)
                    last.then_inc(sem("split_used"), 1)

                def step(f, shift, first):
                    pe.wait_ge(sem("silu_done"), f)
                    hidden(0, 2, shift)
                    act_transposes(f)
                    hidden(1, 3, shift)
                    down(f, 4, shift, first, False)

                pe.wait_ge(sem("transposed_used"), batches_to(0, "ffn"))
                hidden(0, 0, 0)
                hidden(1, 1, 0)
                step(1, 0, True)
                with pe.Fori(2, NF) as f:
                    step(f, 3 * (f - 1), False)
                act_transposes(NF)
                down(NF, FFN_TILES - 1, 0, False, True)

            def experts():
                pe.wait_ge(sem("transposed_used"), batches_to(1, "ffn"))
                pe.wait_ge(sem("router_loaded"), 16)
                for c in range(C):
                    for k in range(KD):
                        last = nc.tensor.matmul(ps[:, 3, c * NE:(c + 1) * NE], hT[:, k, c * P:(c + 1) * P],
                                                rt[:, k, :], start=k == 0, stop=k == KD - 1)
                last.then_inc(sem("logits_done"), 1)
                pe.wait_ge(sem("selected"), 1)
                nc.tensor.matmul(ps[:, 3, 0:NE], before[:], sel[:, 0, :], start=True, stop=True)
                nc.tensor.matmul(ps[:, 3, NE:2 * NE], before[:], sel[:, 1, :], start=True, stop=False)
                nc.tensor.matmul(ps[:, 3, NE:2 * NE], ones[:], sel[:, 0, :], start=False, stop=True)
                nc.tensor.matmul(ps[:, 3, 2 * NE:3 * NE], ones[:], sel[:, 0, :], start=True, stop=False)
                nc.tensor.matmul(ps[:, 3, 2 * NE:3 * NE], ones[:], sel[:, 1, :], start=False,
                                 stop=True).then_inc(sem("places_done"), 1)

                def gather(count):
                    pe.wait_ge(sem("dispatch_ready"), count)
                    for k in range(KD):
                        for c in range(C):
                            last = nc.tensor.matmul(ps[:, 6 + k // 4, k % 4 * P:(k % 4 + 1) * P],
                                                    h[:, c, k * P:(k + 1) * P], disp[:, c, :],
                                                    start=c == 0, stop=c == 1, skip_group_check=True)
                    last.then_inc(sem("gathered"), 1)

                def hidden(bank, m, shift):
                    for i in range(2):
                        w_hi, w_lo = split_tile(m + i, BANK, shift)
                        for k in range(KT):
                            kk = i * KT + k
                            last = split_product(ps[:, bank, :], xe_hi[:, kk, :], xe_lo[:, kk, :], w_hi[:, k, :],
                                                 w_lo[:, k, :], kk == 0, kk == KD - 1)
                        if i == 0:
                            last.then_inc(sem("split_used"), 1)
                    last.then_inc(sem("split_used"), 1)

                def act_transposes(a):
                    pe.wait_ge(sem("act_ready"), a)
                    for j in range(4):
                        last = nc.tensor.transpose(ps[:, 2, j * P:(j + 1) * P], act_out[:, j * P:(j + 1) * P], ident[:])
                    last.then_inc(sem("actT_done"), 1)

                def down(a, m, shift, first, end):
                    pe.wait_ge(sem("actT_ready"), a)
                    for i in range(2):
                        w_hi, w_lo = split_tile(m + i, D, shift)
                        for half in range(2):
                            for j in range(2):
                                t = slice((2 * i + j) * P, (2 * i + j + 1) * P)
                                last = split_product(ps[:, 4 + half, :], aT_hi[:, t], aT_lo[:, t],
                                                     w_hi[:, j, half * BANK:(half + 1) * BANK],
                                                     w_lo[:, j, half * BANK:(half + 1) * BANK],
                                                     first and i == 0 and j == 0, end and i == 1 and j == 1)
                        if i == 0:
                            last.then_inc(sem("split_used"), 1)
                    last.then_inc(sem("split_used"), 1)

                def expert(e, gathers):
                    a0 = NF + NFE * e
                    s0 = MOE_TILES * e
                    M = FFN_TILES
                    pe.wait_ge(sem("xe_ready"), gathers)
                    pe.wait_ge(sem("silu_done"), a0)
                    hidden(0, M, s0)
                    pe.wait_ge(sem("act_ready"), a0)
                    hidden(1, M + 2, s0)

                    def step(f, shift, first):
                        pe.wait_ge(sem("silu_done"), a0 + f)
                        hidden(0, M + 4, shift)
                        act_transposes(a0 + f)
                        hidden(1, M + 6, shift)
                        down(a0 + f, M + 8, shift, first, False)

                    step(1, s0, True)
                    with pe.Fori(2, NFE) as f:
                        step(f, s0 + 6 * (f - 1), False)
                    act_transposes(a0 + NFE)
                    gather(gathers + 1)
                    down(a0 + NFE, M + MOE_TILES - 2, s0, False, True)
                    pe.wait_ge(sem("combine_ready"), e + 1)
                    for c in range(C):
                        last = nc.tensor.transpose(ps[:, 3, c * P:(c + 1) * P], comb[:, c, :], ident[:])
                    last.then_inc(sem("combineT_done"), 1)
                    pe.wait_ge(sem("combineT_ready"), e + 1)
                    pe.wait_ge(sem("y_ready"), e + 1)
                    pe.wait_ge(sem("xe_scaled"), gathers + 1)
                    for c in range(C):
                        for half in range(2):
                            i = 2 * c + half
                            if i == 3:
                                pe.wait_ge(sem("added"), 4 * e + 2)
                            nc.tensor.matmul(ps[:, (3, 6, 7, 3)[i], :], combT[:, c * P:(c + 1) * P],
                                             y_e[:, half * BANK:(half + 1) * BANK], start=True,
                                             stop=True).then_inc(sem("combined"), 1)

                gather(1)
                with pe.Fori(0, NE) as e:
                    expert(e, e + 1)
                pe.wait_ge(sem("routed"), 1)
                busiest = pe.value_load(most[0:1, 0:1])
                with pe.If(busiest > P):
                    pe.wait_ge(sem("added"), 4 * NE + 1)
                    gather(NE + 2)
                    with pe.Fori(0, NE) as e:
                        expert(e + NE, e + NE + 2)

            mixer(0)
            dense()
            mixer(1)
            experts()

        @block.scalar
        def _(act):
            emptied = [0]
            cols = [0]

            def from_batch(moves):
                act.wait_ge(sem("transposed"), emptied[0] + 1)
                for dst, src, scale in moves(ps[:, 4 + emptied[0] % 4, :]):
                    last = nc.scalar.activation(dst, src, ACT.Copy, scale=scale)
                emptied[0] += 1
                last.then_inc(sem("transposed_used"), 1)

            def pairs(dst, q, gain=None):
                def moves(b):
                    if gain is None:
                        return [(dst[:, q:q + 2, :], b.rearrange("p (k t) -> p k t", k=2), 1.0)]
                    return [(dst[:, q + i, :], b[:, i * SEQ:(i + 1) * SEQ], gain(q + i)) for i in range(2)]
                return moves

            def take_columns(dst):
                act.wait_ge(sem("columns_done"), cols[0] + 1)
                pair = 2 * (cols[0] % 2)
                last = nc.scalar.activation(dst, ps[:, pair:pair + 2, 0:dst.shape[2]], ACT.Copy)
                cols[0] += 1
                last.then_inc(sem("columns_used"), 1)

            def sum_squares(slot, src, done):
                for c in range(C):
                    last = nc.scalar.activation(junk(c), src[:, c, :], ACT.Square,
                                                accum_out=ss[:, slot + c:slot + c + 1])
                last.then_inc(sem(done), 1)

            def junk(c):
                return hT[:, 4 * c:4 * c + 4, :].rearrange("p k t -> p (k t)")

            def mixer(l):
                if l == 0:
                    act.wait_ge(sem("mem_loaded"), 16)
                    sum_squares(0, h, "mem_squared")
                    act.wait_ge(sem("x_loaded"), 16)
                    act.wait_ge(sem("mem_squared"), 1)
                if l > 0:
                    act.wait_ge(sem("x_ready"), l)
                sum_squares(2, x, "x_squared")
                if l == 0:
                    for q in range(0, KD, 2):
                        from_batch(pairs(memT, q))
                    act.wait_ge(sem("transposed_used"), emptied[0])
                    act.wait_ge(params, 16 * (3 * L + 5 * L))
                act.wait_ge(sem("x_squared"), 2 * l + 1)
                for k in range(KD):
                    last = nc.scalar.activation(hT[:, k, :], memT[:, k, :], ACT.Copy, scale=gains[:, 1, l, k:k + 1])
                last.then_inc(sem("memT_scaled"), 1)
                act.wait_ge(lparams[l], 16 * 9)
                nc.scalar.activation(dt16[:], dt16[:], ACT.Exp).then_inc(sem("dt_ready"), 1)
                act.wait_ge(sem("angle_ready"), l + 1)
                nc.scalar.activation(sp16[:, 6, :], sp16[:, 2, :], ACT.Exp)
                nc.scalar.activation(sp16[:, 5, :], sp16[:, 9, :], ACT.Sin, scale=-1.0, bias=half_pi[0:NJ, :])
                nc.scalar.activation(sp16[:, 8, :], sp16[:, 4, :], ACT.Sin).then_inc(sem("step_ready"), 1)
                if l == 0:
                    act.wait_ge(sem("rope_angle_ready"), 1)
                    nc.scalar.activation(rope[:, 1], ang[:], ACT.Sin)
                    nc.scalar.activation(rope[:, 0], turns[:], ACT.Sin, scale=-1.0,
                                         bias=half_pi[:]).then_inc(sem("rope_ready"), 1)
                take_columns(kv[:, :, 0:BANK])
                from_batch(lambda b: [(spT[:, 0:6, :], b[:, 0:6 * NJ].rearrange("p (i j) -> p i j", i=6), 1.0)])
                take_columns(kv[:, :, BANK:2 * BANK])
                for r in range(2):
                    from_batch(lambda b: [(bT[:, :, r, :], b.rearrange("p (q s) -> p q s", q=4), 1.0)])
                for r in range(2):
                    def moves(b):
                        v = b.rearrange("p (j g c) -> p j g c", g=2, c=GCH)
                        return [(cT[g * STATE:(g + 1) * STATE, :, r, g * GCH:(g + 1) * GCH],
                                 v[g * STATE:(g + 1) * STATE, :, g, :], 1.0 - 2.0 * r) for g in range(2)]
                    if r == 0:
                        act.wait_ge(sem("cT_zero"), l + 1)
                    from_batch(moves)
                for q in range(0, KD, 2):
                    from_batch(pairs(hT, q, lambda k: gains[:, 0, l, k:k + 1]))
                act.wait_ge(sem("phase_ready"), l + 1)
                nc.scalar.activation(flat(sintab), flat(sintab), ACT.Sin, scale=TWO_PI)
                nc.scalar.activation(flat(costab), flat(costab), ACT.Sin, scale=-TWO_PI,
                                     bias=half_pi[:]).then_inc(sem("rotation_ready"), 1)
                take_columns(z[:, :, 0:BANK])
                take_columns(z[:, :, BANK:2 * BANK])
                for q in range(0, KS, 2):
                    from_batch(pairs(uT, q))
                for n in range(2, IN_FULL):
                    take_columns(z[:, :, n * BANK:(n + 1) * BANK])
                take_columns(z[:, :, IN_FULL * BANK:COLS])
                act.wait_ge(sem("y_used"), KS * (l + 1))
                nc.scalar.activation(flat(gT), flat(gT), ACT.Gelu_apprx_tanh).then_inc(sem("gelu_ready"), 1)
                act.wait_ge(sem("columns_used"), cols[0])
                for c in range(C):
                    last = nc.scalar.activation(z[:, c, GATE0:COLS], z[:, c, GATE0:COLS], ACT.Sigmoid)
                last.then_inc(sem("gates_ready"), 1)
                act.wait_ge(sem("columns_done"), cols[0] + 2)
                pair = 2 * ((cols[0] + 1) % 2)
                act.wait_ge(sem("qk_ready"), l + 1)
                cols[0] += 2
                for qk in range(2):
                    for i in range(0, HEADS // 2, 2):
                        from_batch(pairs(qkT[:, qk], i))
                nc.scalar.activation(sig, ps[:, pair:pair + 2, :], ACT.Sigmoid).then_inc(sem("glu_gate_ready"), 1)
                for dst, g in ((qmT, 0), (kmT, 1)):
                    for i in range(0, XH, 2):
                        from_batch(pairs(dst, i, lambda k: gmq[:, l, g:g + 1]))
                units = C * SLOTS
                for u in range(units):
                    c = u // SLOTS
                    w = NG * (c + 1) * P
                    act.wait_ge(sem("max_ready"), units * l + u + 1)
                    nc.scalar.activation(pr[:, u % 2, 0:w], sc[:, u % 2, 0:w], ACT.Exp, scale=-1.0,
                                         bias=stat[:, u, 0:1], accum_out=stat[:, u, 1:2]).then_inc(sem("probs_ready"), 1)
                    act.wait_ge(sem("probsT_done"), units * l + u + 1)
                    if u > 0:
                        act.wait_ge(sem("attended"), units * l + u)
                    nc.scalar.activation(pT[:, 0:w], flat_banks(4, 2)[:, 0:w], ACT.Copy).then_inc(sem("probsT_ready"), 1)
                for c in range(C):
                    act.wait_ge(sem("mem_max_ready"), C * l + c + 1)
                    for hd in range(XH):
                        last = nc.scalar.activation(
                            t1[:, c, hd * MEM:(hd + 1) * MEM], ps[:, 2 * c + hd // 2, hd % 2 * MEM:(hd % 2 + 1) * MEM],
                            ACT.Exp, scale=XD ** -0.5, bias=rm[:, 0, c, hd:hd + 1], accum_out=rm[:, 1, c, hd:hd + 1])
                    last.then_inc(sem("mem_probs_ready"), 1)
                for c in range(C):
                    act.wait_ge(sem("mem_probsT_done"), C * l + c + 1)
                    nc.scalar.activation(t2[:, c, 0:2 * BANK], flat_banks(4, 2), ACT.Copy).then_inc(
                        sem("mem_probsT_ready"), 1)
                for q in range(0, KS, 2):
                    from_batch(pairs(soT, q))
                from_batch(pairs(oT, 0))
                for q in range(0, XH, 2):
                    from_batch(pairs(omT, q))
                cols[0] += 6
                for q in range(0, KD, 2):
                    from_batch(pairs(hT, q))
                cols[0] += 2
                act.wait_ge(sem("columns_used"), COL_TILES * (l + 1))
                sum_squares(2, x, "x_squared")

            def flat_banks(b, n):
                return ps[:, b:b + n, :].rearrange("p b n -> p (b n)")

            def hi_part(src, src_full, m, shift, after=True):
                act.wait_ge(*src_full)
                if after:
                    act.wait_ge(sem("split_used"), m - H + 1 + shift)
                nc.scalar.activation(hi[:, m % H, :], src, ACT.Copy).then_inc(sem("hi_ready"), 1)

            def dense():
                for q in range(0, KD, 2):
                    def moves(b):
                        return [(hT_hi[:, q + i, :], b[:, i * SEQ:(i + 1) * SEQ], gains[:, 2, 0, q + i:q + i + 1])
                                for i in range(2)]
                    act.wait_ge(sem("transposed"), emptied[0] + 1)
                    for dst, src, scale in moves(ps[:, 4 + emptied[0] % 4, :]):
                        last = nc.scalar.activation(dst, src, ACT.Copy, scale=scale)
                    last.then_inc(sem("hT_hi_ready"), 1)
                    emptied[0] += 1

                def split(m, shift, after=True):
                    n = MIX_TILES + m
                    hi_part(ring[:, n % R, :], (full[n % R], 16 * (n // R + 1 + shift)), m, 3 * shift, after)

                def silu(f, gate_done):
                    act.wait_ge(sem("split_used"), gate_done)
                    nc.scalar.activation(gate_act[:], ps[:, 0, :], ACT.Silu).then_inc(sem("silu_done"), 1)

                def act_hi(f):
                    act.wait_ge(sem("actT_done"), f)
                    nc.scalar.activation(aT_hi[:], ps[:, 2, :], ACT.Copy).then_inc(sem("aT_hi_ready"), 1)

                def step(f, s, wait_act):
                    split(2, s)
                    split(3, s)
                    if wait_act:
                        act.wait_ge(sem("split_used"), 3 * f - 1)
                    act_hi(f)
                    split(4, s)
                    act.wait_ge(sem("act_ready"), f)
                    silu(f, 3 * f)

                split(0, 0, False)
                split(1, 0, False)
                silu(0, 1)
                split(2, 0, False)
                split(3, 0)
                act_hi(1)
                split(4, 0)
                act.wait_ge(sem("act_ready"), 1)
                silu(1, 3)
                with act.Fori(2, NF) as f:
                    step(f, f - 1, True)
                act.wait_ge(sem("split_used"), 3 * NF - 1)
                act_hi(NF)
                split(FFN_TILES - 1, 0)

            def experts():
                for q in range(0, KD, 2):
                    from_batch(pairs(hT, q, lambda k: gains[:, 2, 1, k:k + 1]))
                act.dma_start(rt[:], router[0].rearrange("(k p) e -> p k e", p=P)).then_inc(sem("router_loaded"), 16)
                act.wait_ge(sem("logits_ready"), 1)
                nc.scalar.activation(lg[:].rearrange("p c e -> p (c e)"), lg[:].rearrange("p c e -> p (c e)"),
                                     ACT.Exp).then_inc(sem("routes_exp"), 1)

                def split(c, M, s, turn):
                    hi_part(ring_e[:, c % RM, :], (full_e[c % RM], 16 * (turn + 1)), M, s)

                def expert(e, gathers):
                    a0 = NF + NFE * e
                    t0 = NFE * e
                    s0 = MOE_TILES * e
                    M = FFN_TILES

                    def silu(a, gate_done):
                        act.wait_ge(sem("split_used"), gate_done)
                        act.wait_ge(sem("act_ready"), a)
                        nc.scalar.activation(gate_act[:], ps[:, 0, :], ACT.Silu).then_inc(sem("silu_done"), 1)

                    def act_hi(a, down_done):
                        act.wait_ge(sem("actT_done"), a)
                        act.wait_ge(sem("split_used"), down_done)
                        nc.scalar.activation(aT_hi[:], ps[:, 2, :], ACT.Copy).then_inc(sem("aT_hi_ready"), 1)

                    for i in range(4):
                        split(i, M + i, s0, t0)
                    silu(a0, M + s0 + 2)

                    def step(f, s, turn):
                        for i in range(3):
                            split(4 + i, M + 4 + i, s, turn + (4 + i) // RM)
                        act_hi(a0 + f, M + s + 4)
                        for i in range(3, 5):
                            split(4 + i, M + 4 + i, s, turn + 1)
                        silu(a0 + f, M + s + 6)
                        split(9, M + 9, s, turn + 1)

                    step(1, s0, t0)
                    with act.Fori(2, NFE) as f:
                        step(f, s0 + 6 * (f - 1), t0 + f - 1)
                    act_hi(a0 + NFE, M + s0 + 6 * NFE - 2)
                    for i in range(2):
                        split(4 + i, M + MOE_TILES - 2 + i, s0, t0 + NFE - 1)
                    act.wait_ge(sem("xe_scaled"), gathers + 1)
                    nc.scalar.activation(xe_hi[:], xe[:], ACT.Copy).then_inc(sem("xe_hi_ready"), 1)
                    act.wait_ge(sem("split_used"), M + s0 + MOE_TILES)
                    nc.scalar.activation(y_e[:], flat_banks(4, 2), ACT.Copy).then_inc(sem("y_ready"), 1)

                act.wait_ge(sem("xe_scaled"), 1)
                nc.scalar.activation(xe_hi[:], xe[:], ACT.Copy).then_inc(sem("xe_hi_ready"), 1)
                with act.Fori(0, NE) as e:
                    expert(e, e + 1)
                act.wait_ge(sem("routed"), 1)
                busiest = act.value_load(most[0:1, 0:1])
                with act.If(busiest > P):
                    act.wait_ge(sem("xe_scaled"), NE + 2)
                    nc.scalar.activation(xe_hi[:], xe[:], ACT.Copy).then_inc(sem("xe_hi_ready"), 1)
                    with act.Fori(0, NE) as e:
                        expert(e + NE, e + NE + 2)

            mixer(0)
            dense()
            mixer(1)
            experts()

        @block.vector
        def _(dve):
            done = sem("vector_chain")
            n = [0]
            V = nc.vector

            def chain(ins):
                n[0] += 1
                ins.then_inc(done, 1)
                dve.wait_ge(done, n[0])

            def reduce_angle(r, k, a):
                chain(V.tensor_scalar(k, a, 1 / TWO_PI, ROUND, ALU.mult, ALU.add))
                chain(V.tensor_scalar(k, k, ROUND, None, ALU.subtract))
                chain(V.scalar_tensor_tensor(out=r, in0=k, scalar=-PI_A, in1=a, op0=ALU.mult, op1=ALU.add))
                chain(V.scalar_tensor_tensor(out=r, in0=k, scalar=-PI_B, in1=r, op0=ALU.mult, op1=ALU.add))
                chain(V.scalar_tensor_tensor(out=r, in0=k, scalar=-PI_C, in1=r, op0=ALU.mult, op1=ALU.add))
                chain(V.tensor_scalar(r, r, 3.1415925, -3.1415925, ALU.min, ALU.max))
                return V.scalar_tensor_tensor(out=k, in0=r, scalar=-1.0, in1=r, op0=ALU.mult, op1=ALU.max)

            def scale_rows(dst, src, r0):
                for c in range(C):
                    last = V.tensor_scalar(dst[:, c, :], src[:, c, :], rs[:, r0 + c:r0 + c + 1], None, ALU.mult)
                return last

            def setup():
                dve.wait_ge(sem("mem_rs"), 1)
                scale_rows(h, h, 0).then_inc(sem("h_ready"), 1)

            def constants():
                dve.wait_ge(sem("consts_ready"), 1)
                V.tensor_copy(ramp[:], ramp_i[:])
                for c in range(C):
                    for i, g in enumerate((1, 2)):
                        chain(V.tensor_scalar(grid_i[:, i, :], dist_i[:, c, :], DIL[g] - 1, None, ALU.bitwise_and))
                        last = V.tensor_scalar(gmask(c, g), grid_i[:, i, 0:(c + 1) * P], 0, NEG, ALU.is_gt, ALU.mult)
                last.then_inc(sem("grid_ready"), 1)
                dve.wait_ge(sem("pos_loaded"), 16)
                chain(V.tensor_copy(pos[:], pos_i[:]))
                for c in range(C):
                    last = V.tensor_scalar(turns[:, c, :], invf[:], pos[:, c:c + 1], None, ALU.mult)
                chain(last)
                chain(V.tensor_copy(ang[:], turns[:]))
                reduce_angle(ang[:], turns[:], ang[:]).then_inc(sem("rope_angle_ready"), 1)

            def ssm_setup(l):
                s = sp16
                if l > 0:
                    dve.wait_ge(sem("x_ready"), l)
                dve.wait_ge(lparams[l], 16 * 9)
                dve.wait_ge(sem("dt_ready"), l + 1)
                dt = spread(dt16[:], 2, STATE)
                for i in range(2):
                    last = V.tensor_tensor(s[:, 2 + i, :].rearrange("j (g p) -> j g p", g=2),
                                           s[:, i, :].rearrange("j (g p) -> j g p", g=2), dt, ALU.mult)
                chain(last)
                reduce_angle(s[:, 4, :], s[:, 9, :], s[:, 3, :]).then_inc(sem("angle_ready"), 1)
                chain(V.tensor_scalar(s[:, 10, :], s[:, 4, :], 1 / TWO_PI, None, ALU.mult))
                chain(V.tensor_scalar(s[:, 11, :], s[:, 10, :], ROUND_FINE, None, ALU.add))
                chain(V.tensor_scalar(s[:, 11, :], s[:, 11, :], ROUND_FINE, None, ALU.subtract))
                dve.wait_ge(sem("step_ready"), l + 1)
                V.tensor_tensor(s[:, 8, :], s[:, 8, :], s[:, 6, :], ALU.mult)
                chain(V.tensor_tensor(s[:, 5, :], s[:, 5, :], s[:, 6, :], ALU.mult))
                chain(V.tensor_scalar(s[:, 5, :], s[:, 5, :], 1.0, None, ALU.subtract))
                V.tensor_tensor(s[:, 2, :], s[:, 5, :], s[:, 0, :], ALU.mult)
                V.tensor_tensor(s[:, 9, :], s[:, 8, :], s[:, 1, :], ALU.mult)
                V.tensor_tensor(s[:, 3, :], s[:, 8, :], s[:, 0, :], ALU.mult)
                chain(V.tensor_tensor(s[:, 7, :], s[:, 5, :], s[:, 1, :], ALU.mult))
                V.tensor_tensor(s[:, 2, :], s[:, 2, :], s[:, 9, :], ALU.add)
                chain(V.tensor_tensor(s[:, 3, :], s[:, 3, :], s[:, 7, :], ALU.subtract))
                V.tensor_tensor(s[:, 0, :], s[:, 0, :], s[:, 0, :], ALU.mult)
                chain(V.tensor_tensor(s[:, 1, :], s[:, 1, :], s[:, 1, :], ALU.mult))
                chain(V.tensor_tensor(s[:, 0, :], s[:, 0, :], s[:, 1, :], ALU.add))
                chain(V.reciprocal(s[:, 0, :], s[:, 0, :]))
                V.tensor_tensor(s[:, 2, :], s[:, 2, :], s[:, 0, :], ALU.mult)
                V.tensor_tensor(s[:, 3, :], s[:, 3, :], s[:, 0, :], ALU.mult).then_inc(sem("ssm_params"), 1)
                dve.wait_ge(sem("x_rs"), 2 * l + 1)
                if l == 0:
                    dve.wait_ge(sem("transposed"), 4)
                scale_rows(h, x, 2).then_inc(sem("h_ready"), 1)
                V.memset(b_bar, 0.0)
                V.memset(cT[:], 0.0).then_inc(sem("cT_zero"), 1)
                dve.wait_ge(sem("transposed_used"), batches_to(l, "ssm"))
                f_re, f_im = spread(spT[:, 4, :], 2, GCH), spread(spT[:, 5, :], 2, GCH)
                for r, (p, q, op) in enumerate(((f_re, f_im, ALU.subtract), (f_im, f_re, ALU.add))):
                    V.tensor_tensor(b_tmp, b_raw[:, 0], p, ALU.mult)
                    chain(V.tensor_tensor(b_tmp2, b_raw[:, 1], q, ALU.mult))
                    for g in range(2):
                        rows = slice(g * STATE, (g + 1) * STATE)
                        last = V.tensor_tensor(b_bar[rows, r, :, g * GCH:(g + 1) * GCH], b_tmp[rows], b_tmp2[rows], op)
                    chain(last)
                last = V.memset(stat[:, 0, 3:4], 0.0)
                last.then_inc(sem("b_bar_ready"), 1)
                if l == 0:
                    dve.wait_ge(sem("rope_ready"), 1)
                for j in range(NJ):
                    last = V.tensor_scalar(costab[:, j, :], ramp[:], spT[:, 2, j:j + 1], ROUND, ALU.mult, ALU.add)
                chain(last)
                chain(V.tensor_scalar(flat(costab), flat(costab), ROUND, None, ALU.subtract))
                for j in range(NJ):
                    last = V.scalar_tensor_tensor(out=sintab[:, j, :], in0=ramp[:], scalar=spT[:, 3, j:j + 1],
                                                  in1=costab[:, j, :], op0=ALU.mult, op1=ALU.subtract)
                V.tensor_tensor(spT[:, 6, :], spT[:, 2, :], spT[:, 3, :], ALU.subtract)
                chain(last)
                chain(V.memset(stat[:, 0, 3:4], 0.0))
                for j in range(NJ):
                    last = V.scalar_tensor_tensor(out=sintab[:, j, :], in0=ramp[:], scalar=spT[:, 6, j:j + 1],
                                                  in1=sintab[:, j, :], op0=ALU.mult, op1=ALU.add)
                chain(last)
                chain(V.tensor_scalar(flat(sintab), flat(sintab), 0.4999999, -0.4999999, ALU.min, ALU.max))
                V.scalar_tensor_tensor(out=flat(costab), in0=flat(sintab), scalar=-1.0, in1=flat(sintab),
                                       op0=ALU.mult, op1=ALU.max).then_inc(sem("phase_ready"), 1)

            def ssm(l):
                dve.wait_ge(sem("rotation_ready"), l + 1)
                for v in range(NJ // 2):
                    j = 2 * v
                    cos, sin = costab[:, j:j + 2, :], sintab[:, j:j + 2, :]
                    bu = ps[:, 4:6, :].rearrange("p j (r t) -> p j r t", r=2)
                    dve.wait_ge(sem("bu_done"), NJ // 2 * l + v + 1)
                    V.tensor_tensor(wa[:], bu, spread(cos, 2, 2), ALU.mult)
                    V.tensor_tensor(wb[:, :, 0, :], bu[:, :, 1, :], sin, ALU.mult)
                    last = V.tensor_tensor(wb[:, :, 1, :], bu[:, :, 0, :], sin, ALU.mult)
                    last.then_inc(sem("bu_used"), 1)
                    dve.wait_ge(sem("bu_used"), NJ // 2 * l + v + 1)
                    V.tensor_tensor(wv[:, :, 0, :], wa[:, :, 0, :], wb[:, :, 0, :], ALU.add)
                    chain(V.tensor_tensor(wv[:, :, 1, :], wa[:, :, 1, :], wb[:, :, 1, :], ALU.subtract))
                    for i in range(2):
                        for r in range(2):
                            last = V.tensor_tensor_scan(wp[:, i, r, :], spT[:, 0, j + i:j + i + 1].to_broadcast([P, SEQ]),
                                                        wv[:, i, r, :], 0.0, ALU.mult, ALU.add)
                    chain(last)
                    V.tensor_tensor(wa[:], wp[:], spread(cos, 2, 2), ALU.mult)
                    chain(V.tensor_tensor(wb[:], wp[:], spread(sin, 2, 2), ALU.mult))
                    V.tensor_tensor(wv[:, :, 0, :], wa[:, :, 0, :], wb[:, :, 1, :], ALU.subtract)
                    V.tensor_tensor(wv[:, :, 1, :], wa[:, :, 1, :], wb[:, :, 0, :], ALU.add).then_inc(
                        sem("states_ready"), 1)
                    if v % 2 == 1:
                        q = v // 2
                        dve.wait_ge(sem("y_done"), NJ // 2 * l + v + 1)
                        if q == 0:
                            dve.wait_ge(params, 16 * (3 * L + 5 * L))
                        last = V.scalar_tensor_tensor(out=gT[:, q, :], in0=uT[:, q, :], scalar=dsk[:, l, q:q + 1],
                                                      in1=ps[:, 6, q % 2 * SEQ:(q % 2 + 1) * SEQ], op0=ALU.mult,
                                                      op1=ALU.add)
                        last.then_inc(sem("y_used"), 1)

            def attention_inputs(l):
                if l == 0:
                    dve.wait_ge(sem("rope_ready"), 1)
                for qk in range(2):
                    for r in range(2):
                        for half in range(2):
                            g = gqk[:, l, qk, half * 32:(half + 1) * 32]
                            last = V.tensor_tensor(rgain[:, qk, r, :, half * 32:(half + 1) * 32], rope[:, r],
                                                   spread(g, 1, C), ALU.mult)
                chain(last)
                dve.wait_ge(sem("columns_used"), COL_TILES * l + 2 + IN_FULL + 1)
                qk = z[:, :, Q0:Q0 + 2 * AW]
                by_head = qk.rearrange("p c (h d) -> p c h d", d=HD)
                chain(V.tensor_tensor(t1[:], qk, qk, ALU.mult))
                V.tensor_reduce(rqk[:], t1[:].rearrange("p c (h d) -> p c h d", d=HD), AX.X, ALU.add).then_inc(
                    sem("qk_squared"), 1)
                mq = z[:, :, MQ0:MQ0 + XW]
                mk = kv[:, :, 0:XW]
                chain(V.tensor_tensor(t2[:, :, 0:XW], mq, mq, ALU.mult))
                chain(V.tensor_tensor(t2[:, :, XW:2 * XW], mk, mk, ALU.mult))
                for i in range(2):
                    last = V.tensor_reduce(rm[:, i], t2[:, :, i * XW:(i + 1) * XW].rearrange(
                        "p c (h d) -> p c h d", d=XD), AX.X, ALU.add)
                last.then_inc(sem("mqk_squared"), 1)
                dve.wait_ge(sem("qk_squared"), l + 1)
                dve.wait_ge(sem("mqk_squared"), l + 1)
                for t, r in ((t1, 0), (t2, 1)):
                    for i in range(2):
                        for c in range(C):
                            w = slice(i * AW, (i + 1) * AW)
                            last = V.tensor_tensor(t[:, c, w].rearrange("p (h d) -> p h d", d=HD),
                                                   qk[:, c, w].rearrange("p (h d) -> p h d", d=HD),
                                                   spread(rgain[:, i, r, c, :], 1, HEADS), ALU.mult)
                chain(last)
                a = t1[:].rearrange("p c (h d) -> p c h d", d=HD)
                b = t2[:].rearrange("p c (h d) -> p c h d", d=HD)
                lo_, hi_ = slice(0, HD // 2), slice(HD // 2, HD)
                V.tensor_tensor(by_head[:, :, :, lo_], a[:, :, :, lo_], b[:, :, :, hi_], ALU.subtract)
                chain(V.tensor_tensor(by_head[:, :, :, hi_], b[:, :, :, lo_], a[:, :, :, hi_], ALU.add))
                dve.wait_ge(sem("qk_rs"), l + 1)
                V.tensor_tensor(by_head, by_head, spread(rqk2[:], 3, HD), ALU.mult).then_inc(sem("qk_ready"), 1)
                dve.wait_ge(sem("mqk_rs"), l + 1)
                for i, t in enumerate((mq, mk)):
                    v = t.rearrange("p c (h d) -> p c h d", d=XD)
                    last = V.tensor_tensor(v, v, spread(rm2[:, i], 3, XD), ALU.mult)
                last.then_inc(sem("mqk_ready"), 1)

            def attention(l):
                units = C * SLOTS

                def take(u):
                    c, s = u // SLOTS, u % SLOTS
                    dve.wait_ge(sem("attended"), units * l + u + 1)
                    chain(V.reciprocal(stat[:, u, 2:3], stat[:, u, 1:2]))
                    V.tensor_scalar(oatt[:, c, s * HD:(s + 1) * HD], ps[:, 6 + u % 2, 0:HD], stat[:, u, 2:3], None,
                                    ALU.mult).then_inc(sem("att_out_ready"), 1)

                if l == 0:
                    dve.wait_ge(sem("mask_ready"), 1)
                for u in range(units):
                    c = u // SLOTS
                    w = NG * (c + 1) * P
                    dve.wait_ge(sem("scores_done"), units * l + u + 1)
                    if u >= 2:
                        dve.wait_ge(sem("probs_ready"), units * l + u - 1)
                    last = V.scalar_tensor_tensor(
                        out=sc[:, u % 2, 0:w], in0=ps[:, 2 * (u % 2):2 * (u % 2) + 2, :].rearrange(
                            "p b n -> p (b n)")[:, 0:w], scalar=-HD ** -0.5,
                        in1=mask[:, c * NG * P:c * NG * P + w], op0=ALU.mult, op1=ALU.subtract)
                    last.then_inc(sem("scores_used"), 1)
                    dve.wait_ge(sem("scores_used"), units * l + u + 1)
                    V.tensor_reduce(stat[:, u, 0:1], sc[:, u % 2, 0:w], AX.X, ALU.min).then_inc(sem("max_ready"), 1)
                    if u >= 2:
                        take(u - 2)
                take(units - 2)
                take(units - 1)
                for c in range(C):
                    dve.wait_ge(sem("mem_scores_done"), C * l + c + 1)
                    chain(V.tensor_reduce(rm2[:, 0, c, :], ps[:, 2 * c:2 * c + 2, :].rearrange(
                        "p b (h m) -> p (b h) m", m=MEM), AX.X, ALU.max))
                    V.tensor_scalar(rm[:, 0, c, :], rm2[:, 0, c, :], -XD ** -0.5, None, ALU.mult).then_inc(
                        sem("mem_max_ready"), 1)
                for c in range(C):
                    dve.wait_ge(sem("mem_attended"), C * l + c + 1)
                    chain(V.reciprocal(rm2[:, 1, c, :], rm[:, 1, c, :]))
                    V.tensor_tensor(omem[:, c, :].rearrange("p (h d) -> p h d", d=XD),
                                    ps[:, 7, :].rearrange("p (h d) -> p h d", d=XD),
                                    spread(rm2[:, 1, c, :], 2, XD), ALU.mult).then_inc(sem("mem_out_ready"), 1)

            def glu(l):
                dve.wait_ge(sem("glu_gate_ready"), l + 1)
                pair = 2 * (cols[0] % 2)
                last = V.tensor_tensor(sout, ps[:, pair:pair + 2, :], sig, ALU.mult)
                last.then_inc(sem("columns_used"), 2)
                cols[0] += 2

            cols = [0]
            CT = 2 + IN_FULL + 1

            def merge(l):
                dve.wait_ge(sem("gates_ready"), l + 1)
                for b in range(3):
                    for half in range(2):
                        dve.wait_ge(sem("columns_done"), cols[0] + 1)
                        pair = 2 * (cols[0] % 2)
                        o = slice(half * BANK, (half + 1) * BANK)
                        g = z[:, :, GATE0 + b * D + half * BANK:GATE0 + b * D + (half + 1) * BANK]
                        if b == 0:
                            last = V.tensor_tensor(merged[:, :, o], ps[:, pair:pair + 2, :], g, ALU.mult)
                            last.then_inc(sem("columns_used"), 1)
                            dve.wait_ge(sem("columns_used"), cols[0] + 1)
                        else:
                            last = V.tensor_tensor(g, ps[:, pair:pair + 2, :], g, ALU.mult)
                            last.then_inc(sem("columns_used"), 1)
                            dve.wait_ge(sem("columns_used"), cols[0] + 1)
                            last = V.tensor_tensor(merged[:, :, o], merged[:, :, o], g, ALU.add)
                            if b == 2 and half == 1:
                                last.then_inc(sem("merged_ready"), 1)
                            else:
                                chain(last)
                        cols[0] += 1
                for half in range(2):
                    dve.wait_ge(sem("columns_done"), cols[0] + 1)
                    pair = 2 * (cols[0] % 2)
                    o = slice(half * BANK, (half + 1) * BANK)
                    last = V.tensor_tensor(x[:, :, o], ps[:, pair:pair + 2, :], x[:, :, o], ALU.add)
                    last.then_inc(sem("columns_used"), 1)
                    cols[0] += 1
                dve.wait_ge(sem("x_rs"), 2 * l + 2)
                scale_rows(h, x, 2).then_inc(sem("h_ready"), 1)

            def lo_part(src, m, shift):
                dve.wait_ge(sem("hi_ready"), m + 1 + shift)
                last = V.tensor_tensor(lo[:, m % H, :], src, hi[:, m % H, :].bitcast(F32), ALU.subtract)
                last.then_inc(sem("lo_ready"), 1)

            def act_low(a):
                dve.wait_ge(sem("aT_hi_ready"), a)
                V.tensor_tensor(aT_lo[:], ps[:, 2, :], aT_hi[:].bitcast(F32), ALU.subtract).then_inc(
                    sem("actT_ready"), 1)

            def act_product(a, up_done):
                dve.wait_ge(sem("split_used"), up_done)
                dve.wait_ge(sem("silu_done"), a)
                V.tensor_tensor(act_out[:], ps[:, 1, :], gate_act[:], ALU.mult).then_inc(sem("act_ready"), 1)

            def dense():
                for q in range(0, KD, 2):
                    dve.wait_ge(sem("hT_hi_ready"), q // 2 + 1)
                    for i in range(2):
                        b = ps[:, 4 + (batches_to(0, "merged") + q // 2) % 4, i * SEQ:(i + 1) * SEQ]
                        last = V.scalar_tensor_tensor(out=hT_lo[:, q + i, :], in0=b, scalar=gains[:, 2, 0, q + i:q + i + 1],
                                                      in1=hT_hi[:, q + i, :].bitcast(F32), op0=ALU.mult,
                                                      op1=ALU.subtract)
                    last.then_inc(sem("transposed_used"), 1)

                def split(m, shift):
                    n_ = MIX_TILES + m
                    lo_part(ring[:, n_ % R, :], m, 3 * shift)

                split(0, 0)
                split(1, 0)
                act_product(1, 2)

                def step(f, s):
                    split(2, s)
                    split(3, s)
                    act_low(f)
                    split(4, s)
                    act_product(f + 1, 3 * f + 1)
                with dve.Fori(1, NF) as f:
                    step(f, f - 1)
                act_low(NF)
                split(FFN_TILES - 1, 0)
                dve.wait_ge(sem("split_used"), FFN_TILES)
                for c in range(C):
                    last = V.tensor_tensor(x[:, c, :], ps[:, 4 + 2 * c:6 + 2 * c, :].rearrange("p b n -> p (b n)"),
                                           x[:, c, :], ALU.add)
                last.then_inc(sem("x_ready"), 1)
                dve.wait_ge(sem("x_ready"), 1)

            def route():
                for c in range(1):
                    V.memset(slot_of[:], -1.0)
                V.memset(tie[:], 0.0)
                chain(V.memset(rstat[:], 0.0))
                for e in range(1, NE):
                    last = V.memset(tie[:, e, 0:e], 1.0)
                dve.wait_ge(sem("logits_done"), 1)
                chain(V.tensor_copy(lg[:], ps[:, 3, 0:C * NE].rearrange("p (c e) -> p c e", c=C)))
                mine = spread(lg[:], 3, NE)
                other = spread(lg[:], 2, NE)
                for c in range(C):
                    V.tensor_tensor(cmp_[:, 0, c], other[:, c], mine[:, c], ALU.is_gt)
                    chain(V.tensor_tensor(cmp_[:, 1, c], other[:, c], mine[:, c], ALU.is_equal))
                    chain(V.tensor_tensor(cmp_[:, 1, c], cmp_[:, 1, c], tie[:], ALU.mult))
                    chain(V.tensor_tensor(cmp_[:, 0, c], cmp_[:, 0, c], cmp_[:, 1, c], ALU.add))
                chain(V.tensor_reduce(sel[:], cmp_[:, 0], AX.X, ALU.add))
                last = V.tensor_scalar(sel[:], sel[:], 2.0, None, ALU.is_lt)
                last.then_inc(sem("selected"), 1)
                dve.wait_ge(sem("selected"), 1)
                chain(V.tensor_reduce(rstat[:, 0:2], lg[:], AX.X, ALU.max))
                V.tensor_tensor(lg[:], lg[:], spread(rstat[:, 0:2], 2, NE), ALU.subtract).then_inc(
                    sem("logits_ready"), 1)
                dve.wait_ge(sem("routes_exp"), 1)
                chain(V.tensor_tensor(gate[:], lg[:], sel[:], ALU.mult))
                chain(V.tensor_reduce(rstat[:, 2:4], gate[:], AX.X, ALU.add))
                chain(V.reciprocal(rstat[:, 2:4], rstat[:, 2:4]))
                chain(V.tensor_tensor(gate[:], gate[:], spread(rstat[:, 2:4], 2, NE), ALU.mult))
                dve.wait_ge(sem("places_done"), 1)
                where = slot_of[:, :, 0:NE]
                chain(V.tensor_scalar(where, ps[:, 3, 0:C * NE].rearrange("p (c e) -> p c e", c=C), 1.0, None, ALU.add))
                chain(V.tensor_tensor(where, where, sel[:], ALU.mult))
                chain(V.tensor_scalar(where, where, 1.0, None, ALU.subtract))
                chain(V.tensor_reduce(rstat[:, 4:5], ps[:, 3, 2 * NE:3 * NE], AX.X, ALU.max))
                last = V.tensor_copy(most[:], rstat[:, 4:5])
                last.then_inc(sem("routed"), 1)
                V.memset(rstat[:, 5:6], 0.0).then_inc(sem("added"), 1)

            def experts():
                route()

                def dispatch(e):
                    for c in range(C):
                        last = V.tensor_scalar(disp[:, c, :], ramp[:, 0:P], slot_of[:, c, bass.ds(e, 1)], None,
                                               ALU.is_equal)
                    last.then_inc(sem("dispatch_ready"), 1)

                def scale_gathered(count):
                    dve.wait_ge(sem("gathered"), count)
                    V.tensor_tensor(xe[:], ps[:, 6:8, :].rearrange("p b (k t) -> p (b k) t", t=P),
                                    spread(gains[:, 2, 1, :], 2, P), ALU.mult).then_inc(sem("xe_scaled"), 1)

                def gathered_low(count):
                    dve.wait_ge(sem("xe_hi_ready"), count)
                    V.tensor_tensor(xe_lo[:], xe[:], xe_hi[:].bitcast(F32), ALU.subtract).then_inc(
                        sem("xe_ready"), 1)

                def split(c, M, s):
                    lo_part(ring_e[:, c % RM, :], M, s)

                def expert(e_here, e, gathers):
                    a0 = NF + NFE * e
                    s0 = MOE_TILES * e
                    M = FFN_TILES
                    for i in range(4):
                        split(i, M + i, s0)
                    dve.wait_ge(sem("gathered"), gathers)
                    dispatch(e_here + 1)
                    for c in range(C):
                        last = V.tensor_scalar(comb[:, c, :], ramp[:, 0:P], slot_of[:, c, bass.ds(e_here, 1)],
                                               gate[:, c, bass.ds(e_here, 1)], ALU.is_equal, ALU.mult)
                    last.then_inc(sem("combine_ready"), 1)
                    act_product(a0 + 1, M + s0 + 4)

                    def step(f, s):
                        for i in range(3):
                            split(4 + i, M + 4 + i, s)
                        act_low(a0 + f)
                        for i in range(3, 6):
                            split(4 + i, M + 4 + i, s)
                        act_product(a0 + f + 1, M + s + 8)
                    with dve.Fori(1, NFE) as f:
                        step(f, s0 + 6 * (f - 1))
                    act_low(a0 + NFE)
                    split(4, M + MOE_TILES - 2, s0)
                    scale_gathered(gathers + 1)
                    split(5, M + MOE_TILES - 1, s0)
                    gathered_low(gathers + 1)
                    dve.wait_ge(sem("combineT_done"), e + 1)
                    V.tensor_copy(combT[:], ps[:, 3, 0:C * P]).then_inc(sem("combineT_ready"), 1)
                    dve.wait_ge(sem("added"), 4 * e + 1)
                    for c in range(C):
                        for half in range(2):
                            i = 2 * c + half
                            o = slice(half * BANK, (half + 1) * BANK)
                            dve.wait_ge(sem("combined"), 4 * e + i + 1)
                            V.tensor_tensor(x[:, c, o], ps[:, (3, 6, 7, 3)[i], :], x[:, c, o], ALU.add).then_inc(
                                sem("added"), 1)

                dve.wait_ge(sem("routed"), 1)
                dispatch(0)
                scale_gathered(1)
                gathered_low(1)
                with dve.Fori(0, NE) as e:
                    expert(e, e, e + 1)
                busiest = dve.value_load(most[0:1, 0:1])
                with dve.If(busiest > P):
                    dve.wait_ge(sem("gathered"), NE + 1)
                    V.tensor_scalar(slot_of[:], slot_of[:], float(P), None, ALU.subtract).then_inc(sem("slots_moved"), 1)
                    dve.wait_ge(sem("slots_moved"), 1)
                    dispatch(0)
                    scale_gathered(NE + 2)
                    gathered_low(NE + 2)
                    with dve.Fori(0, NE) as e:
                        expert(e, e + NE, e + NE + 2)
                V.memset(rstat[:, 0:1], 0.0).then_inc(sem("x_final"), 1)

            setup()
            constants()
            for l in range(L):
                ssm_setup(l)
                ssm(l)
                attention_inputs(l)
                cols[0] += CT
                glu(l)
                attention(l)
                merge(l)
                if l == 0:
                    dense()
            experts()


_INS = ['x', 'mem', 'positions', 'norm_mix', 'w_in', 'ssm_a_re', 'ssm_a_im', 'ssm_log_dt', 'ssm_b_re', 'ssm_b_im',
        'ssm_c_re', 'ssm_c_im', 'ssm_d', 'ssm_w_glu', 'w_ssm_out', 'att_q_norm', 'att_k_norm', 'w_att_out',
        'norm_mem', 'w_mem_kv', 'mem_q_norm', 'mem_k_norm', 'w_mem_out', 'w_o', 'norm_ffn', 'ffn_w_gate',
        'ffn_w_up', 'ffn_w_down', 'moe_w_router', 'moe_w_gate', 'moe_w_up', 'moe_w_down']


def kernel(**inputs):
    import numpy as _np
    import concourse.bacc as _bacc
    from concourse import mybir as _mybir
    from concourse.bass_utils import run_bass_kernel_spmd as _run

    nc = _bacc.Bacc("TRN2", target_bir_lowering=False, num_devices=1)
    arrays, args = {}, []
    for name in _INS:
        a = _np.ascontiguousarray(inputs[name])
        arrays[f"in_{name}"] = a
        args.append(nc.dram_tensor(f"in_{name}", a.shape, _mybir.dt.from_np(a.dtype), kind="ExternalInput").ap())
    shape = inputs["x"].shape
    args.append(nc.dram_tensor("out", shape, _mybir.dt.float32, kind="ExternalOutput").ap())
    decoder_trunk(nc, *args)
    r = _run(nc, [arrays], core_ids=[0])
    return r.results[0]["out"]
```

```python
import math
from contextlib import ExitStack

import numpy as np
import concourse.bass as bass
from concourse import mybir

F32 = mybir.dt.float32
F32R = mybir.dt.float32r
I32 = mybir.dt.int32
ALU = mybir.AluOpType
ACT = mybir.ActivationFunctionType
AX = mybir.AxisListType

P = 128
BANK = 512
NEG = -1e30
EPS = 1e-6
TWO_PI = 2 * math.pi
ROUND = 1.5 * 2.0 ** 23
ROUND_FINE = ROUND * 2.0 ** -14
PI_A = 6.28125
PI_B = float(np.float32(np.round((TWO_PI - PI_A) * 2 ** 22) / 2 ** 22))
PI_C = float(np.float32(TWO_PI - PI_A - PI_B))


def decoder_trunk(nc, x_in, mem_in, positions, norm_mix, w_in, a_re, a_im, log_dt, b_re, b_im,
                  c_re, c_im, ssm_d, w_glu, w_ssm_out, g_q, g_k, w_att_out, norm_mem, w_mem_kv,
                  g_mq, g_mk, w_mem_out, w_o, norm_ffn, ffn_gate, ffn_up, ffn_down, router,
                  moe_gate, moe_up, moe_down, out, dbg=None):
    _, SEQ, D = x_in.shape
    MEM = mem_in.shape[1]
    L = norm_mix.shape[0]
    C = SEQ // P
    KD = D // P
    COLS = w_in.shape[2]
    GROUPS, STATE = a_re.shape[1:]
    GCH = b_re.shape[3]
    SSM = GROUPS * GCH
    KS = SSM // P
    NJ = GROUPS * STATE // P
    HD = g_q.shape[1]
    SLOTS = w_att_out.shape[1] // HD
    DIL = (1, 4, 16)
    SPAN = 128
    NG = len(DIL)
    HEADS = NG * SLOTS
    AW = HEADS * HD
    XD = g_mq.shape[1]
    XW = w_mem_kv.shape[2] // 2
    XH = XW // XD
    Q0, K0, V0, MQ0, GATE0 = SSM, SSM + AW, SSM + 2 * AW, SSM + 3 * AW, SSM + 3 * AW + XW
    FF = ffn_gate.shape[2]
    NE = router.shape[2]
    FE = moe_gate.shape[3]
    assert SEQ == MEM == 2 * P and 2 * STATE == P and L == 2 and HD == 64 and XD == P

    TILE = 2048
    KT = TILE // BANK
    R = 3
    RM = 6
    H = 3
    KV_TILES, IN_FULL = 4, COLS // BANK
    MIX_TILES = KV_TILES + 2 * IN_FULL + 1 + 2 + 2 + 1 + 2 + 4
    NF = FF // 256
    FFN_TILES = 3 * NF
    NFE = FE // BANK
    MOE_TILES = 6 * NFE
    assert COLS == IN_FULL * BANK + 256 and FF % 256 == 0 and FE % BANK == 0 and NF % 2 == 1
    assert FFN_TILES % H == 0 and MOE_TILES % RM == 0

    ctx = ExitStack()
    sems = {}

    def sem(name):
        if name not in sems:
            sems[name] = ctx.enter_context(nc.semaphore(name))
        return sems[name]

    def buffers(stack):
        return lambda name, shape, dt=F32: stack.enter_context(nc.sbuf_tensor(name, shape, dt))

    with ctx:
        sb = buffers(ctx)
        ps = ctx.enter_context(nc.psum_tensor("ps", [P, 8, BANK], F32))

        x = sb("x", [P, C, D])
        h = sb("h", [P, C, D])
        hT = sb("hT", [P, KD, SEQ])
        ring = sb("ring", [P, R, TILE])
        ident = sb("ident", [P, P])
        ones = sb("ones", [P, P])
        before = sb("before", [P, P])
        ramp_i = sb("ramp_i", [P, SEQ], I32)
        ramp = sb("ramp", [P, SEQ])
        gains = sb("gains", [P, 3, L, KD])
        ss = sb("ss", [P, 4])
        rs = sb("rs", [P, 4])
        half_neg = sb("half_neg", [P, 64])
        half_pi = sb("half_pi", [P, 1])

        memT = sb("memT", [P, KD, MEM])
        mask = sb("mask", [P, NG * 3 * P])
        dsk = sb("dsk", [P, L, KS])
        gmq = sb("gmq", [P, L, 2])
        gqk = sb("gqk", [P, L, 2, HD])
        rope = sb("rope", [P, 2, C, HD // 2])

        mix = ExitStack()
        mb = buffers(mix)
        z = mb("z", [P, C, COLS])
        kv = mb("kv", [P, C, 2 * XW])
        uT = mb("uT", [P, KS, SEQ])
        gT = mb("gT", [P, KS, SEQ])
        qmT = mb("qmT", [P, XH, SEQ])
        kmT = mb("kmT", [P, XH, MEM])
        bT = mb("bT", [P, NJ // 4, 2, P])
        cT = mb("cT", [P, NJ, 2, 2 * GCH])
        pos_i = mb("pos_i", [P, C], I32)
        pos = mb("pos", [P, C])
        rgain = mb("rgain", [P, 2, 2, C, HD])
        spT = mb("spT", [P, 8, NJ])
        dt16 = mb("dt16", [NJ, 2])
        rqk = mb("rqk", [P, C, 2 * HEADS])
        rqk2 = mb("rqk2", [P, C, 2 * HEADS])
        rm = mb("rm", [P, 2, C, XH])
        rm2 = mb("rm2", [P, 2, C, XH])
        stat = mb("stat", [P, 8, 4])
        early = ExitStack()
        eb = buffers(early)
        costab = eb("costab", [P, NJ, SEQ])
        sintab = eb("sintab", [P, NJ, SEQ])
        wa = eb("wa", [P, 2, 2, SEQ])
        wb = eb("wb", [P, 2, 2, SEQ])
        wv = eb("wv", [P, 2, 2, SEQ])
        wp = eb("wp", [P, 2, 2, SEQ])
        early.close()
        first = ExitStack()
        sb1 = buffers(first)
        invf = sb1("invf", [P, HD // 2])
        dist_i = sb1("dist_i", [P, C, SEQ], I32)
        grid_i = sb1("grid_i", [P, 2, SEQ], I32)
        ang = sb1("ang", [P, C, HD // 2])
        turns = sb1("turns", [P, C, HD // 2])
        first.close()
        late = ExitStack()
        lb = buffers(late)
        t1 = lb("t1", [P, C, 2 * AW])
        t2 = lb("t2", [P, C, 2 * AW])
        qkT = lb("qkT", [P, 2, HEADS // 2, SEQ])
        sc = lb("sc", [P, 2, NG * 2 * P])
        pr = lb("pr", [P, 2, NG * 2 * P])
        pT = lb("pT", [P, NG * 2 * P])
        late.close()
        last_ring = ExitStack()
        ring_e = buffers(last_ring)("ring_e", [P, RM, TILE])
        last_ring.close()
        mix.close()

        ffn = ExitStack()
        fb = buffers(ffn)
        hi = fb("hi", [P, H, TILE], F32R)
        lo = fb("lo", [P, H, TILE], F32R)
        aT_hi = fb("aT_hi", [P, BANK], F32R)
        aT_lo = fb("aT_lo", [P, BANK], F32R)
        gate_act = fb("gate_act", [P, BANK])
        act_out = fb("act_out", [P, BANK])
        dense_only = ExitStack()
        hT_hi = buffers(dense_only)("hT_hi", [P, KD, SEQ], F32R)
        hT_lo = buffers(dense_only)("hT_lo", [P, KD, SEQ], F32R)
        dense_only.close()
        xe = fb("xe", [P, KD, P])
        xe_hi = fb("xe_hi", [P, KD, P], F32R)
        xe_lo = fb("xe_lo", [P, KD, P], F32R)
        y_e = fb("y_e", [P, D])
        disp = fb("disp", [P, C, P])
        comb = fb("comb", [P, C, P])
        combT = fb("combT", [P, C * P])
        rt = fb("rt", [P, KD, NE])
        lg = fb("lg", [P, C, NE])
        cmp_ = fb("cmp", [P, 2, C, NE, NE])
        tie = fb("tie", [P, NE, NE])
        sel = fb("sel", [P, C, NE])
        gate = fb("gate", [P, C, NE])
        slot_of = fb("slot_of", [P, C, NE + 1])
        rstat = fb("rstat", [P, 8])
        most = fb("most", [P, 1], I32)
        ffn.close()

        def flat(t):
            names = "abcd"[:len(t.shape) - 1]
            return t[:].rearrange(f"p {' '.join(names)} -> p ({' '.join(names)})")

        def spread(a, axis, n):
            a = a.unsqueeze(axis)
            shape = list(a.shape)
            shape[axis] = n
            return a.to_broadcast(shape)

        def gmask(c, g):
            o = NG * P * c + g * (c + 1) * P
            return mask[:, o:o + (c + 1) * P]

        ADD_BANKS = (3, 6, 7, 2)

        sout = z[:, :, 0:SSM]
        soT = uT
        oatt = z[:, :, Q0:Q0 + SLOTS * HD]
        oT = hT
        omem = z[:, :, MQ0:MQ0 + XW]
        omT = gT
        sig = z[:, :, K0:K0 + SSM]
        merged = h
        b_raw = z[:, 1, GATE0:GATE0 + 2 * NJ * GCH].rearrange("p (r j c) -> p r j c", r=2, j=NJ)
        b_bar = z[:, 1, GATE0 + 512:GATE0 + 512 + 2 * NJ * 2 * GCH].rearrange(
            "p (r j c) -> p r j c", r=2, j=NJ)
        b_tmp = z[:, 0, GATE0 + 1024:GATE0 + 1024 + NJ * GCH].rearrange("p (j c) -> p j c", j=NJ)
        b_tmp2 = z[:, 0, GATE0 + 1280:GATE0 + 1280 + NJ * GCH].rearrange("p (j c) -> p j c", j=NJ)
        sp16 = z[0:NJ, 0, GATE0 + 1536:GATE0 + 1536 + 12 * P].rearrange("j (i s) -> j i s", i=12)
        c_raw = z[:, 0, GATE0:GATE0 + 2 * 4 * P].rearrange("p (r q s) -> p r q s", r=2, q=4)

        def blocks(w, k0, k1, n0, n1):
            return w[k0 * P:k1 * P, n0:n1].rearrange("(k p) n -> p k n", p=P)

        def mix_tiles(l):
            t = [blocks(w_mem_kv[l], KT * i, KT * i + KT, BANK * n, BANK * n + BANK)
                 for n in range(2) for i in range(2)]
            t += [blocks(w_in[l], KT * i, KT * i + KT, BANK * n, BANK * n + BANK)
                  for n in range(IN_FULL) for i in range(2)]
            t += [blocks(w_in[l], 0, KD, IN_FULL * BANK, COLS)]
            t += [blocks(w_glu[l], 0, KT, BANK * n, BANK * n + BANK) for n in range(2)]
            t += [blocks(w_ssm_out[l], 0, KT, BANK * n, BANK * n + BANK) for n in range(2)]
            t += [blocks(w_att_out[l], 0, 2, 0, D)]
            t += [blocks(w_mem_out[l], 0, KT, BANK * n, BANK * n + BANK) for n in range(2)]
            t += [blocks(w_o[l], KT * i, KT * i + KT, BANK * n, BANK * n + BANK)
                  for n in range(2) for i in range(2)]
            assert len(t) == MIX_TILES
            return t

        full = [sem(f"tile_arrived_{r}") for r in range(R)]
        COL_TILES = 2 + IN_FULL + 1 + 2 + 3 * 2 + 2

        def tile_uses():
            uses, col, mid = [], 0, 0
            for count, per_column in ((KV_TILES, 2), (2 * IN_FULL, 2), (1, 1), (2, 1), (2, 1), (1, 0.5), (2, 1), (4, 2)):
                for i in range(count):
                    if per_column == 2 and i % 2 == 0:
                        mid += 1
                        uses.append(("middle_tiles_used", mid))
                    else:
                        col += 2 if per_column == 0.5 else 1
                        uses.append(("columns_done", col))
            assert col == COL_TILES and len(uses) == MIX_TILES
            return uses, mid

        USES, MIDDLE = tile_uses()

        ATT_UNITS = C * SLOTS
        UNITS = ATT_UNITS + C * XH // 2
        VISIT_PARTS = (2, 1) * (NJ // 4)
        SSM_COLS = 2 + sum(VISIT_PARTS) // 2
        FILL = [(t, i) for t in range(SSM_COLS + 1, IN_FULL) for i in range(2)][1:] + [(IN_FULL, 0), ("glu", 0), ("glu", 1)]
        assert (SSM_COLS - 1) * BANK >= GATE0 and len(FILL) <= UNITS

        BATCHES = (("ssm", 1), ("b", 2), ("c", 2), ("h", KD // 2), ("u", KS // 2), ("qk", HEADS // 2), ("mem_qk", XH),
                   ("ssm_out", KS // 2), ("att_out", 1), ("mem_out", XH // 2), ("merged", KD // 2), ("ffn", KD // 2))

        def batches_to(l, name):
            n = KD // 2 + l * sum(b for _, b in BATCHES)
            for key, b in BATCHES:
                n += b
                if key == name:
                    return n
        full_e = [sem(f"expert_tile_arrived_{r}") for r in range(RM)]
        params = sem("params_loaded")
        lparams = [sem(f"layer_params_loaded{l}") for l in range(L)]
        N_SMALL = 7
        BASE = [0, MIX_TILES + FFN_TILES]

        ctx.enter_context(nc.allow_non_contiguous_dma(reason="gains and skips by channel: small"))
        block = ctx.enter_context(nc.Block())

        @block.sync
        def _(sp):
            def load(n, src, shift=0):
                if n >= R:
                    i = n - R if n < BASE[1] + R else n - R - BASE[1]
                    if MIX_TILES <= i and n < BASE[1] + R:
                        sp.wait_ge(sem("lo_ready"), i - MIX_TILES + 1 + R * shift)
                    else:
                        name, count = USES[i]
                        sp.wait_ge(sem(name), count + (0 if n < BASE[1] + R else {"columns_done": COL_TILES}.get(name, MIDDLE)))
                v = ring[:, n % R, :].rearrange("p (k n) -> p k n", n=src.shape[2])
                sp.dma_start(v, src).then_inc(full[n % R], 16)

            sp.dma_start(h[:], mem_in[0].rearrange("(c p) d -> p c d", p=P)).then_inc(sem("mem_loaded"), 16)
            sp.dma_start(x[:], x_in[0].rearrange("(c p) d -> p c d", p=P)).then_inc(sem("x_loaded"), 16)
            for i in range(R):
                load(i, mix_tiles(0)[i])
            for i, g in enumerate((norm_mix, norm_mem, norm_ffn)):
                for l in range(L):
                    sp.dma_start(gains[:, i, l, :], g[l].rearrange("(k p) -> p k", p=P)).then_inc(params, 16)
            for l in range(L):
                sp.dma_start(dsk[:, l, :], ssm_d[l].rearrange("(q p) -> p q", p=P)).then_inc(params, 16)
                sp.dma_start(gmq[:, l, 0:1], g_mq[l].rearrange("(p o) -> p o", o=1)).then_inc(params, 16)
                sp.dma_start(gmq[:, l, 1:2], g_mk[l].rearrange("(p o) -> p o", o=1)).then_inc(params, 16)
                sp.dma_start(gqk[:, l, 0, :], g_q[l:l + 1, :].to_broadcast([P, HD])).then_inc(params, 16)
                sp.dma_start(gqk[:, l, 1, :], g_k[l:l + 1, :].to_broadcast([P, HD])).then_inc(params, 16)
            sp.dma_start(pos_i[:], positions.rearrange("o (c p) -> p (o c)", p=P)).then_inc(sem("pos_loaded"), 16)
            for l in range(L):
                for i, src in enumerate(mix_tiles(l)):
                    if l > 0 or i >= R:
                        load(BASE[l] + i, src)
                if l == 0:
                    n0 = MIX_TILES

                    def gate_tile(w, f):
                        return w[0][:, bass.ds(f * 256, 256)].rearrange("(k p) n -> p k n", p=P)

                    def down_tile(f):
                        return ffn_down[0][bass.ds(f * 256, 256), :].rearrange("(k p) n -> p k n", p=P)
                    load(n0, gate_tile(ffn_gate, 0))
                    load(n0 + 1, gate_tile(ffn_up, 0))
                    load(n0 + 2, gate_tile(ffn_gate, 1))
                    load(n0 + 3, gate_tile(ffn_up, 1))
                    load(n0 + 4, down_tile(0))
                    with sp.Fori(2, NF) as f:
                        load(n0 + 5, gate_tile(ffn_gate, f), f - 2)
                        load(n0 + 6, gate_tile(ffn_up, f), f - 2)
                        load(n0 + 7, down_tile(f - 1), f - 2)
                    load(n0 + 3 * NF - 1, down_tile(NF - 1))

            sp.wait_ge(sem("slot_used"), L * (UNITS + 2))
            sp.wait_ge(sem("probsT_ready"), L * UNITS)

            def load_e(c, src, turn, first=False):
                if not first:
                    sp.wait_ge(sem("lo_ready"), FFN_TILES + RM * (turn - 1) + c % RM + 1)
                v = ring_e[:, c % RM, :].rearrange("p (k n) -> p k n", n=src.shape[2])
                sp.dma_start(v, src).then_inc(full_e[c % RM], 16)

            def moe_src(e, f, i):
                w = (moe_gate, moe_gate, moe_up, moe_up)[i]
                src = w[0].rearrange("e k n -> (e k) n")[
                    bass.ds(e * D + (i % 2) * KT * P, KT * P), bass.ds(f * BANK, BANK)]
                return src.rearrange("(k p) n -> p k n", p=P)

            def moe_down_src(e, f, i):
                src = moe_down[0].rearrange("e k n -> (e k) n")[
                    bass.ds(e * FE + f * BANK + i * 2 * P, 2 * P), :]
                return src.rearrange("(k p) n -> p k n", p=P)

            def expert_loads(e, turn0, first):
                for i in range(4):
                    load_e(i, moe_src(e, 0, i), turn0, first)
                for i in range(2):
                    load_e(4 + i, moe_src(e, 1, i), turn0, first)
                for i in range(2):
                    load_e(i, moe_src(e, 1, 2 + i), turn0 + 1)
                for i in range(2):
                    load_e(2 + i, moe_down_src(e, 0, i), turn0 + 1)
                with sp.Fori(2, NFE) as f:
                    for i in range(2):
                        load_e(4 + i, moe_src(e, f, i), turn0 + f - 1)
                    for i in range(2):
                        load_e(i, moe_src(e, f, 2 + i), turn0 + f)
                    for i in range(2):
                        load_e(2 + i, moe_down_src(e, f - 1, i), turn0 + f)
                for i in range(2):
                    load_e(4 + i, moe_down_src(e, NFE - 1, i), turn0 + NFE - 1)

            expert_loads(0, 0, True)
            with sp.Fori(1, NE) as e:
                expert_loads(e, NFE * e, False)
            sp.wait_ge(sem("routed"), 1)
            busiest = sp.value_load(most[0:1, 0:1])
            with sp.If(busiest > P):
                with sp.Fori(0, NE) as e:
                    expert_loads(e, NFE * NE + NFE * e, False)
            sp.wait_ge(sem("x_final"), 1)
            sp.dma_start(out[0].rearrange("(c p) d -> p c d", p=P), x[:]).then_inc(sem("stored"), 16)
            sp.wait_ge(sem("stored"), 16)

        @block.gpsimd
        def _(pool):
            built = sem("pool_chain")
            n = [0]

            def chain(ins):
                n[0] += 1
                ins.then_inc(built, 1)
                pool.wait_ge(built, n[0])

            nc.gpsimd.memset(half_neg[:], -0.5)
            nc.gpsimd.memset(half_pi[:], math.pi / 2)
            nc.gpsimd.memset(ones[:], 1.0)
            chain(nc.gpsimd.memset(ident[:], 0.0))
            nc.gpsimd.affine_select(out=ident[:], in_=ident[:], compare_op=ALU.not_equal, fill=1.0, base=0,
                                    pattern=[[-1, P]], channel_multiplier=1).then_inc(sem("ident_ready"), 1)
            nc.gpsimd.affine_select(out=before[:], in_=ones[:], compare_op=ALU.is_gt, fill=0.0, base=0,
                                    pattern=[[1, P]], channel_multiplier=-1)
            nc.gpsimd.iota(ramp_i[:], pattern=[[1, SEQ]], base=0, channel_multiplier=0)
            for i in range(HD // 2):
                nc.gpsimd.memset(invf[:, i:i + 1], float(np.float32(10000.0) ** np.float32(-i / (HD // 2))))
            for c in range(C):
                last = nc.gpsimd.iota(dist_i[:, c, :], pattern=[[-1, SEQ]], base=SEQ + c * P, channel_multiplier=1)
            last.then_inc(sem("consts_ready"), 1)
            for c in range(C):
                chain(nc.gpsimd.memset(gmask(c, 0), 0.0))
                chain(nc.gpsimd.affine_select(out=gmask(c, 0), in_=gmask(c, 0), compare_op=ALU.is_ge, fill=NEG,
                                              base=SPAN - c * P, pattern=[[1, (c + 1) * P]], channel_multiplier=-1))
            def rsqrt_mean(dst, src, count, of, done):
                pool.wait_ge(*of)
                chain(nc.gpsimd.tensor_scalar(src, src, 1.0 / count, EPS, ALU.mult, ALU.add))
                nc.gpsimd.tensor_tensor(dst, src, half_neg[:, 0:src.shape[1]], ALU.pow).then_inc(done, 1)

            rsqrt_mean(rs[:, 0:C], ss[:, 0:C], D, (sem("mem_squared"), 1), sem("mem_rs"))
            for l in range(L):
                rsqrt_mean(rs[:, 2:2 + C], ss[:, 2:2 + C], D, (sem("x_squared"), 2 * l + 1), sem("x_rs"))
                if l == 0:
                    pool.wait_ge(sem("grid_ready"), 1)
                    for c in range(C):
                        for g in range(NG):
                            last = nc.gpsimd.affine_select(out=gmask(c, g), in_=gmask(c, g), compare_op=ALU.is_ge, fill=NEG,
                                                           base=c * P, pattern=[[-1, (c + 1) * P]], channel_multiplier=1)
                    last.then_inc(sem("mask_ready"), 1)
                rsqrt_mean(flat(rqk2), flat(rqk), HD, (sem("qk_squared"), l + 1), sem("qk_rs"))
                rsqrt_mean(flat(rm2), flat(rm), XD, (sem("mqk_squared"), l + 1), sem("mqk_rs"))
                rsqrt_mean(rs[:, 2:2 + C], ss[:, 2:2 + C], D, (sem("x_squared"), 2 * l + 2), sem("x_rs"))

        @block.tensor
        def _(pe):
            tr = [0]
            used = [0]

            def batch(ins, wait=None):
                if wait:
                    pe.wait_ge(*wait)
                if tr[0] >= 4:
                    pe.wait_ge(sem("transposed_used"), tr[0] - 3)
                col = 0
                for a in ins:
                    o = ps[0:a.shape[1], 4 + tr[0] % 4, col:col + a.shape[0]]
                    last = nc.tensor.transpose(o, a, ident[0:a.shape[0], 0:a.shape[0]])
                    col += a.shape[0]
                tr[0] += 1
                last.then_inc(sem("transposed"), 1)

            def tile(n, width=BANK):
                pe.wait_ge(full[n % R], 16 * (n // R + 1))
                return ring[:, n % R, :].rearrange("p (k n) -> p k n", n=width)

            acc = [0]

            def part(n, i, tiles, lhs, k_tile, width=BANK):
                pair = 2 * (acc[0] % 2)
                if acc[0] >= 2 and i == 0:
                    pe.wait_ge(sem("columns_used"), acc[0] - 1)
                w = tile(n + i, width)
                for c in range(C):
                    for k in range(k_tile):
                        kk = i * k_tile + k
                        last = nc.tensor.matmul(ps[:, pair + c, 0:width], lhs[:, kk, c * P:(c + 1) * P],
                                                w[:, k, :], start=kk == 0, stop=kk == tiles * k_tile - 1)
                if i < tiles - 1:
                    last.then_inc(sem("middle_tiles_used"), 1)
                else:
                    acc[0] += 1
                    last.then_inc(sem("columns_done"), 1)

            def columns(n, tiles, lhs, k_tile, width=BANK):
                for i in range(tiles):
                    part(n, i, tiles, lhs, k_tile, width)

            def mixer(l):
                n = BASE[l]
                if l == 0:
                    pe.wait_ge(sem("ident_ready"), 1)
                    for k in range(0, KD, 2):
                        batch([h[:, c, (k + i) * P:(k + i + 1) * P] for i in range(2) for c in range(C)],
                              (sem("h_ready"), 1))
                pe.wait_ge(sem("memT_scaled"), l + 1)
                columns(n, 2, hT, KT)
                batch([sp16[:, i, :] for i in (6, 7, 10, 11, 2, 3)], (sem("ssm_params"), l + 1))
                columns(n + 2, 2, hT, KT)
                n += KV_TILES
                for r in range(2):
                    batch([b_bar[:, r, 4 * q:4 * q + 4, :].rearrange("p j c -> p (j c)") for q in range(4)],
                          (sem("b_bar_ready"), l + 1))
                for r in range(2):
                    batch([c_raw[:, r, q, :] for q in range(4)])
                for k in range(0, KD, 2):
                    batch([h[:, c, (k + i) * P:(k + i + 1) * P] for i in range(2) for c in range(C)],
                          (sem("h_ready"), 2 * l + 2))
                pe.wait_ge(sem("transposed_used"), batches_to(l, "h"))
                n_in = n
                columns(n, 2, hT, KT)
                columns(n + 2, 2, hT, KT)
                pe.wait_ge(sem("columns_used"), acc[0] - 1)
                for q in range(0, KS, 2):
                    batch([z[:, c, (q + i) * P:(q + i + 1) * P] for i in range(2) for c in range(C)])
                pe.wait_ge(sem("transposed_used"), tr[0])
                parts = [(t, i) for t in range(2, SSM_COLS) for i in range(2)]
                for v in range(NJ // 2):
                    if v > 0:
                        pe.wait_ge(sem("bu_used"), NJ // 2 * l + v)
                    for i in range(2):
                        j = 2 * v + i
                        o = 32 * (j % 4)
                        for r in range(2):
                            last = nc.tensor.matmul(ps[:, 4 + i, r * SEQ:(r + 1) * SEQ], bT[o:o + 32, j // 4, r, :],
                                                    uT[o:o + 32, j // 4, :], start=True, stop=True)
                    last.then_inc(sem("bu_done"), 1)
                    for _ in range(VISIT_PARTS[v]):
                        t, i = parts.pop(0)
                        part(n_in + 2 * t, i, 2, hT, KT)
                    pe.wait_ge(sem("states_ready"), NJ // 2 * l + v + 1)
                    if v >= 4 and v % 2 == 0:
                        pe.wait_ge(sem("y_used"), KS * l + v // 2 - 1)
                    for i in range(2):
                        j = 2 * v + i
                        o = 32 * (j % 4)
                        for r in range(2):
                            last = nc.tensor.matmul(ps[o:o + 32, 6, (j // 4 % 2) * SEQ:(j // 4 % 2 + 1) * SEQ],
                                                    cT[:, j, r, :], wv[:, i, r, :], start=r == 0, stop=r == 1,
                                                    skip_group_check=True)
                    last.then_inc(sem("y_done"), 1)
                columns(n_in + 2 * SSM_COLS, 2, hT, KT)
                part(n_in + 2 * (SSM_COLS + 1), 0, 2, hT, KT)
                for qk in range(2):
                    for i in range(0, HEADS // 2, 2):
                        o = Q0 + qk * AW + i * P
                        batch([z[:, c, o + d * P:o + (d + 1) * P] for d in range(2) for c in range(C)],
                              (sem("qk_ready"), l + 1))
                for src, o in ((z, MQ0), (kv, 0)):
                    for i in range(0, XH, 2):
                        batch([src[:, c, o + (i + d) * XD:o + (i + d + 1) * XD] for d in range(2) for c in range(C)],
                              (sem("mqk_ready"), l + 1))
                pe.wait_ge(sem("transposed_used"), tr[0])

                def scores(u):
                    if u >= ATT_UNITS:
                        c, hd = (u - ATT_UNITS) // 2, (u - ATT_UNITS) % 2 * 2
                        for i in range(2):
                            last = nc.tensor.matmul(ps[:, 4, i * MEM:(i + 1) * MEM], qmT[:, hd + i, c * P:(c + 1) * P],
                                                    kmT[:, hd + i, :], start=True, stop=True)
                        return last
                    c, s = u // SLOTS, u % SLOTS
                    nk = (c + 1) * P
                    for g in range(NG):
                        hd = g * SLOTS + s
                        o = HD * (hd % 2)
                        bank, col = 4 + g * nk // BANK, g * nk % BANK
                        last = nc.tensor.matmul(ps[:, bank, col:col + nk], qkT[o:o + HD, 0, hd // 2, c * P:(c + 1) * P],
                                                qkT[o:o + HD, 1, hd // 2, 0:nk], start=True, stop=True)
                    return last

                def blocks_of(u):
                    return 4 if u >= ATT_UNITS else NG * (u // SLOTS + 1)

                def transpose_probs(u):
                    for b in range(blocks_of(u)):
                        nc.tensor.transpose(ps[:, 6 + b // 4, b % 4 * P:(b % 4 + 1) * P],
                                            pr[:, u % 2, b * P:(b + 1) * P], ident[:])

                def weigh_values(u):
                    nb = blocks_of(u)
                    for b in range(nb):
                        if u >= ATT_UNITS:
                            hd, kc = (u - ATT_UNITS) % 2 * 2 + b // 2, b % 2
                            o, v = 2 * P + b // 2 * XD, kv[:, kc, XW + hd * XD:XW + (hd + 1) * XD]
                            first, end = kc == 0, kc == 1
                        else:
                            c, s = u // SLOTS, u % SLOTS
                            g, kc = b // (c + 1), b % (c + 1)
                            o, vo = 2 * P, V0 + (g * SLOTS + s) * HD
                            v = z[:, kc, vo:vo + HD]
                            first, end = b == 0, b == nb - 1
                        last = nc.tensor.matmul(ps[:, 5, o:o + v.shape[1]], pT[:, b * P:(b + 1) * P], v,
                                                start=first, stop=end, skip_group_check=True)
                    return last

                for s in range(UNITS + 2):
                    if s >= 1:
                        pe.wait_ge(sem("slot_used"), (UNITS + 2) * l + s)
                    if 1 <= s <= UNITS:
                        pe.wait_ge(sem("probs_ready"), UNITS * l + s)
                    if s >= 2:
                        pe.wait_ge(sem("probsT_ready"), UNITS * l + s - 1)
                    if 1 <= s <= UNITS:
                        transpose_probs(s - 1)
                    if s >= 2:
                        last = weigh_values(s - 2)
                    if s < UNITS:
                        last = scores(s)
                    last.then_inc(sem("slot_done"), 1)
                    if s < len(FILL):
                        t, i = FILL[s]
                        if t == "glu":
                            if i == 0:
                                pe.wait_ge(sem("gelu_ready"), l + 1)
                            part(n_in + 2 * IN_FULL + 1 + i, 0, 1, gT, KS)
                        elif t == IN_FULL:
                            part(n_in + 2 * t, 0, 1, hT, KD, 256)
                        else:
                            part(n_in + 2 * t, i, 2, hT, KT)
                n = n_in + 2 * IN_FULL + 3
                pe.wait_ge(sem("slot_used"), (UNITS + 2) * (l + 1))
                for q in range(0, KS, 2):
                    batch([sout[:, c, (q + i) * P:(q + i + 1) * P] for i in range(2) for c in range(C)],
                          (sem("columns_used"), acc[0]))
                batch([oatt[:, c, i * P:(i + 1) * P] for i in range(2) for c in range(C)])
                for q in range(0, XH, 2):
                    batch([omem[:, c, (q + i) * P:(q + i + 1) * P] for i in range(2) for c in range(C)])
                pe.wait_ge(sem("transposed_used"), tr[0])
                for lhs, tiles in ((soT, 2), (oT, 1), (omT, 2)):
                    if tiles == 2:
                        for t in range(2):
                            columns(n, 1, lhs, KS)
                            n += 1
                    else:
                        w = tile(n, D)
                        for half in range(2):
                            pair = 2 * (acc[0] % 2)
                            pe.wait_ge(sem("columns_used"), acc[0] - 1)
                            for c in range(C):
                                for k in range(2):
                                    last = nc.tensor.matmul(ps[:, pair + c, :], lhs[:, k, c * P:(c + 1) * P],
                                                            w[:, k, half * BANK:(half + 1) * BANK],
                                                            start=k == 0, stop=k == 1)
                            acc[0] += 1
                            last.then_inc(sem("columns_done"), 1)
                        n += 1
                for k in range(0, KD, 2):
                    batch([merged[:, c, (k + i) * P:(k + i + 1) * P] for i in range(2) for c in range(C)],
                          (sem("merged_ready"), l + 1))
                pe.wait_ge(sem("transposed_used"), tr[0])
                columns(n, 2, hT, KT)
                columns(n + 2, 2, hT, KT)
                for k in range(0, KD, 2):
                    batch([h[:, c, (k + i) * P:(k + i + 1) * P] for i in range(2) for c in range(C)],
                          (sem("h_ready"), 2 * l + 3))

            def split_product(o, x_hi, x_lo, w_hi, w_lo, first, end):
                nc.tensor.matmul(o, x_hi, w_hi, start=first, stop=False, skip_group_check=True)
                nc.tensor.matmul(o, x_hi, w_lo, start=False, stop=False, skip_group_check=True)
                return nc.tensor.matmul(o, x_lo, w_hi, start=False, stop=end, skip_group_check=True)

            def split_tile(m, width, shift=0):
                pe.wait_ge(sem("lo_ready"), m + 1 + shift)
                return (hi[:, m % H, :].rearrange("p (k n) -> p k n", n=width),
                        lo[:, m % H, :].rearrange("p (k n) -> p k n", n=width))

            def dense():
                def hidden(bank, m, shift):
                    w_hi, w_lo = split_tile(m, 256, shift)
                    for c in range(C):
                        for k in range(KD):
                            last = split_product(ps[:, bank, c * 256:(c + 1) * 256], hT_hi[:, k, c * P:(c + 1) * P],
                                                 hT_lo[:, k, c * P:(c + 1) * P], w_hi[:, k, :], w_lo[:, k, :],
                                                 k == 0, k == KD - 1)
                    last.then_inc(sem("split_used"), 1)

                def act_transposes(f):
                    pe.wait_ge(sem("act_ready"), f)
                    for j in range(2):
                        for c in range(C):
                            last = nc.tensor.transpose(ps[:, 2, j * SEQ + c * P:j * SEQ + (c + 1) * P],
                                                       act_out[:, c * 256 + j * P:c * 256 + (j + 1) * P], ident[:])
                    last.then_inc(sem("actT_done"), 1)

                def down(f, m, shift, first, end):
                    pe.wait_ge(sem("actT_ready"), f)
                    w_hi, w_lo = split_tile(m, D, shift)
                    for c in range(C):
                        for half in range(2):
                            for j in range(2):
                                t = slice(j * SEQ + c * P, j * SEQ + (c + 1) * P)
                                last = split_product(ps[:, 4 + 2 * c + half, :], aT_hi[:, t], aT_lo[:, t],
                                                     w_hi[:, j, half * BANK:(half + 1) * BANK],
                                                     w_lo[:, j, half * BANK:(half + 1) * BANK],
                                                     first and j == 0, end and j == 1)
                    last.then_inc(sem("split_used"), 1)

                def step(f, shift, first):
                    pe.wait_ge(sem("silu_done"), f)
                    hidden(0, 2, shift)
                    act_transposes(f)
                    hidden(1, 3, shift)
                    down(f, 4, shift, first, False)

                pe.wait_ge(sem("transposed_used"), batches_to(0, "ffn"))
                hidden(0, 0, 0)
                hidden(1, 1, 0)
                step(1, 0, True)
                with pe.Fori(2, NF) as f:
                    step(f, 3 * (f - 1), False)
                act_transposes(NF)
                down(NF, FFN_TILES - 1, 0, False, True)

            def experts():
                pe.wait_ge(sem("transposed_used"), batches_to(1, "ffn"))
                pe.wait_ge(sem("router_loaded"), 16)
                for c in range(C):
                    for k in range(KD):
                        last = nc.tensor.matmul(ps[:, 3, c * NE:(c + 1) * NE], hT[:, k, c * P:(c + 1) * P],
                                                rt[:, k, :], start=k == 0, stop=k == KD - 1)
                last.then_inc(sem("logits_done"), 1)
                pe.wait_ge(sem("selected"), 1)
                nc.tensor.matmul(ps[:, 3, 0:NE], before[:], sel[:, 0, :], start=True, stop=True)
                nc.tensor.matmul(ps[:, 3, NE:2 * NE], before[:], sel[:, 1, :], start=True, stop=False)
                nc.tensor.matmul(ps[:, 3, NE:2 * NE], ones[:], sel[:, 0, :], start=False, stop=True)
                nc.tensor.matmul(ps[:, 3, 2 * NE:3 * NE], ones[:], sel[:, 0, :], start=True, stop=False)
                nc.tensor.matmul(ps[:, 3, 2 * NE:3 * NE], ones[:], sel[:, 1, :], start=False,
                                 stop=True).then_inc(sem("places_done"), 1)

                def gather(count):
                    pe.wait_ge(sem("dispatch_ready"), count)
                    for k in range(KD):
                        for c in range(C):
                            last = nc.tensor.matmul(ps[:, 6 + k // 4, k % 4 * P:(k % 4 + 1) * P],
                                                    h[:, c, k * P:(k + 1) * P], disp[:, c, :],
                                                    start=c == 0, stop=c == 1, skip_group_check=True)
                    last.then_inc(sem("gathered"), 1)

                def hidden(bank, m, shift):
                    for i in range(2):
                        w_hi, w_lo = split_tile(m + i, BANK, shift)
                        for k in range(KT):
                            kk = i * KT + k
                            last = split_product(ps[:, bank, :], xe_hi[:, kk, :], xe_lo[:, kk, :], w_hi[:, k, :],
                                                 w_lo[:, k, :], kk == 0, kk == KD - 1)
                        if i == 0:
                            last.then_inc(sem("split_used"), 1)
                    last.then_inc(sem("split_used"), 1)

                def act_transposes(a):
                    pe.wait_ge(sem("act_ready"), a)
                    for j in range(4):
                        last = nc.tensor.transpose(ps[:, 2, j * P:(j + 1) * P], act_out[:, j * P:(j + 1) * P], ident[:])
                    last.then_inc(sem("actT_done"), 1)

                def down(a, m, shift, first, end):
                    pe.wait_ge(sem("actT_ready"), a)
                    for i in range(2):
                        w_hi, w_lo = split_tile(m + i, D, shift)
                        for half in range(2):
                            for j in range(2):
                                t = slice((2 * i + j) * P, (2 * i + j + 1) * P)
                                last = split_product(ps[:, 4 + half, :], aT_hi[:, t], aT_lo[:, t],
                                                     w_hi[:, j, half * BANK:(half + 1) * BANK],
                                                     w_lo[:, j, half * BANK:(half + 1) * BANK],
                                                     first and i == 0 and j == 0, end and i == 1 and j == 1)
                        if i == 0:
                            last.then_inc(sem("split_used"), 1)
                    last.then_inc(sem("split_used"), 1)

                def gate_first(e, gathers):
                    pe.wait_ge(sem("xe_ready"), gathers)
                    pe.wait_ge(sem("silu_done"), NF + NFE * e)
                    hidden(0, FFN_TILES, MOE_TILES * e)

                def expert(e, gathers, last_one):
                    a0 = NF + NFE * e
                    s0 = MOE_TILES * e
                    M = FFN_TILES
                    pe.wait_ge(sem("act_ready"), a0)
                    hidden(1, M + 2, s0)
                    pe.wait_ge(sem("added"), 4 * e + 1)

                    def step(f, shift, first):
                        pe.wait_ge(sem("silu_done"), a0 + f)
                        hidden(0, M + 4, shift)
                        act_transposes(a0 + f)
                        hidden(1, M + 6, shift)
                        down(a0 + f, M + 8, shift, first, False)

                    step(1, s0, True)
                    with pe.Fori(2, NFE) as f:
                        step(f, s0 + 6 * (f - 1), False)
                    act_transposes(a0 + NFE)
                    if not last_one:
                        gather(gathers + 1)
                    down(a0 + NFE, M + MOE_TILES - 2, s0, False, True)
                    pe.wait_ge(sem("combine_ready"), e + 1)
                    for c in range(C):
                        last = nc.tensor.transpose(ps[:, 3, c * P:(c + 1) * P], comb[:, c, :], ident[:])
                    last.then_inc(sem("combineT_done"), 1)
                    if not last_one:
                        gate_first(e + 1, gathers + 1)
                    pe.wait_ge(sem("combineT_ready"), e + 1)
                    pe.wait_ge(sem("y_ready"), e + 1)
                    pe.wait_ge(sem("actT_ready"), a0 + NFE)
                    for c in range(C):
                        for half in range(2):
                            nc.tensor.matmul(ps[:, ADD_BANKS[2 * c + half], :], combT[:, c * P:(c + 1) * P],
                                             y_e[:, half * BANK:(half + 1) * BANK], start=True,
                                             stop=True).then_inc(sem("combined"), 1)

                def one_pass(base, gathers):
                    gather(gathers + 1)
                    gate_first(base, gathers + 1)
                    with pe.Fori(0, NE - 1) as e:
                        expert(e + base, e + gathers + 1, False)
                    expert(base + NE - 1, gathers + NE, True)

                one_pass(0, 0)
                pe.wait_ge(sem("routed"), 1)
                busiest = pe.value_load(most[0:1, 0:1])
                with pe.If(busiest > P):
                    pe.wait_ge(sem("added"), 4 * NE + 1)
                    one_pass(NE, NE)

            mixer(0)
            dense()
            mixer(1)
            experts()

        @block.scalar
        def _(act):
            emptied = [0]
            cols = [0]

            def from_batch(moves):
                act.wait_ge(sem("transposed"), emptied[0] + 1)
                for dst, src, scale in moves(ps[:, 4 + emptied[0] % 4, :]):
                    last = nc.scalar.activation(dst, src, ACT.Copy, scale=scale)
                emptied[0] += 1
                last.then_inc(sem("transposed_used"), 1)

            def pairs(dst, q, gain=None):
                def moves(b):
                    if gain is None:
                        return [(dst[:, q:q + 2, :], b.rearrange("p (k t) -> p k t", k=2), 1.0)]
                    return [(dst[:, q + i, :], b[:, i * SEQ:(i + 1) * SEQ], gain(q + i)) for i in range(2)]
                return moves

            def take_columns(dst):
                act.wait_ge(sem("columns_done"), cols[0] + 1)
                pair = 2 * (cols[0] % 2)
                last = nc.scalar.activation(dst, ps[:, pair:pair + 2, 0:dst.shape[2]], ACT.Copy)
                cols[0] += 1
                last.then_inc(sem("columns_used"), 1)

            def sum_squares(slot, src, done):
                for c in range(C):
                    last = nc.scalar.activation(junk(c), src[:, c, :], ACT.Square,
                                                accum_out=ss[:, slot + c:slot + c + 1])
                last.then_inc(sem(done), 1)

            def junk(c):
                return hT[:, 4 * c:4 * c + 4, :].rearrange("p k t -> p (k t)")

            def load_layer(l):
                s = lparams[l]
                act.dma_start(sp16[:, 0, :], a_re[l].rearrange("(j g) p -> j (g p)", g=2)).then_inc(s, 16)
                act.dma_start(sp16[:, 1, :], a_im[l].rearrange("(j g) p -> j (g p)", g=2)).then_inc(s, 16)
                act.dma_start(dt16[:], log_dt[l].rearrange("(j g) -> j g", g=2)).then_inc(s, 16)
                for r, w in enumerate((b_re, b_im)):
                    act.dma_start(b_raw[:, r], w[l].rearrange("(j g) p c -> (g p) j c", g=2)).then_inc(s, 16)
                for r, w in enumerate((c_re, c_im)):
                    for half in range(2):
                        act.dma_start(c_raw[:, r, :, half * STATE:(half + 1) * STATE],
                                       w[l].rearrange("(q g) c p -> (g c) q p", q=4)).then_inc(s, 16)

            def mixer(l):
                if l > 0:
                    act.wait_ge(sem("x_ready"), l)
                load_layer(l)
                if l == 0:
                    act.wait_ge(sem("mem_loaded"), 16)
                    sum_squares(0, h, "mem_squared")
                    act.wait_ge(sem("x_loaded"), 16)
                    act.wait_ge(sem("mem_squared"), 1)
                sum_squares(2, x, "x_squared")
                if l == 0:
                    for q in range(0, KD, 2):
                        from_batch(pairs(memT, q))
                    act.wait_ge(sem("transposed_used"), emptied[0])
                    act.wait_ge(params, 16 * (3 * L + 5 * L))
                act.wait_ge(sem("x_squared"), 2 * l + 1)
                for k in range(KD):
                    last = nc.scalar.activation(hT[:, k, :], memT[:, k, :], ACT.Copy, scale=gains[:, 1, l, k:k + 1])
                last.then_inc(sem("memT_scaled"), 1)
                act.wait_ge(lparams[l], 16 * 9)
                nc.scalar.activation(dt16[:], dt16[:], ACT.Exp).then_inc(sem("dt_ready"), 1)
                act.wait_ge(sem("angle_ready"), l + 1)
                nc.scalar.activation(sp16[:, 6, :], sp16[:, 2, :], ACT.Exp)
                nc.scalar.activation(sp16[:, 5, :], sp16[:, 9, :], ACT.Sin, scale=-1.0, bias=half_pi[0:NJ, :])
                nc.scalar.activation(sp16[:, 8, :], sp16[:, 4, :], ACT.Sin).then_inc(sem("step_ready"), 1)
                if l == 0:
                    act.wait_ge(sem("rope_angle_ready"), 1)
                    nc.scalar.activation(rope[:, 1], ang[:], ACT.Sin)
                    nc.scalar.activation(rope[:, 0], turns[:], ACT.Sin, scale=-1.0,
                                         bias=half_pi[:]).then_inc(sem("rope_ready"), 1)
                take_columns(kv[:, :, 0:BANK])
                from_batch(lambda b: [(spT[:, 0:6, :], b[:, 0:6 * NJ].rearrange("p (i j) -> p i j", i=6), 1.0)])
                take_columns(kv[:, :, BANK:2 * BANK])
                for r in range(2):
                    from_batch(lambda b: [(bT[:, :, r, :], b.rearrange("p (q s) -> p q s", q=4), 1.0)])
                for r in range(2):
                    def moves(b):
                        v = b.rearrange("p (j g c) -> p j g c", g=2, c=GCH)
                        return [(cT[g * STATE:(g + 1) * STATE, :, r, g * GCH:(g + 1) * GCH],
                                 v[g * STATE:(g + 1) * STATE, :, g, :], 1.0 - 2.0 * r) for g in range(2)]
                    if r == 0:
                        act.wait_ge(sem("cT_zero"), l + 1)
                    from_batch(moves)
                for q in range(0, KD, 2):
                    from_batch(pairs(hT, q, lambda k: gains[:, 0, l, k:k + 1]))
                act.wait_ge(sem("phase_ready"), l + 1)
                nc.scalar.activation(flat(sintab), flat(sintab), ACT.Sin, scale=TWO_PI)
                nc.scalar.activation(flat(costab), flat(costab), ACT.Sin, scale=-TWO_PI,
                                     bias=half_pi[:]).then_inc(sem("rotation_ready"), 1)
                take_columns(z[:, :, 0:BANK])
                take_columns(z[:, :, BANK:2 * BANK])
                for q in range(0, KS, 2):
                    from_batch(pairs(uT, q))
                for n in range(2, SSM_COLS):
                    take_columns(z[:, :, n * BANK:(n + 1) * BANK])
                act.wait_ge(sem("y_used"), KS * (l + 1))
                nc.scalar.activation(flat(gT), flat(gT), ACT.Gelu_apprx_tanh).then_inc(sem("gelu_ready"), 1)
                take_columns(z[:, :, SSM_COLS * BANK:(SSM_COLS + 1) * BANK])
                for qk in range(2):
                    for i in range(0, HEADS // 2, 2):
                        from_batch(pairs(qkT[:, qk], i))
                for dst, g in ((qmT, 0), (kmT, 1)):
                    for i in range(0, XH, 2):
                        from_batch(pairs(dst, i, lambda k: gmq[:, l, g:g + 1]))
                for s in range(UNITS + 2):
                    if 1 <= s <= UNITS:
                        w = (4 if s > ATT_UNITS else NG * ((s - 1) // SLOTS + 1)) * P
                        act.wait_ge(sem("slot_done"), (UNITS + 2) * l + s + 1)
                        nc.scalar.activation(pT[:, 0:w], flat_banks(6, 2)[:, 0:w], ACT.Copy).then_inc(
                            sem("probsT_ready"), 1)
                    if s < ATT_UNITS:
                        w = NG * (s // SLOTS + 1) * P
                        act.wait_ge(sem("max_ready"), UNITS * l + s + 1)
                        nc.scalar.activation(pr[:, s % 2, 0:w], sc[:, s % 2, 0:w], ACT.Exp, scale=-1.0,
                                             bias=stat[:, s, 0:1], accum_out=stat[:, s, 1:2]).then_inc(
                                                 sem("probs_ready"), 1)
                    elif s < UNITS:
                        c, hd = (s - ATT_UNITS) // 2, (s - ATT_UNITS) % 2 * 2
                        act.wait_ge(sem("max_ready"), UNITS * l + s + 1)
                        for i in range(2):
                            last = nc.scalar.activation(
                                pr[:, s % 2, i * MEM:(i + 1) * MEM], ps[:, 4, i * MEM:(i + 1) * MEM], ACT.Exp,
                                scale=XD ** -0.5, bias=rm[:, 0, c, hd + i:hd + i + 1],
                                accum_out=rm[:, 1, c, hd + i:hd + i + 1])
                        last.then_inc(sem("probs_ready"), 1)
                    if s < len(FILL):
                        t, i = FILL[s]
                        if t == "glu" and i == 1:
                            act.wait_ge(sem("columns_done"), cols[0] + 2)
                            pair = 2 * ((cols[0] + 1) % 2)
                            nc.scalar.activation(sig, ps[:, pair:pair + 2, :], ACT.Sigmoid).then_inc(
                                sem("glu_gate_ready"), 1)
                        elif t == IN_FULL:
                            take_columns(z[:, :, IN_FULL * BANK:COLS])
                        elif t != "glu" and i == 1:
                            take_columns(z[:, :, t * BANK:(t + 1) * BANK])
                act.wait_ge(sem("columns_used"), cols[0])
                for c in range(C):
                    last = nc.scalar.activation(z[:, c, GATE0:COLS], z[:, c, GATE0:COLS], ACT.Sigmoid)
                last.then_inc(sem("gates_ready"), 1)
                cols[0] += 2
                for q in range(0, KS, 2):
                    from_batch(pairs(soT, q))
                from_batch(pairs(oT, 0))
                for q in range(0, XH, 2):
                    from_batch(pairs(omT, q))
                cols[0] += 6
                for q in range(0, KD, 2):
                    from_batch(pairs(hT, q))
                cols[0] += 2
                act.wait_ge(sem("columns_used"), COL_TILES * (l + 1))
                sum_squares(2, x, "x_squared")

            def flat_banks(b, n):
                return ps[:, b:b + n, :].rearrange("p b n -> p (b n)")

            def hi_part(src, src_full, m, shift, after=True):
                act.wait_ge(*src_full)
                if after:
                    act.wait_ge(sem("split_used"), m - H + 1 + shift)
                nc.scalar.activation(hi[:, m % H, :], src, ACT.Copy).then_inc(sem("hi_ready"), 1)

            def dense():
                for q in range(0, KD, 2):
                    def moves(b):
                        return [(hT_hi[:, q + i, :], b[:, i * SEQ:(i + 1) * SEQ], gains[:, 2, 0, q + i:q + i + 1])
                                for i in range(2)]
                    act.wait_ge(sem("transposed"), emptied[0] + 1)
                    for dst, src, scale in moves(ps[:, 4 + emptied[0] % 4, :]):
                        last = nc.scalar.activation(dst, src, ACT.Copy, scale=scale)
                    last.then_inc(sem("hT_hi_ready"), 1)
                    emptied[0] += 1

                def split(m, shift, after=True):
                    n = MIX_TILES + m
                    hi_part(ring[:, n % R, :], (full[n % R], 16 * (n // R + 1 + shift)), m, 3 * shift, after)

                def silu(f, gate_done):
                    act.wait_ge(sem("split_used"), gate_done)
                    nc.scalar.activation(gate_act[:], ps[:, 0, :], ACT.Silu).then_inc(sem("silu_done"), 1)

                def act_hi(f):
                    act.wait_ge(sem("actT_done"), f)
                    nc.scalar.activation(aT_hi[:], ps[:, 2, :], ACT.Copy).then_inc(sem("aT_hi_ready"), 1)

                def step(f, s, wait_act):
                    split(2, s)
                    split(3, s)
                    if wait_act:
                        act.wait_ge(sem("split_used"), 3 * f - 1)
                    act_hi(f)
                    split(4, s)
                    act.wait_ge(sem("act_ready"), f)
                    silu(f, 3 * f)

                split(0, 0, False)
                split(1, 0, False)
                silu(0, 1)
                split(2, 0, False)
                split(3, 0)
                act_hi(1)
                split(4, 0)
                act.wait_ge(sem("act_ready"), 1)
                silu(1, 3)
                with act.Fori(2, NF) as f:
                    step(f, f - 1, True)
                act.wait_ge(sem("split_used"), 3 * NF - 1)
                act_hi(NF)
                split(FFN_TILES - 1, 0)

            def experts():
                for q in range(0, KD, 2):
                    from_batch(pairs(hT, q, lambda k: gains[:, 2, 1, k:k + 1]))
                act.dma_start(rt[:], router[0].rearrange("(k p) e -> p k e", p=P)).then_inc(sem("router_loaded"), 16)
                act.wait_ge(sem("logits_ready"), 1)
                nc.scalar.activation(lg[:].rearrange("p c e -> p (c e)"), lg[:].rearrange("p c e -> p (c e)"),
                                     ACT.Exp).then_inc(sem("routes_exp"), 1)

                def split(c, M, s, turn):
                    hi_part(ring_e[:, c % RM, :], (full_e[c % RM], 16 * (turn + 1)), M, s)

                def gathered_high(count):
                    act.wait_ge(sem("xe_scaled"), count)
                    nc.scalar.activation(xe_hi[:], xe[:], ACT.Copy).then_inc(sem("xe_hi_ready"), 1)

                def expert(e, gathers, last_one):
                    a0 = NF + NFE * e
                    t0 = NFE * e
                    s0 = MOE_TILES * e
                    M = FFN_TILES

                    def silu(a, gate_done):
                        act.wait_ge(sem("split_used"), gate_done)
                        act.wait_ge(sem("act_ready"), a)
                        nc.scalar.activation(gate_act[:], ps[:, 0, :], ACT.Silu).then_inc(sem("silu_done"), 1)

                    def act_hi(a, down_done):
                        act.wait_ge(sem("actT_done"), a)
                        act.wait_ge(sem("split_used"), down_done)
                        nc.scalar.activation(aT_hi[:], ps[:, 2, :], ACT.Copy).then_inc(sem("aT_hi_ready"), 1)

                    for i in range(2, 4):
                        split(i, M + i, s0, t0)
                    silu(a0, M + s0 + 2)

                    def step(f, s, turn):
                        for i in range(4):
                            split(4 + i, M + 4 + i, s, turn + (4 + i) // RM)
                        act_hi(a0 + f, M + s + 4)
                        split(8, M + 8, s, turn + 1)
                        silu(a0 + f, M + s + 6)
                        split(9, M + 9, s, turn + 1)

                    step(1, s0, t0)
                    with act.Fori(2, NFE) as f:
                        step(f, s0 + 6 * (f - 1), t0 + f - 1)
                    act_hi(a0 + NFE, M + s0 + 6 * NFE - 2)
                    for i in range(2):
                        split(4 + i, M + MOE_TILES - 2 + i, s0, t0 + NFE - 1)
                    if not last_one:
                        gathered_high(gathers + 1)
                        split(0, M, s0 + MOE_TILES, t0 + NFE)
                    act.wait_ge(sem("split_used"), M + s0 + MOE_TILES)
                    nc.scalar.activation(y_e[:], flat_banks(4, 2), ACT.Copy).then_inc(sem("y_ready"), 1)
                    if not last_one:
                        split(1, M + 1, s0 + MOE_TILES, t0 + NFE)

                def one_pass(base, gathers):
                    gathered_high(gathers + 1)
                    for i in range(2):
                        split(i, FFN_TILES + i, MOE_TILES * base, NFE * base)
                    with act.Fori(0, NE - 1) as e:
                        expert(e + base, e + gathers + 1, False)
                    expert(base + NE - 1, gathers + NE, True)

                one_pass(0, 0)
                act.wait_ge(sem("routed"), 1)
                busiest = act.value_load(most[0:1, 0:1])
                with act.If(busiest > P):
                    one_pass(NE, NE)

            mixer(0)
            dense()
            mixer(1)
            experts()

        @block.vector
        def _(dve):
            done = sem("vector_chain")
            n = [0]
            V = nc.vector

            def chain(ins):
                n[0] += 1
                ins.then_inc(done, 1)
                dve.wait_ge(done, n[0])

            def reduce_angle(r, k, a):
                chain(V.tensor_scalar(k, a, 1 / TWO_PI, ROUND, ALU.mult, ALU.add))
                chain(V.tensor_scalar(k, k, ROUND, None, ALU.subtract))
                chain(V.scalar_tensor_tensor(out=r, in0=k, scalar=-PI_A, in1=a, op0=ALU.mult, op1=ALU.add))
                chain(V.scalar_tensor_tensor(out=r, in0=k, scalar=-PI_B, in1=r, op0=ALU.mult, op1=ALU.add))
                chain(V.scalar_tensor_tensor(out=r, in0=k, scalar=-PI_C, in1=r, op0=ALU.mult, op1=ALU.add))
                chain(V.tensor_scalar(r, r, 3.1415925, -3.1415925, ALU.min, ALU.max))
                return V.scalar_tensor_tensor(out=k, in0=r, scalar=-1.0, in1=r, op0=ALU.mult, op1=ALU.max)

            def scale_rows(dst, src, r0):
                for c in range(C):
                    last = V.tensor_scalar(dst[:, c, :], src[:, c, :], rs[:, r0 + c:r0 + c + 1], None, ALU.mult)
                return last

            def setup():
                dve.wait_ge(sem("mem_rs"), 1)
                scale_rows(h, h, 0).then_inc(sem("h_ready"), 1)

            def constants():
                dve.wait_ge(sem("consts_ready"), 1)
                V.tensor_copy(ramp[:], ramp_i[:])
                for c in range(C):
                    for i, g in enumerate((1, 2)):
                        chain(V.tensor_scalar(grid_i[:, i, :], dist_i[:, c, :], DIL[g] - 1, None, ALU.bitwise_and))
                        last = V.tensor_scalar(gmask(c, g), grid_i[:, i, 0:(c + 1) * P], 0, NEG, ALU.is_gt, ALU.mult)
                last.then_inc(sem("grid_ready"), 1)
                dve.wait_ge(sem("pos_loaded"), 16)
                chain(V.tensor_copy(pos[:], pos_i[:]))
                for c in range(C):
                    last = V.tensor_scalar(turns[:, c, :], invf[:], pos[:, c:c + 1], None, ALU.mult)
                chain(last)
                chain(V.tensor_copy(ang[:], turns[:]))
                reduce_angle(ang[:], turns[:], ang[:]).then_inc(sem("rope_angle_ready"), 1)

            def ssm_setup(l):
                s = sp16
                if l > 0:
                    dve.wait_ge(sem("x_ready"), l)
                dve.wait_ge(lparams[l], 16 * 9)
                dve.wait_ge(sem("dt_ready"), l + 1)
                dt = spread(dt16[:], 2, STATE)
                for i in range(2):
                    last = V.tensor_tensor(s[:, 2 + i, :].rearrange("j (g p) -> j g p", g=2),
                                           s[:, i, :].rearrange("j (g p) -> j g p", g=2), dt, ALU.mult)
                chain(last)
                reduce_angle(s[:, 4, :], s[:, 9, :], s[:, 3, :]).then_inc(sem("angle_ready"), 1)
                chain(V.tensor_scalar(s[:, 10, :], s[:, 4, :], 1 / TWO_PI, None, ALU.mult))
                chain(V.tensor_scalar(s[:, 11, :], s[:, 10, :], ROUND_FINE, None, ALU.add))
                chain(V.tensor_scalar(s[:, 11, :], s[:, 11, :], ROUND_FINE, None, ALU.subtract))
                dve.wait_ge(sem("step_ready"), l + 1)
                V.tensor_tensor(s[:, 8, :], s[:, 8, :], s[:, 6, :], ALU.mult)
                chain(V.tensor_tensor(s[:, 5, :], s[:, 5, :], s[:, 6, :], ALU.mult))
                chain(V.tensor_scalar(s[:, 5, :], s[:, 5, :], 1.0, None, ALU.subtract))
                V.tensor_tensor(s[:, 2, :], s[:, 5, :], s[:, 0, :], ALU.mult)
                V.tensor_tensor(s[:, 9, :], s[:, 8, :], s[:, 1, :], ALU.mult)
                V.tensor_tensor(s[:, 3, :], s[:, 8, :], s[:, 0, :], ALU.mult)
                chain(V.tensor_tensor(s[:, 7, :], s[:, 5, :], s[:, 1, :], ALU.mult))
                V.tensor_tensor(s[:, 2, :], s[:, 2, :], s[:, 9, :], ALU.add)
                chain(V.tensor_tensor(s[:, 3, :], s[:, 3, :], s[:, 7, :], ALU.subtract))
                V.tensor_tensor(s[:, 0, :], s[:, 0, :], s[:, 0, :], ALU.mult)
                chain(V.tensor_tensor(s[:, 1, :], s[:, 1, :], s[:, 1, :], ALU.mult))
                chain(V.tensor_tensor(s[:, 0, :], s[:, 0, :], s[:, 1, :], ALU.add))
                chain(V.reciprocal(s[:, 0, :], s[:, 0, :]))
                V.tensor_tensor(s[:, 2, :], s[:, 2, :], s[:, 0, :], ALU.mult)
                V.tensor_tensor(s[:, 3, :], s[:, 3, :], s[:, 0, :], ALU.mult).then_inc(sem("ssm_params"), 1)
                dve.wait_ge(sem("x_rs"), 2 * l + 1)
                if l == 0:
                    dve.wait_ge(sem("transposed"), 4)
                scale_rows(h, x, 2).then_inc(sem("h_ready"), 1)
                V.memset(b_bar, 0.0)
                V.memset(cT[:], 0.0).then_inc(sem("cT_zero"), 1)
                dve.wait_ge(sem("transposed_used"), batches_to(l, "ssm"))
                f_re, f_im = spread(spT[:, 4, :], 2, GCH), spread(spT[:, 5, :], 2, GCH)
                for r, (p, q, op) in enumerate(((f_re, f_im, ALU.subtract), (f_im, f_re, ALU.add))):
                    V.tensor_tensor(b_tmp, b_raw[:, 0], p, ALU.mult)
                    chain(V.tensor_tensor(b_tmp2, b_raw[:, 1], q, ALU.mult))
                    for g in range(2):
                        rows = slice(g * STATE, (g + 1) * STATE)
                        last = V.tensor_tensor(b_bar[rows, r, :, g * GCH:(g + 1) * GCH], b_tmp[rows], b_tmp2[rows], op)
                    chain(last)
                last = V.memset(stat[:, 0, 3:4], 0.0)
                last.then_inc(sem("b_bar_ready"), 1)
                if l == 0:
                    dve.wait_ge(sem("rope_ready"), 1)
                for j in range(NJ):
                    last = V.tensor_scalar(costab[:, j, :], ramp[:], spT[:, 2, j:j + 1], ROUND, ALU.mult, ALU.add)
                chain(last)
                chain(V.tensor_scalar(flat(costab), flat(costab), ROUND, None, ALU.subtract))
                for j in range(NJ):
                    last = V.scalar_tensor_tensor(out=sintab[:, j, :], in0=ramp[:], scalar=spT[:, 3, j:j + 1],
                                                  in1=costab[:, j, :], op0=ALU.mult, op1=ALU.subtract)
                V.tensor_tensor(spT[:, 6, :], spT[:, 2, :], spT[:, 3, :], ALU.subtract)
                chain(last)
                chain(V.memset(stat[:, 0, 3:4], 0.0))
                for j in range(NJ):
                    last = V.scalar_tensor_tensor(out=sintab[:, j, :], in0=ramp[:], scalar=spT[:, 6, j:j + 1],
                                                  in1=sintab[:, j, :], op0=ALU.mult, op1=ALU.add)
                chain(last)
                chain(V.tensor_scalar(flat(sintab), flat(sintab), 0.4999999, -0.4999999, ALU.min, ALU.max))
                V.scalar_tensor_tensor(out=flat(costab), in0=flat(sintab), scalar=-1.0, in1=flat(sintab),
                                       op0=ALU.mult, op1=ALU.max).then_inc(sem("phase_ready"), 1)

            def ssm(l):
                dve.wait_ge(sem("rotation_ready"), l + 1)
                for v in range(NJ // 2):
                    j = 2 * v
                    cos, sin = costab[:, j:j + 2, :], sintab[:, j:j + 2, :]
                    bu = ps[:, 4:6, :].rearrange("p j (r t) -> p j r t", r=2)
                    dve.wait_ge(sem("bu_done"), NJ // 2 * l + v + 1)
                    V.tensor_tensor(wa[:], bu, spread(cos, 2, 2), ALU.mult)
                    V.tensor_tensor(wb[:, :, 0, :], bu[:, :, 1, :], sin, ALU.mult)
                    last = V.tensor_tensor(wb[:, :, 1, :], bu[:, :, 0, :], sin, ALU.mult)
                    last.then_inc(sem("bu_used"), 1)
                    dve.wait_ge(sem("bu_used"), NJ // 2 * l + v + 1)
                    V.tensor_tensor(wv[:, :, 0, :], wa[:, :, 0, :], wb[:, :, 0, :], ALU.add)
                    chain(V.tensor_tensor(wv[:, :, 1, :], wa[:, :, 1, :], wb[:, :, 1, :], ALU.subtract))
                    for i in range(2):
                        for r in range(2):
                            last = V.tensor_tensor_scan(wp[:, i, r, :], spT[:, 0, j + i:j + i + 1].to_broadcast([P, SEQ]),
                                                        wv[:, i, r, :], 0.0, ALU.mult, ALU.add)
                    chain(last)
                    V.tensor_tensor(wa[:], wp[:], spread(cos, 2, 2), ALU.mult)
                    chain(V.tensor_tensor(wb[:], wp[:], spread(sin, 2, 2), ALU.mult))
                    V.tensor_tensor(wv[:, :, 0, :], wa[:, :, 0, :], wb[:, :, 1, :], ALU.subtract)
                    V.tensor_tensor(wv[:, :, 1, :], wa[:, :, 1, :], wb[:, :, 0, :], ALU.add).then_inc(
                        sem("states_ready"), 1)
                    if v % 2 == 1:
                        q = v // 2
                        dve.wait_ge(sem("y_done"), NJ // 2 * l + v + 1)
                        if q == 0:
                            dve.wait_ge(params, 16 * (3 * L + 5 * L))
                        last = V.scalar_tensor_tensor(out=gT[:, q, :], in0=uT[:, q, :], scalar=dsk[:, l, q:q + 1],
                                                      in1=ps[:, 6, q % 2 * SEQ:(q % 2 + 1) * SEQ], op0=ALU.mult,
                                                      op1=ALU.add)
                        last.then_inc(sem("y_used"), 1)

            def attention_inputs(l):
                if l == 0:
                    dve.wait_ge(sem("rope_ready"), 1)
                for qk in range(2):
                    for r in range(2):
                        for half in range(2):
                            g = gqk[:, l, qk, half * 32:(half + 1) * 32]
                            last = V.tensor_tensor(rgain[:, qk, r, :, half * 32:(half + 1) * 32], rope[:, r],
                                                   spread(g, 1, C), ALU.mult)
                chain(last)
                dve.wait_ge(sem("columns_used"), COL_TILES * l + 2 + SSM_COLS - 1)
                qk = z[:, :, Q0:Q0 + 2 * AW]
                by_head = qk.rearrange("p c (h d) -> p c h d", d=HD)
                chain(V.tensor_tensor(t1[:], qk, qk, ALU.mult))
                V.tensor_reduce(rqk[:], t1[:].rearrange("p c (h d) -> p c h d", d=HD), AX.X, ALU.add).then_inc(
                    sem("qk_squared"), 1)
                mq = z[:, :, MQ0:MQ0 + XW]
                mk = kv[:, :, 0:XW]
                chain(V.tensor_tensor(t2[:, :, 0:XW], mq, mq, ALU.mult))
                chain(V.tensor_tensor(t2[:, :, XW:2 * XW], mk, mk, ALU.mult))
                for i in range(2):
                    last = V.tensor_reduce(rm[:, i], t2[:, :, i * XW:(i + 1) * XW].rearrange(
                        "p c (h d) -> p c h d", d=XD), AX.X, ALU.add)
                last.then_inc(sem("mqk_squared"), 1)
                dve.wait_ge(sem("qk_squared"), l + 1)
                dve.wait_ge(sem("mqk_squared"), l + 1)
                for t, r in ((t1, 0), (t2, 1)):
                    for i in range(2):
                        for c in range(C):
                            w = slice(i * AW, (i + 1) * AW)
                            last = V.tensor_tensor(t[:, c, w].rearrange("p (h d) -> p h d", d=HD),
                                                   qk[:, c, w].rearrange("p (h d) -> p h d", d=HD),
                                                   spread(rgain[:, i, r, c, :], 1, HEADS), ALU.mult)
                chain(last)
                a = t1[:].rearrange("p c (h d) -> p c h d", d=HD)
                b = t2[:].rearrange("p c (h d) -> p c h d", d=HD)
                lo_, hi_ = slice(0, HD // 2), slice(HD // 2, HD)
                V.tensor_tensor(by_head[:, :, :, lo_], a[:, :, :, lo_], b[:, :, :, hi_], ALU.subtract)
                chain(V.tensor_tensor(by_head[:, :, :, hi_], b[:, :, :, lo_], a[:, :, :, hi_], ALU.add))
                dve.wait_ge(sem("qk_rs"), l + 1)
                V.tensor_tensor(by_head, by_head, spread(rqk2[:], 3, HD), ALU.mult).then_inc(sem("qk_ready"), 1)
                dve.wait_ge(sem("mqk_rs"), l + 1)
                for i, t in enumerate((mq, mk)):
                    v = t.rearrange("p c (h d) -> p c h d", d=XD)
                    last = V.tensor_tensor(v, v, spread(rm2[:, i], 3, XD), ALU.mult)
                last.then_inc(sem("mqk_ready"), 1)

            def attention(l):
                def take(u):
                    if u >= ATT_UNITS:
                        c, hd = (u - ATT_UNITS) // 2, (u - ATT_UNITS) % 2 * 2
                        chain(V.reciprocal(rm2[:, 1, c, hd:hd + 2], rm[:, 1, c, hd:hd + 2]))
                        return V.tensor_tensor(omem[:, c, hd * XD:(hd + 2) * XD].rearrange("p (h d) -> p h d", d=XD),
                                               ps[:, 5, 2 * P:BANK].rearrange("p (h d) -> p h d", d=XD),
                                               spread(rm2[:, 1, c, hd:hd + 2], 2, XD), ALU.mult)
                    c, s = u // SLOTS, u % SLOTS
                    chain(V.reciprocal(stat[:, u, 2:3], stat[:, u, 1:2]))
                    return V.tensor_scalar(oatt[:, c, s * HD:(s + 1) * HD], ps[:, 5, 2 * P:2 * P + HD],
                                           stat[:, u, 2:3], None, ALU.mult)

                if l == 0:
                    dve.wait_ge(sem("mask_ready"), 1)
                for s in range(UNITS + 2):
                    dve.wait_ge(sem("slot_done"), (UNITS + 2) * l + s + 1)
                    if s >= 2:
                        last = take(s - 2)
                    if s < ATT_UNITS:
                        c = s // SLOTS
                        w = NG * (c + 1) * P
                        if s >= 2:
                            dve.wait_ge(sem("probs_ready"), UNITS * l + s - 1)
                        last = V.scalar_tensor_tensor(
                            out=sc[:, s % 2, 0:w], in0=ps[:, 4:6, :].rearrange("p b n -> p (b n)")[:, 0:w],
                            scalar=-HD ** -0.5, in1=mask[:, c * NG * P:c * NG * P + w], op0=ALU.mult, op1=ALU.subtract)
                        last.then_inc(sem("slot_used"), 1)
                        dve.wait_ge(sem("slot_used"), (UNITS + 2) * l + s + 1)
                        V.tensor_reduce(stat[:, s, 0:1], sc[:, s % 2, 0:w], AX.X, ALU.min).then_inc(sem("max_ready"), 1)
                    elif s < UNITS:
                        c, hd = (s - ATT_UNITS) // 2, (s - ATT_UNITS) % 2 * 2
                        last = V.tensor_reduce(rm2[:, 0, c, hd:hd + 2], ps[:, 4, :].rearrange("p (h m) -> p h m", m=MEM),
                                               AX.X, ALU.max)
                        last.then_inc(sem("slot_used"), 1)
                        dve.wait_ge(sem("slot_used"), (UNITS + 2) * l + s + 1)
                        V.tensor_scalar(rm[:, 0, c, hd:hd + 2], rm2[:, 0, c, hd:hd + 2], -XD ** -0.5, None,
                                        ALU.mult).then_inc(sem("max_ready"), 1)
                    else:
                        last.then_inc(sem("slot_used"), 1)
                    if s == len(FILL):
                        glu(l)

            def glu(l):
                dve.wait_ge(sem("glu_gate_ready"), l + 1)
                pair = 2 * (cols[0] % 2)
                last = V.tensor_tensor(sout, ps[:, pair:pair + 2, :], sig, ALU.mult)
                last.then_inc(sem("columns_used"), 2)
                cols[0] += 2

            cols = [0]
            CT = 2 + IN_FULL + 1

            def merge(l):
                dve.wait_ge(sem("gates_ready"), l + 1)
                for b in range(3):
                    for half in range(2):
                        dve.wait_ge(sem("columns_done"), cols[0] + 1)
                        pair = 2 * (cols[0] % 2)
                        o = slice(half * BANK, (half + 1) * BANK)
                        g = z[:, :, GATE0 + b * D + half * BANK:GATE0 + b * D + (half + 1) * BANK]
                        if b == 0:
                            last = V.tensor_tensor(merged[:, :, o], ps[:, pair:pair + 2, :], g, ALU.mult)
                            last.then_inc(sem("columns_used"), 1)
                            dve.wait_ge(sem("columns_used"), cols[0] + 1)
                        else:
                            last = V.tensor_tensor(g, ps[:, pair:pair + 2, :], g, ALU.mult)
                            last.then_inc(sem("columns_used"), 1)
                            dve.wait_ge(sem("columns_used"), cols[0] + 1)
                            last = V.tensor_tensor(merged[:, :, o], merged[:, :, o], g, ALU.add)
                            if b == 2 and half == 1:
                                last.then_inc(sem("merged_ready"), 1)
                            else:
                                chain(last)
                        cols[0] += 1
                for half in range(2):
                    dve.wait_ge(sem("columns_done"), cols[0] + 1)
                    pair = 2 * (cols[0] % 2)
                    o = slice(half * BANK, (half + 1) * BANK)
                    last = V.tensor_tensor(x[:, :, o], ps[:, pair:pair + 2, :], x[:, :, o], ALU.add)
                    last.then_inc(sem("columns_used"), 1)
                    cols[0] += 1
                dve.wait_ge(sem("x_rs"), 2 * l + 2)
                scale_rows(h, x, 2).then_inc(sem("h_ready"), 1)

            def lo_part(src, m, shift):
                dve.wait_ge(sem("hi_ready"), m + 1 + shift)
                last = V.tensor_tensor(lo[:, m % H, :], src, hi[:, m % H, :].bitcast(F32), ALU.subtract)
                last.then_inc(sem("lo_ready"), 1)

            def act_low(a):
                dve.wait_ge(sem("aT_hi_ready"), a)
                V.tensor_tensor(aT_lo[:], ps[:, 2, :], aT_hi[:].bitcast(F32), ALU.subtract).then_inc(
                    sem("actT_ready"), 1)

            def act_product(a, up_done):
                dve.wait_ge(sem("split_used"), up_done)
                dve.wait_ge(sem("silu_done"), a)
                V.tensor_tensor(act_out[:], ps[:, 1, :], gate_act[:], ALU.mult).then_inc(sem("act_ready"), 1)

            def dense():
                for q in range(0, KD, 2):
                    dve.wait_ge(sem("hT_hi_ready"), q // 2 + 1)
                    for i in range(2):
                        b = ps[:, 4 + (batches_to(0, "merged") + q // 2) % 4, i * SEQ:(i + 1) * SEQ]
                        last = V.scalar_tensor_tensor(out=hT_lo[:, q + i, :], in0=b, scalar=gains[:, 2, 0, q + i:q + i + 1],
                                                      in1=hT_hi[:, q + i, :].bitcast(F32), op0=ALU.mult,
                                                      op1=ALU.subtract)
                    last.then_inc(sem("transposed_used"), 1)

                def split(m, shift):
                    n_ = MIX_TILES + m
                    lo_part(ring[:, n_ % R, :], m, 3 * shift)

                split(0, 0)
                split(1, 0)
                act_product(1, 2)

                def step(f, s):
                    split(2, s)
                    split(3, s)
                    act_low(f)
                    split(4, s)
                    act_product(f + 1, 3 * f + 1)
                with dve.Fori(1, NF) as f:
                    step(f, f - 1)
                act_low(NF)
                split(FFN_TILES - 1, 0)
                dve.wait_ge(sem("split_used"), FFN_TILES)
                for c in range(C):
                    last = V.tensor_tensor(x[:, c, :], ps[:, 4 + 2 * c:6 + 2 * c, :].rearrange("p b n -> p (b n)"),
                                           x[:, c, :], ALU.add)
                last.then_inc(sem("x_ready"), 1)
                dve.wait_ge(sem("x_ready"), 1)

            def route():
                for c in range(1):
                    V.memset(slot_of[:], -1.0)
                V.memset(tie[:], 0.0)
                chain(V.memset(rstat[:], 0.0))
                for e in range(1, NE):
                    last = V.memset(tie[:, e, 0:e], 1.0)
                dve.wait_ge(sem("logits_done"), 1)
                chain(V.tensor_copy(lg[:], ps[:, 3, 0:C * NE].rearrange("p (c e) -> p c e", c=C)))
                mine = spread(lg[:], 3, NE)
                other = spread(lg[:], 2, NE)
                for c in range(C):
                    V.tensor_tensor(cmp_[:, 0, c], other[:, c], mine[:, c], ALU.is_gt)
                    chain(V.tensor_tensor(cmp_[:, 1, c], other[:, c], mine[:, c], ALU.is_equal))
                    chain(V.tensor_tensor(cmp_[:, 1, c], cmp_[:, 1, c], tie[:], ALU.mult))
                    chain(V.tensor_tensor(cmp_[:, 0, c], cmp_[:, 0, c], cmp_[:, 1, c], ALU.add))
                chain(V.tensor_reduce(sel[:], cmp_[:, 0], AX.X, ALU.add))
                last = V.tensor_scalar(sel[:], sel[:], 2.0, None, ALU.is_lt)
                last.then_inc(sem("selected"), 1)
                dve.wait_ge(sem("selected"), 1)
                chain(V.tensor_reduce(rstat[:, 0:2], lg[:], AX.X, ALU.max))
                V.tensor_tensor(lg[:], lg[:], spread(rstat[:, 0:2], 2, NE), ALU.subtract).then_inc(
                    sem("logits_ready"), 1)
                dve.wait_ge(sem("routes_exp"), 1)
                chain(V.tensor_tensor(gate[:], lg[:], sel[:], ALU.mult))
                chain(V.tensor_reduce(rstat[:, 2:4], gate[:], AX.X, ALU.add))
                chain(V.reciprocal(rstat[:, 2:4], rstat[:, 2:4]))
                chain(V.tensor_tensor(gate[:], gate[:], spread(rstat[:, 2:4], 2, NE), ALU.mult))
                dve.wait_ge(sem("places_done"), 1)
                where = slot_of[:, :, 0:NE]
                chain(V.tensor_scalar(where, ps[:, 3, 0:C * NE].rearrange("p (c e) -> p c e", c=C), 1.0, None, ALU.add))
                chain(V.tensor_tensor(where, where, sel[:], ALU.mult))
                chain(V.tensor_scalar(where, where, 1.0, None, ALU.subtract))
                chain(V.tensor_reduce(rstat[:, 4:5], ps[:, 3, 2 * NE:3 * NE], AX.X, ALU.max))
                last = V.tensor_copy(most[:], rstat[:, 4:5])
                last.then_inc(sem("routed"), 1)
                V.memset(rstat[:, 5:6], 0.0).then_inc(sem("added"), 1)

            def experts():
                route()

                def dispatch(e):
                    for c in range(C):
                        last = V.tensor_scalar(disp[:, c, :], ramp[:, 0:P], slot_of[:, c, bass.ds(e, 1)], None,
                                               ALU.is_equal)
                    last.then_inc(sem("dispatch_ready"), 1)

                def scale_gathered(count):
                    dve.wait_ge(sem("gathered"), count)
                    V.tensor_tensor(xe[:], ps[:, 6:8, :].rearrange("p b (k t) -> p (b k) t", t=P),
                                    spread(gains[:, 2, 1, :], 2, P), ALU.mult).then_inc(sem("xe_scaled"), 1)

                def gathered_low(count):
                    dve.wait_ge(sem("xe_hi_ready"), count)
                    V.tensor_tensor(xe_lo[:], xe[:], xe_hi[:].bitcast(F32), ALU.subtract).then_inc(
                        sem("xe_ready"), 1)

                def split(c, M, s):
                    lo_part(ring_e[:, c % RM, :], M, s)

                def add_rows(e):
                    dve.wait_ge(sem("added"), 4 * e + 1)
                    for c in range(C):
                        for half in range(2):
                            i = 2 * c + half
                            o = slice(half * BANK, (half + 1) * BANK)
                            dve.wait_ge(sem("combined"), 4 * e + i + 1)
                            V.tensor_tensor(x[:, c, o], ps[:, ADD_BANKS[i], :], x[:, c, o], ALU.add).then_inc(
                                sem("added"), 1)

                def expert(e_here, e, gathers, first_one, last_one):
                    a0 = NF + NFE * e
                    s0 = MOE_TILES * e
                    M = FFN_TILES
                    for i in range(2, 4):
                        split(i, M + i, s0)
                    if not first_one:
                        add_rows(e - 1)
                    dve.wait_ge(sem("gathered"), gathers)
                    if not last_one:
                        dispatch(e_here + 1)
                    if not first_one:
                        dve.wait_ge(sem("combineT_done"), e)
                    for c in range(C):
                        last = V.tensor_scalar(comb[:, c, :], ramp[:, 0:P], slot_of[:, c, bass.ds(e_here, 1)],
                                               gate[:, c, bass.ds(e_here, 1)], ALU.is_equal, ALU.mult)
                    last.then_inc(sem("combine_ready"), 1)
                    act_product(a0 + 1, M + s0 + 4)

                    def step(f, s):
                        for i in range(4):
                            split(4 + i, M + 4 + i, s)
                        act_low(a0 + f)
                        for i in range(4, 6):
                            split(4 + i, M + 4 + i, s)
                        act_product(a0 + f + 1, M + s + 8)
                    with dve.Fori(1, NFE) as f:
                        step(f, s0 + 6 * (f - 1))
                    act_low(a0 + NFE)
                    split(4, M + MOE_TILES - 2, s0)
                    if not last_one:
                        scale_gathered(gathers + 1)
                    split(5, M + MOE_TILES - 1, s0)
                    if not last_one:
                        gathered_low(gathers + 1)
                        split(0, M, s0 + MOE_TILES)
                    dve.wait_ge(sem("combineT_done"), e + 1)
                    V.tensor_copy(combT[:], ps[:, 3, 0:C * P]).then_inc(sem("combineT_ready"), 1)
                    if not last_one:
                        split(1, M + 1, s0 + MOE_TILES)
                    else:
                        add_rows(e)

                def one_pass(base, gathers):
                    dispatch(0)
                    scale_gathered(gathers + 1)
                    gathered_low(gathers + 1)
                    for i in range(2):
                        split(i, FFN_TILES + i, MOE_TILES * base)
                    expert(0, base, gathers + 1, True, False)
                    with dve.Fori(1, NE - 1) as e:
                        expert(e, e + base, e + gathers + 1, False, False)
                    expert(NE - 1, base + NE - 1, gathers + NE, False, True)

                dve.wait_ge(sem("routed"), 1)
                one_pass(0, 0)
                busiest = dve.value_load(most[0:1, 0:1])
                with dve.If(busiest > P):
                    V.tensor_scalar(slot_of[:], slot_of[:], float(P), None, ALU.subtract).then_inc(sem("slots_moved"), 1)
                    dve.wait_ge(sem("slots_moved"), 1)
                    one_pass(NE, NE)
                V.memset(rstat[:, 0:1], 0.0).then_inc(sem("x_final"), 1)

            setup()
            constants()
            for l in range(L):
                ssm_setup(l)
                ssm(l)
                attention_inputs(l)
                cols[0] += CT
                attention(l)
                merge(l)
                if l == 0:
                    dense()
            experts()


_INS = ['x', 'mem', 'positions', 'norm_mix', 'w_in', 'ssm_a_re', 'ssm_a_im', 'ssm_log_dt', 'ssm_b_re', 'ssm_b_im',
        'ssm_c_re', 'ssm_c_im', 'ssm_d', 'ssm_w_glu', 'w_ssm_out', 'att_q_norm', 'att_k_norm', 'w_att_out',
        'norm_mem', 'w_mem_kv', 'mem_q_norm', 'mem_k_norm', 'w_mem_out', 'w_o', 'norm_ffn', 'ffn_w_gate',
        'ffn_w_up', 'ffn_w_down', 'moe_w_router', 'moe_w_gate', 'moe_w_up', 'moe_w_down']


def kernel(**inputs):
    import numpy as _np
    import concourse.bacc as _bacc
    from concourse import mybir as _mybir
    from concourse.bass_utils import run_bass_kernel_spmd as _run

    nc = _bacc.Bacc("TRN2", target_bir_lowering=False, num_devices=1)
    arrays, args = {}, []
    for name in _INS:
        a = _np.ascontiguousarray(inputs[name])
        arrays[f"in_{name}"] = a
        args.append(nc.dram_tensor(f"in_{name}", a.shape, _mybir.dt.from_np(a.dtype), kind="ExternalInput").ap())
    shape = inputs["x"].shape
    args.append(nc.dram_tensor("out", shape, _mybir.dt.float32, kind="ExternalOutput").ap())
    decoder_trunk(nc, *args)
    r = _run(nc, [arrays], core_ids=[0])
    return r.results[0]["out"]
```

```python
import math
from contextlib import ExitStack

import numpy as np
import concourse.bass as bass
from concourse import mybir

F32 = mybir.dt.float32
F32R = mybir.dt.float32r
I32 = mybir.dt.int32
ALU = mybir.AluOpType
ACT = mybir.ActivationFunctionType
AX = mybir.AxisListType

P = 128
BANK = 512
NEG = -1e30
EPS = 1e-6
TWO_PI = 2 * math.pi
ROUND = 1.5 * 2.0 ** 23
ROUND_FINE = ROUND * 2.0 ** -14
PI_A = 6.28125
PI_B = float(np.float32(np.round((TWO_PI - PI_A) * 2 ** 22) / 2 ** 22))
PI_C = float(np.float32(TWO_PI - PI_A - PI_B))


def decoder_trunk(nc, x_in, mem_in, positions, norm_mix, w_in, a_re, a_im, log_dt, b_re, b_im,
                  c_re, c_im, ssm_d, w_glu, w_ssm_out, g_q, g_k, w_att_out, norm_mem, w_mem_kv,
                  g_mq, g_mk, w_mem_out, w_o, norm_ffn, ffn_gate, ffn_up, ffn_down, router,
                  moe_gate, moe_up, moe_down, out):
    _, SEQ, D = x_in.shape
    MEM = mem_in.shape[1]
    L = norm_mix.shape[0]
    C = SEQ // P
    KD = D // P
    COLS = w_in.shape[2]
    GROUPS, STATE = a_re.shape[1:]
    GCH = b_re.shape[3]
    SSM = GROUPS * GCH
    KS = SSM // P
    NJ = GROUPS * STATE // P
    HD = g_q.shape[1]
    SLOTS = w_att_out.shape[1] // HD
    DIL = (1, 4, 16)
    SPAN = 128
    NG = len(DIL)
    HEADS = NG * SLOTS
    AW = HEADS * HD
    XD = g_mq.shape[1]
    XW = w_mem_kv.shape[2] // 2
    XH = XW // XD
    Q0, K0, V0, MQ0, GATE0 = SSM, SSM + AW, SSM + 2 * AW, SSM + 3 * AW, SSM + 3 * AW + XW
    FF = ffn_gate.shape[2]
    NE = router.shape[2]
    FE = moe_gate.shape[3]
    assert SEQ == MEM == 2 * P and 2 * STATE == P and L == 2 and HD == 64 and XD == P

    TILE = 2048
    KT = TILE // BANK
    R = 3
    RM = 6
    H = 3
    KV_TILES, IN_FULL = 4, COLS // BANK
    MIX_TILES = KV_TILES + 2 * IN_FULL + 1 + 2 + 2 + 1 + 2 + 4
    NF = FF // 256
    FFN_TILES = 3 * NF
    NFE = FE // BANK
    MOE_TILES = 6 * NFE
    assert COLS == IN_FULL * BANK + 256 and FF % 256 == 0 and FE % BANK == 0 and NF % 2 == 1
    assert FFN_TILES % H == 0 and MOE_TILES % RM == 0

    ctx = ExitStack()
    sems = {}

    def sem(name):
        if name not in sems:
            sems[name] = ctx.enter_context(nc.semaphore(name))
        return sems[name]

    def buffers(stack):
        return lambda name, shape, dt=F32: stack.enter_context(nc.sbuf_tensor(name, shape, dt))

    with ctx:
        sb = buffers(ctx)
        ps = ctx.enter_context(nc.psum_tensor("ps", [P, 8, BANK], F32))

        x = sb("x", [P, C, D])
        h = sb("h", [P, C, D])
        def renamed(name, shape, dt):
            with ExitStack() as place:
                return place.enter_context(nc.sbuf_tensor(name, shape, dt))

        xT_lo = renamed("xT_lo", [P, KD, SEQ], F32R)
        hT = sb("hT", [P, KD, SEQ])
        xT_hi = sb("xT_hi", [P, KD, SEQ], F32R)
        ring_lo = renamed("ring_lo", [P, R, TILE], F32R)
        ring = sb("ring", [P, R, TILE])
        ident = sb("ident", [P, P])
        ones = sb("ones", [P, P])
        before = sb("before", [P, P])
        ramp_i = sb("ramp_i", [P, SEQ], I32)
        ramp = sb("ramp", [P, SEQ])
        gains = sb("gains", [P, 3, L, KD])
        ss = sb("ss", [P, 4])
        rs = sb("rs", [P, 4])
        half_neg = sb("half_neg", [P, 64])
        half_pi = sb("half_pi", [P, 1])
        rt = sb("rt", [P, KD, NE])

        memT = sb("memT", [P, KD, MEM])
        mask = sb("mask", [P, NG * 3 * P])
        dsk = sb("dsk", [P, L, KS])
        gmq = sb("gmq", [P, L, 2])
        gqk = sb("gqk", [P, L, 2, HD])
        rope = sb("rope", [P, 2, C, HD // 2])

        mix = ExitStack()
        mb = buffers(mix)
        hi_m = mb("hi_m", [P, 2, TILE], F32R)
        z = mb("z", [P, C, COLS])
        kv = mb("kv", [P, C, 2 * XW])
        uT = mb("uT", [P, KS, SEQ])
        gT = mb("gT", [P, KS, SEQ])
        last_ring = ExitStack()
        ring_e = buffers(last_ring)("ring_e", [P, RM, TILE])
        last_ring.close()
        bT = mb("bT", [P, NJ // 4, 2, P])
        cT = mb("cT", [P, NJ, 2, 2 * GCH])
        pos_i = mb("pos_i", [P, C], I32)
        pos = mb("pos", [P, C])
        rgain = mb("rgain", [P, 2, 2, C, HD])
        spT = mb("spT", [P, 8, NJ])
        dt16 = mb("dt16", [NJ, 2])
        rqk = mb("rqk", [P, C, 2 * HEADS])
        rqk2 = mb("rqk2", [P, C, 2 * HEADS])
        rm = mb("rm", [P, 2, C, XH])
        rm2 = mb("rm2", [P, 2, C, XH])
        stat = mb("stat", [P, 8, 4])
        early = ExitStack()
        eb = buffers(early)
        costab = eb("costab", [P, NJ, SEQ])
        sintab = eb("sintab", [P, NJ, SEQ])
        early.close()
        first = ExitStack()
        sb1 = buffers(first)
        invf = sb1("invf", [P, HD // 2])
        dist_i = sb1("dist_i", [P, C, SEQ], I32)
        grid_i = sb1("grid_i", [P, 2, SEQ], I32)
        ang = sb1("ang", [P, C, HD // 2])
        turns = sb1("turns", [P, C, HD // 2])
        first.close()
        late = ExitStack()
        lb = buffers(late)
        squares = ExitStack()
        t1 = buffers(squares)("t1", [P, C, 2 * AW])
        t2 = buffers(squares)("t2", [P, C, 2 * AW])
        squares.close()
        qkT = lb("qkT", [P, 2, HEADS // 2, SEQ])
        sc = lb("sc", [P, 2, NG * 2 * P])
        pr = lb("pr", [P, 2, NG * 2 * P])
        pT = lb("pT", [P, NG * 2 * P])
        qmT = lb("qmT", [P, XH, SEQ])
        kmT = lb("kmT", [P, XH, MEM])
        late.close()
        mix.close()

        ffn = ExitStack()
        fb = buffers(ffn)
        hi = fb("hi", [P, H, TILE], F32R)
        lo = fb("lo", [P, H, TILE], F32R)
        aT_hi = fb("aT_hi", [P, BANK], F32R)
        aT_lo = fb("aT_lo", [P, BANK], F32R)
        gate_act = fb("gate_act", [P, BANK])
        act_out = fb("act_out", [P, BANK])
        dense_only = ExitStack()
        hT_hi = buffers(dense_only)("hT_hi", [P, KD, SEQ], F32R)
        hT_lo = buffers(dense_only)("hT_lo", [P, KD, SEQ], F32R)
        dense_only.close()
        xe = fb("xe", [P, KD, P])
        xe_hi = fb("xe_hi", [P, KD, P], F32R)
        xe_lo = fb("xe_lo", [P, KD, P], F32R)
        y_hi = fb("y_hi", [P, D], F32R)
        y_lo = fb("y_lo", [P, D], F32R)
        disp = fb("disp", [P, C, P])
        dispT = fb("dispT", [P, C * P], F32R)
        lg = fb("lg", [P, C, NE])
        cmp_ = fb("cmp", [P, 2, C, NE, NE])
        tie = fb("tie", [P, NE, NE])
        sel = fb("sel", [P, C, NE])
        gate = fb("gate", [P, C, NE])
        slot_of = fb("slot_of", [P, C, NE + 1])
        rstat = fb("rstat", [P, 8])
        most = fb("most", [P, 1], I32)
        ffn.close()

        def flat(t):
            names = "abcd"[:len(t.shape) - 1]
            return t[:].rearrange(f"p {' '.join(names)} -> p ({' '.join(names)})")

        def spread(a, axis, n):
            a = a.unsqueeze(axis)
            shape = list(a.shape)
            shape[axis] = n
            return a.to_broadcast(shape)

        def gmask(c, g):
            o = NG * P * c + g * (c + 1) * P
            return mask[:, o:o + (c + 1) * P]

        ADD_BANKS = (3, 6, 7, 2)

        sout = z[:, :, 0:SSM]
        soT = uT
        xT = "xT"
        oatt = z[:, :, Q0:Q0 + SLOTS * HD]
        oT = hT
        omem = z[:, :, MQ0:MQ0 + XW]
        omT = gT
        sig = z[:, :, K0:K0 + SSM]
        merged = h
        b_raw = z[:, 1, GATE0:GATE0 + 2 * NJ * GCH].rearrange("p (r j c) -> p r j c", r=2, j=NJ)
        b_bar = z[:, 1, GATE0 + 512:GATE0 + 512 + 2 * NJ * 2 * GCH].rearrange(
            "p (r j c) -> p r j c", r=2, j=NJ)
        b_tmp = z[:, 0, GATE0 + 1024:GATE0 + 1024 + NJ * GCH].rearrange("p (j c) -> p j c", j=NJ)
        b_tmp2 = z[:, 0, GATE0 + 1280:GATE0 + 1280 + NJ * GCH].rearrange("p (j c) -> p j c", j=NJ)
        sp16 = z[0:NJ, 0, GATE0 + 1536:GATE0 + 1536 + 12 * P].rearrange("j (i s) -> j i s", i=12)
        c_raw = z[:, 0, GATE0:GATE0 + 2 * 4 * P].rearrange("p (r q s) -> p r q s", r=2, q=4)

        def blocks(w, k0, k1, n0, n1):
            return w[k0 * P:k1 * P, n0:n1].rearrange("(k p) n -> p k n", p=P)

        def mix_tiles(l):
            t = [blocks(w_mem_kv[l], KT * i, KT * i + KT, BANK * n, BANK * n + BANK)
                 for n in range(2) for i in range(2)]
            t += [blocks(w_in[l], KT * i, KT * i + KT, BANK * n, BANK * n + BANK)
                  for n in range(IN_FULL) for i in range(2)]
            t += [blocks(w_in[l], 0, KD, IN_FULL * BANK, COLS)]
            t += [blocks(w_glu[l], 0, KT, BANK * n, BANK * n + BANK) for n in range(2)]
            t += [blocks(w_ssm_out[l], 0, KT, BANK * n, BANK * n + BANK) for n in range(2)]
            t += [blocks(w_att_out[l], 0, 2, 0, D)]
            t += [blocks(w_mem_out[l], 0, KT, BANK * n, BANK * n + BANK) for n in range(2)]
            t += [blocks(w_o[l], KT * i, KT * i + KT, BANK * n, BANK * n + BANK)
                  for n in range(2) for i in range(2)]
            assert len(t) == MIX_TILES
            return t

        full = [sem(f"tile_arrived_{r}") for r in range(R)]
        COL_TILES = 2 + IN_FULL + 1 + 2 + 1 + 3 * 2 + 2

        def tile_uses():
            uses, col, mid = [], 0, 0
            for count, per_column, others in ((KV_TILES, 2, 0), (2 * IN_FULL, 2, 0), (1, 1, 0), (2, 1, 0),
                                              (2, 1, 1), (1, 0.5, 0), (2, 1, 0), (4, 2, 0)):
                col += others
                for i in range(count):
                    if per_column == 2 and i % 2 == 0:
                        mid += 1
                        uses.append(("middle_tiles_used", mid))
                    else:
                        col += 2 if per_column == 0.5 else 1
                        uses.append(("columns_done", col))
            assert col == COL_TILES and len(uses) == MIX_TILES
            return uses, mid

        USES, MIDDLE = tile_uses()

        VISIT_PARTS = (2, 1) * (NJ // 4)
        SSM_COLS = 2 + sum(VISIT_PARTS) // 2
        SPLIT = [*range(KV_TILES), *range(KV_TILES + 2 * (SSM_COLS + 1) + 1, KV_TILES + 2 * IN_FULL + 1),
                 *range(MIX_TILES - 4, MIX_TILES)]

        def mixer_use(l, i):
            name, count = USES[i]
            return sem(name), count + l * {"columns_done": COL_TILES}.get(name, MIDDLE)

        ATT_UNITS = C * SLOTS
        UNITS = ATT_UNITS + C * XH // 2
        wa, wb, wv, wp = [z[:, i // 2, SSM_COLS * BANK + i % 2 * 4 * SEQ:SSM_COLS * BANK + (i % 2 + 1) * 4 * SEQ]
                          .rearrange("p (i r t) -> p i r t", i=2, r=2) for i in range(4)]
        SQUARES_AT = (3, 4, 6, 5)
        assert Q0 + AW <= 4 * BANK and Q0 + 2 * AW <= 5 * BANK and MQ0 + XW <= 7 * BANK
        FILL = [(t, i) for t in range(SSM_COLS + 1, IN_FULL) for i in range(2)][1:] + [(IN_FULL, 0), ("glu", 0), ("glu", 1)]
        AHEAD = len(FILL) - 2 - 2
        GLU_AT = len(FILL)
        FILL += [("none", 0), ("transposes", 0), ("branch", 0), ("branch", 1)]
        assert (SSM_COLS - 1) * BANK >= GATE0 and len(FILL) <= UNITS

        BATCHES = (("ssm", 1), ("h", KD // 2), ("b", 2), ("c", 2), ("u", KS // 2), ("qk", HEADS // 2), ("mem_qk", XH),
                   ("att_out", 1), ("mem_out", XH // 2), ("merged", KD // 2), ("ffn", KD // 2))

        def batches_to(l, name):
            n = KD // 2 + l * sum(b for _, b in BATCHES)
            for key, b in BATCHES:
                n += b
                if key == name:
                    return n
        full_e = [sem(f"expert_tile_arrived_{r}") for r in range(RM)]
        params = sem("params_loaded")
        lparams = [sem(f"layer_params_loaded{l}") for l in range(L)]
        N_SMALL = 7
        BASE = [0, MIX_TILES + FFN_TILES]

        ctx.enter_context(nc.allow_non_contiguous_dma(reason="gains and skips by channel: small"))
        block = ctx.enter_context(nc.Block())

        @block.sync
        def _(sp):
            def load(n, src, shift=0):
                if n >= R:
                    i = n - R if n < BASE[1] + R else n - R - BASE[1]
                    if MIX_TILES <= i and n < BASE[1] + R:
                        sp.wait_ge(sem("lo_ready"), i - MIX_TILES + 1 + R * shift)
                    else:
                        name, count = USES[i]
                        sp.wait_ge(sem(name), count + (0 if n < BASE[1] + R else {"columns_done": COL_TILES}.get(name, MIDDLE)))
                v = ring[:, n % R, :].rearrange("p (k n) -> p k n", n=src.shape[2])
                sp.dma_start(v, src).then_inc(full[n % R], 16)

            sp.dma_start(h[:], mem_in[0].rearrange("(c p) d -> p c d", p=P)).then_inc(sem("mem_loaded"), 16)
            sp.dma_start(gains[:, 1, 0, :], norm_mem[0].rearrange("(k p) -> p k", p=P)).then_inc(sem("mem_gain_loaded"), 16)
            sp.dma_start(x[:], x_in[0].rearrange("(c p) d -> p c d", p=P)).then_inc(sem("x_loaded"), 16)
            for i in range(R):
                load(i, mix_tiles(0)[i])
            for i, g in enumerate((norm_mix, norm_mem, norm_ffn)):
                for l in range(L):
                    if (i, l) != (1, 0):
                        sp.dma_start(gains[:, i, l, :], g[l].rearrange("(k p) -> p k", p=P)).then_inc(params, 16)
            for l in range(L):
                sp.dma_start(dsk[:, l, :], ssm_d[l].rearrange("(q p) -> p q", p=P)).then_inc(params, 16)
                sp.dma_start(gmq[:, l, 0:1], g_mq[l].rearrange("(p o) -> p o", o=1)).then_inc(params, 16)
                sp.dma_start(gmq[:, l, 1:2], g_mk[l].rearrange("(p o) -> p o", o=1)).then_inc(params, 16)
                sp.dma_start(gqk[:, l, 0, :], g_q[l:l + 1, :].to_broadcast([P, HD])).then_inc(params, 16)
                sp.dma_start(gqk[:, l, 1, :], g_k[l:l + 1, :].to_broadcast([P, HD])).then_inc(params, 16)
            sp.dma_start(pos_i[:], positions.rearrange("o (c p) -> p (o c)", p=P)).then_inc(sem("pos_loaded"), 16)
            for l in range(L):
                for i, src in enumerate(mix_tiles(l)):
                    if l > 0 or i >= R:
                        load(BASE[l] + i, src)
                if l == 0:
                    n0 = MIX_TILES

                    def gate_tile(w, f):
                        return w[0][:, bass.ds(f * 256, 256)].rearrange("(k p) n -> p k n", p=P)

                    def down_tile(f):
                        return ffn_down[0][bass.ds(f * 256, 256), :].rearrange("(k p) n -> p k n", p=P)
                    load(n0, gate_tile(ffn_gate, 0))
                    load(n0 + 1, gate_tile(ffn_up, 0))
                    load(n0 + 2, gate_tile(ffn_gate, 1))
                    load(n0 + 3, gate_tile(ffn_up, 1))
                    load(n0 + 4, down_tile(0))
                    with sp.Fori(2, NF) as f:
                        load(n0 + 5, gate_tile(ffn_gate, f), f - 2)
                        load(n0 + 6, gate_tile(ffn_up, f), f - 2)
                        load(n0 + 7, down_tile(f - 1), f - 2)
                    load(n0 + 3 * NF - 1, down_tile(NF - 1))

            sp.dma_start(rt[:], router[0].rearrange("(k p) e -> p k e", p=P)).then_inc(sem("router_loaded"), 16)
            sp.wait_ge(sem("slot_used"), L * (UNITS + 2))
            sp.wait_ge(sem("probsT_ready"), L * UNITS)

            def load_e(c, src, turn, first=False):
                if not first:
                    sp.wait_ge(sem("lo_ready"), FFN_TILES + RM * (turn - 1) + c % RM + 1)
                v = ring_e[:, c % RM, :].rearrange("p (k n) -> p k n", n=src.shape[2])
                sp.dma_start(v, src).then_inc(full_e[c % RM], 16)

            def moe_src(e, f, i):
                w = (moe_gate, moe_gate, moe_up, moe_up)[i]
                src = w[0].rearrange("e k n -> (e k) n")[
                    bass.ds(e * D + (i % 2) * KT * P, KT * P), bass.ds(f * BANK, BANK)]
                return src.rearrange("(k p) n -> p k n", p=P)

            def moe_down_src(e, f, i):
                src = moe_down[0].rearrange("e k n -> (e k) n")[
                    bass.ds(e * FE + f * BANK + i * 2 * P, 2 * P), :]
                return src.rearrange("(k p) n -> p k n", p=P)

            def expert_loads(e, turn0, first):
                for i in range(4):
                    load_e(i, moe_src(e, 0, i), turn0, first)
                for i in range(2):
                    load_e(4 + i, moe_src(e, 1, i), turn0, first)
                for i in range(2):
                    load_e(i, moe_src(e, 1, 2 + i), turn0 + 1)
                for i in range(2):
                    load_e(2 + i, moe_down_src(e, 0, i), turn0 + 1)
                with sp.Fori(2, NFE) as f:
                    for i in range(2):
                        load_e(4 + i, moe_src(e, f, i), turn0 + f - 1)
                    for i in range(2):
                        load_e(i, moe_src(e, f, 2 + i), turn0 + f)
                    for i in range(2):
                        load_e(2 + i, moe_down_src(e, f - 1, i), turn0 + f)
                for i in range(2):
                    load_e(4 + i, moe_down_src(e, NFE - 1, i), turn0 + NFE - 1)

            expert_loads(0, 0, True)
            with sp.Fori(1, NE) as e:
                expert_loads(e, NFE * e, False)
            sp.wait_ge(sem("routed"), 1)
            busiest = sp.value_load(most[0:1, 0:1])
            with sp.If(busiest > P):
                with sp.Fori(0, NE) as e:
                    expert_loads(e, NFE * NE + NFE * e, False)
            sp.wait_ge(sem("x_final"), 1)
            sp.dma_start(out[0].rearrange("(c p) d -> p c d", p=P), x[:]).then_inc(sem("stored"), 16)
            sp.wait_ge(sem("stored"), 16)

        @block.gpsimd
        def _(pool):
            built = sem("pool_chain")
            n = [0]

            def chain(ins):
                n[0] += 1
                ins.then_inc(built, 1)
                pool.wait_ge(built, n[0])

            nc.gpsimd.memset(half_neg[:], -0.5)
            nc.gpsimd.memset(half_pi[:], math.pi / 2)
            nc.gpsimd.memset(ones[:], 1.0)
            chain(nc.gpsimd.memset(ident[:], 0.0))
            nc.gpsimd.affine_select(out=ident[:], in_=ident[:], compare_op=ALU.not_equal, fill=1.0, base=0,
                                    pattern=[[-1, P]], channel_multiplier=1).then_inc(sem("ident_ready"), 1)
            nc.gpsimd.affine_select(out=before[:], in_=ones[:], compare_op=ALU.is_gt, fill=0.0, base=0,
                                    pattern=[[1, P]], channel_multiplier=-1)
            nc.gpsimd.iota(ramp_i[:], pattern=[[1, SEQ]], base=0, channel_multiplier=0)
            for i in range(HD // 2):
                nc.gpsimd.memset(invf[:, i:i + 1], float(np.float32(10000.0) ** np.float32(-i / (HD // 2))))
            for c in range(C):
                last = nc.gpsimd.iota(dist_i[:, c, :], pattern=[[-1, SEQ]], base=SEQ + c * P, channel_multiplier=1)
            last.then_inc(sem("consts_ready"), 1)
            for c in range(C):
                chain(nc.gpsimd.memset(gmask(c, 0), 0.0))
                chain(nc.gpsimd.affine_select(out=gmask(c, 0), in_=gmask(c, 0), compare_op=ALU.is_ge, fill=NEG,
                                              base=SPAN - c * P, pattern=[[1, (c + 1) * P]], channel_multiplier=-1))
            def rsqrt_mean(dst, src, count, of, done):
                pool.wait_ge(*of)
                chain(nc.gpsimd.tensor_scalar(src, src, 1.0 / count, EPS, ALU.mult, ALU.add))
                nc.gpsimd.tensor_tensor(dst, src, half_neg[:, 0:src.shape[1]], ALU.pow).then_inc(done, 1)

            rsqrt_mean(rs[:, 0:C], ss[:, 0:C], D, (sem("mem_squared"), 1), sem("mem_rs"))
            for l in range(L):
                rsqrt_mean(rs[:, 2:2 + C], ss[:, 2:2 + C], D, (sem("x_squared"), 2 * l + 1), sem("x_rs"))
                if l == 0:
                    pool.wait_ge(sem("grid_ready"), 1)
                    for c in range(C):
                        for g in range(NG):
                            last = nc.gpsimd.affine_select(out=gmask(c, g), in_=gmask(c, g), compare_op=ALU.is_ge, fill=NEG,
                                                           base=c * P, pattern=[[-1, (c + 1) * P]], channel_multiplier=1)
                    last.then_inc(sem("mask_ready"), 1)
                rsqrt_mean(flat(rqk2), flat(rqk), HD, (sem("qk_squared"), l + 1), sem("qk_rs"))
                rsqrt_mean(flat(rm2), flat(rm), XD, (sem("mqk_squared"), l + 1), sem("mqk_rs"))
                rsqrt_mean(rs[:, 2:2 + C], ss[:, 2:2 + C], D, (sem("x_squared"), 2 * l + 2), sem("x_rs"))

        @block.tensor
        def _(pe):
            tr = [0]
            used = [0]

            def batch(ins, wait=None):
                if wait:
                    pe.wait_ge(*wait)
                if tr[0] >= 4:
                    pe.wait_ge(sem("transposed_used"), tr[0] - 3)
                col = 0
                for a in ins:
                    o = ps[0:a.shape[1], 4 + tr[0] % 4, col:col + a.shape[0]]
                    last = nc.tensor.transpose(o, a, ident[0:a.shape[0], 0:a.shape[0]])
                    col += a.shape[0]
                tr[0] += 1
                last.then_inc(sem("transposed"), 1)

            def tile(n, width=BANK):
                pe.wait_ge(full[n % R], 16 * (n // R + 1))
                return ring[:, n % R, :].rearrange("p (k n) -> p k n", n=width)

            def split_product(o, x_hi, x_lo, w_hi, w_lo, first, end):
                nc.tensor.matmul(o, x_hi, w_hi, start=first, stop=False, skip_group_check=True)
                nc.tensor.matmul(o, x_hi, w_lo, start=False, stop=False, skip_group_check=True)
                return nc.tensor.matmul(o, x_lo, w_hi, start=False, stop=end, skip_group_check=True)

            acc = [0]
            split_tiles = [0]

            def part(n, i, tiles, lhs, k_tile, width=BANK):
                pair = 2 * (acc[0] % 2)
                if acc[0] >= 2 and i == 0:
                    pe.wait_ge(sem("columns_used"), acc[0] - 1)
                if lhs is xT:
                    m = split_tiles[0]
                    split_tiles[0] += 1
                    pe.wait_ge(sem("mixer_lo_ready"), m + 1)
                    w_hi = hi_m[:, m % 2, :].rearrange("p (k n) -> p k n", n=width)
                    w_lo = ring_lo[:, (n + i) % R, :].rearrange("p (k n) -> p k n", n=width)
                else:
                    w = tile(n + i, width)
                for c in range(C):
                    for k in range(k_tile):
                        kk = i * k_tile + k
                        o, t = ps[:, pair + c, 0:width], slice(c * P, (c + 1) * P)
                        first, end = kk == 0, kk == tiles * k_tile - 1
                        if lhs is xT:
                            last = split_product(o, xT_hi[:, kk, t], xT_lo[:, kk, t], w_hi[:, k, :], w_lo[:, k, :],
                                                 first, end)
                        else:
                            last = nc.tensor.matmul(o, lhs[:, kk, t], w[:, k, :], start=first, stop=end,
                                                    skip_group_check=True)
                if i < tiles - 1:
                    last.then_inc(sem("middle_tiles_used"), 1)
                else:
                    acc[0] += 1
                    last.then_inc(sem("columns_done"), 1)

            def columns(n, tiles, lhs, k_tile, width=BANK):
                for i in range(tiles):
                    part(n, i, tiles, lhs, k_tile, width)

            def mixer(l):
                n = BASE[l]
                if l == 0:
                    pe.wait_ge(sem("ident_ready"), 1)
                    for k in range(0, KD, 2):
                        batch([h[:, c, (k + i) * P:(k + i + 1) * P] for i in range(2) for c in range(C)],
                              (sem("h_ready"), 1))
                pe.wait_ge(sem("memT_scaled"), l + 1)
                columns(n, 2, xT, KT)
                columns(n + 2, 2, xT, KT)
                n += KV_TILES
                batch([sp16[:, i, :] for i in (6, 7, 10, 11, 2, 3)], (sem("ssm_params"), l + 1))
                for k in range(0, KD, 2):
                    batch([h[:, c, (k + i) * P:(k + i + 1) * P] for i in range(2) for c in range(C)],
                          (sem("h_ready"), 2 * l + 2))
                pe.wait_ge(sem("transposed_used"), batches_to(l, "h"))
                n_in = n
                columns(n, 2, hT, KT)
                for r in range(2):
                    batch([b_bar[:, r, 4 * q:4 * q + 4, :].rearrange("p j c -> p (j c)") for q in range(4)],
                          (sem("b_bar_ready"), l + 1))
                for r in range(2):
                    batch([c_raw[:, r, q, :] for q in range(4)])
                pe.wait_ge(sem("columns_used"), acc[0])
                for q in range(0, KS, 2):
                    batch([z[:, c, (q + i) * P:(q + i + 1) * P] for i in range(2) for c in range(C)])
                columns(n + 2, 2, hT, KT)
                pe.wait_ge(sem("transposed_used"), tr[0])
                parts = [(t, i) for t in range(2, SSM_COLS) for i in range(2)]
                for v in range(NJ // 2):
                    if v > 0:
                        pe.wait_ge(sem("bu_used"), NJ // 2 * l + v)
                    for i in range(2):
                        j = 2 * v + i
                        o = 32 * (j % 4)
                        for r in range(2):
                            last = nc.tensor.matmul(ps[:, 4 + i, r * SEQ:(r + 1) * SEQ], bT[o:o + 32, j // 4, r, :],
                                                    uT[o:o + 32, j // 4, :], start=True, stop=True)
                    last.then_inc(sem("bu_done"), 1)
                    for _ in range(VISIT_PARTS[v]):
                        t, i = parts.pop(0)
                        part(n_in + 2 * t, i, 2, hT, KT)
                    pe.wait_ge(sem("states_ready"), NJ // 2 * l + v + 1)
                    if v >= 4 and v % 2 == 0:
                        pe.wait_ge(sem("y_used"), KS * l + v // 2 - 1)
                    for i in range(2):
                        j = 2 * v + i
                        o = 32 * (j % 4)
                        for r in range(2):
                            last = nc.tensor.matmul(ps[o:o + 32, 6, (j // 4 % 2) * SEQ:(j // 4 % 2 + 1) * SEQ],
                                                    cT[:, j, r, :], wv[:, i, r, :], start=r == 0, stop=r == 1,
                                                    skip_group_check=True)
                    last.then_inc(sem("y_done"), 1)
                columns(n_in + 2 * SSM_COLS, 2, hT, KT)
                part(n_in + 2 * (SSM_COLS + 1), 0, 2, hT, KT)
                for qk in range(2):
                    for i in range(0, HEADS // 2, 2):
                        o = Q0 + qk * AW + i * P
                        batch([z[:, c, o + d * P:o + (d + 1) * P] for d in range(2) for c in range(C)],
                              (sem("qk_ready"), l + 1))
                for src, o in ((z, MQ0), (kv, 0)):
                    for i in range(0, XH, 2):
                        batch([src[:, c, o + (i + d) * XD:o + (i + d + 1) * XD] for d in range(2) for c in range(C)],
                              (sem("mqk_ready"), l + 1))
                pe.wait_ge(sem("transposed_used"), tr[0])

                def scores(u):
                    if u >= ATT_UNITS:
                        c, hd = (u - ATT_UNITS) // 2, (u - ATT_UNITS) % 2 * 2
                        for i in range(2):
                            last = nc.tensor.matmul(ps[:, 4, i * MEM:(i + 1) * MEM], qmT[:, hd + i, c * P:(c + 1) * P],
                                                    kmT[:, hd + i, :], start=True, stop=True)
                        return last
                    c, s = u // SLOTS, u % SLOTS
                    nk = (c + 1) * P
                    for g in range(NG):
                        hd = g * SLOTS + s
                        o = HD * (hd % 2)
                        bank, col = 4 + g * nk // BANK, g * nk % BANK
                        last = nc.tensor.matmul(ps[:, bank, col:col + nk], qkT[o:o + HD, 0, hd // 2, c * P:(c + 1) * P],
                                                qkT[o:o + HD, 1, hd // 2, 0:nk], start=True, stop=True)
                    return last

                def blocks_of(u):
                    return 4 if u >= ATT_UNITS else NG * (u // SLOTS + 1)

                def transpose_probs(u):
                    for b in range(blocks_of(u)):
                        nc.tensor.transpose(ps[:, 6 + b // 4, b % 4 * P:(b % 4 + 1) * P],
                                            pr[:, u % 2, b * P:(b + 1) * P], ident[:])

                def weigh_values(u):
                    nb = blocks_of(u)
                    for b in range(nb):
                        if u >= ATT_UNITS:
                            hd, kc = (u - ATT_UNITS) % 2 * 2 + b // 2, b % 2
                            o, v = 2 * P + b // 2 * XD, kv[:, kc, XW + hd * XD:XW + (hd + 1) * XD]
                            first, end = kc == 0, kc == 1
                        else:
                            c, s = u // SLOTS, u % SLOTS
                            g, kc = b // (c + 1), b % (c + 1)
                            o, vo = 2 * P, V0 + (g * SLOTS + s) * HD
                            v = z[:, kc, vo:vo + HD]
                            first, end = b == 0, b == nb - 1
                        last = nc.tensor.matmul(ps[:, 5, o:o + v.shape[1]], pT[:, b * P:(b + 1) * P], v,
                                                start=first, stop=end, skip_group_check=True)
                    return last

                for s in range(UNITS + 2):
                    if s >= 1:
                        pe.wait_ge(sem("slot_used"), (UNITS + 2) * l + s)
                    if 1 <= s <= UNITS:
                        pe.wait_ge(sem("probs_ready"), UNITS * l + s)
                    if s >= 2:
                        pe.wait_ge(sem("probsT_ready"), UNITS * l + s - 1)
                    if 1 <= s <= UNITS:
                        transpose_probs(s - 1)
                    if s >= 2:
                        last = weigh_values(s - 2)
                    if s < UNITS:
                        last = scores(s)
                    last.then_inc(sem("slot_done"), 1)
                    if s < len(FILL):
                        t, i = FILL[s]
                        if t == "glu":
                            if i == 0:
                                pe.wait_ge(sem("gelu_ready"), l + 1)
                            part(n_in + 2 * IN_FULL + 1 + i, 0, 1, gT, KS)
                        elif t == "transposes":
                            pe.wait_ge(sem("columns_used"), acc[0])
                            pair = 2 * (acc[0] % 2)
                            for q in range(KS):
                                for c in range(C):
                                    col = (q % 2 * C + c) * P
                                    last = nc.tensor.transpose(ps[:, pair + q // 2, col:col + P],
                                                               sout[:, c, q * P:(q + 1) * P], ident[:])
                            acc[0] += 1
                            last.then_inc(sem("columns_done"), 1)
                        elif t == "branch":
                            if i == 0:
                                pe.wait_ge(sem("columns_used"), acc[0])
                            part(n_in + 2 * IN_FULL + 3 + i, 0, 1, soT, KS)
                        elif t == "none":
                            pass
                        elif t == IN_FULL:
                            part(n_in + 2 * t, 0, 1, xT, KD, 256)
                        else:
                            part(n_in + 2 * t, i, 2, xT, KT)
                n = n_in + 2 * IN_FULL + 5
                pe.wait_ge(sem("slot_used"), (UNITS + 2) * (l + 1))
                batch([oatt[:, c, i * P:(i + 1) * P] for i in range(2) for c in range(C)])
                for q in range(0, XH, 2):
                    batch([omem[:, c, (q + i) * P:(q + i + 1) * P] for i in range(2) for c in range(C)])
                pe.wait_ge(sem("transposed_used"), tr[0])
                for lhs, tiles in ((oT, 1), (omT, 2)):
                    if tiles == 2:
                        for t in range(2):
                            columns(n, 1, lhs, KS)
                            n += 1
                    else:
                        w = tile(n, D)
                        for half in range(2):
                            pair = 2 * (acc[0] % 2)
                            pe.wait_ge(sem("columns_used"), acc[0] - 1)
                            for c in range(C):
                                for k in range(2):
                                    last = nc.tensor.matmul(ps[:, pair + c, :], lhs[:, k, c * P:(c + 1) * P],
                                                            w[:, k, half * BANK:(half + 1) * BANK],
                                                            start=k == 0, stop=k == 1)
                            acc[0] += 1
                            last.then_inc(sem("columns_done"), 1)
                        n += 1
                for k in range(0, KD, 2):
                    batch([merged[:, c, (k + i) * P:(k + i + 1) * P] for i in range(2) for c in range(C)],
                          (sem("merged_ready"), l + 1))
                pe.wait_ge(sem("transposed_used"), tr[0])
                columns(n, 2, xT, KT)
                columns(n + 2, 2, xT, KT)
                for k in range(0, KD, 2):
                    batch([h[:, c, (k + i) * P:(k + i + 1) * P] for i in range(2) for c in range(C)],
                          (sem("h_ready"), 2 * l + 3))

            def split_tile(m, width, shift=0):
                pe.wait_ge(sem("lo_ready"), m + 1 + shift)
                return (hi[:, m % H, :].rearrange("p (k n) -> p k n", n=width),
                        lo[:, m % H, :].rearrange("p (k n) -> p k n", n=width))

            def dense():
                def hidden(bank, m, shift):
                    w_hi, w_lo = split_tile(m, 256, shift)
                    for c in range(C):
                        for k in range(KD):
                            last = split_product(ps[:, bank, c * 256:(c + 1) * 256], hT_hi[:, k, c * P:(c + 1) * P],
                                                 hT_lo[:, k, c * P:(c + 1) * P], w_hi[:, k, :], w_lo[:, k, :],
                                                 k == 0, k == KD - 1)
                    last.then_inc(sem("split_used"), 1)

                def act_transposes(f):
                    pe.wait_ge(sem("act_ready"), f)
                    for j in range(2):
                        for c in range(C):
                            last = nc.tensor.transpose(ps[:, 2, j * SEQ + c * P:j * SEQ + (c + 1) * P],
                                                       act_out[:, c * 256 + j * P:c * 256 + (j + 1) * P], ident[:])
                    last.then_inc(sem("actT_done"), 1)

                def down(f, m, shift, first, end):
                    pe.wait_ge(sem("actT_ready"), f)
                    w_hi, w_lo = split_tile(m, D, shift)
                    for c in range(C):
                        for half in range(2):
                            for j in range(2):
                                t = slice(j * SEQ + c * P, j * SEQ + (c + 1) * P)
                                last = split_product(ps[:, 4 + 2 * c + half, :], aT_hi[:, t], aT_lo[:, t],
                                                     w_hi[:, j, half * BANK:(half + 1) * BANK],
                                                     w_lo[:, j, half * BANK:(half + 1) * BANK],
                                                     first and j == 0, end and j == 1)
                    last.then_inc(sem("split_used"), 1)

                def step(f, shift, first):
                    pe.wait_ge(sem("silu_done"), f)
                    hidden(0, 2, shift)
                    act_transposes(f)
                    hidden(1, 3, shift)
                    down(f, 4, shift, first, False)

                pe.wait_ge(sem("transposed_used"), batches_to(0, "ffn"))
                hidden(0, 0, 0)
                hidden(1, 1, 0)
                step(1, 0, True)
                with pe.Fori(2, NF) as f:
                    step(f, 3 * (f - 1), False)
                act_transposes(NF)
                down(NF, FFN_TILES - 1, 0, False, True)

            def experts():
                pe.wait_ge(sem("transposed_used"), batches_to(1, "ffn"))
                pe.wait_ge(sem("router_loaded"), 16)
                for c in range(C):
                    for k in range(KD):
                        last = nc.tensor.matmul(ps[:, 3, c * NE:(c + 1) * NE], hT[:, k, c * P:(c + 1) * P],
                                                rt[:, k, :], start=k == 0, stop=k == KD - 1)
                last.then_inc(sem("logits_done"), 1)
                pe.wait_ge(sem("selected"), 1)
                nc.tensor.matmul(ps[:, 3, 0:NE], before[:], sel[:, 0, :], start=True, stop=True)
                nc.tensor.matmul(ps[:, 3, NE:2 * NE], before[:], sel[:, 1, :], start=True, stop=False)
                nc.tensor.matmul(ps[:, 3, NE:2 * NE], ones[:], sel[:, 0, :], start=False, stop=True)
                nc.tensor.matmul(ps[:, 3, 2 * NE:3 * NE], ones[:], sel[:, 0, :], start=True, stop=False)
                nc.tensor.matmul(ps[:, 3, 2 * NE:3 * NE], ones[:], sel[:, 1, :], start=False,
                                 stop=True).then_inc(sem("places_done"), 1)

                def gather(count):
                    pe.wait_ge(sem("dispatch_ready"), count)
                    for k in range(KD):
                        for c in range(C):
                            last = nc.tensor.matmul(ps[:, 6 + k // 4, k % 4 * P:(k % 4 + 1) * P],
                                                    h[:, c, k * P:(k + 1) * P], disp[:, c, :],
                                                    start=c == 0, stop=c == 1, skip_group_check=True)
                    last.then_inc(sem("gathered"), 1)

                def hidden(bank, m, shift):
                    for i in range(2):
                        w_hi, w_lo = split_tile(m + i, BANK, shift)
                        for k in range(KT):
                            kk = i * KT + k
                            last = split_product(ps[:, bank, :], xe_hi[:, kk, :], xe_lo[:, kk, :], w_hi[:, k, :],
                                                 w_lo[:, k, :], kk == 0, kk == KD - 1)
                        if i == 0:
                            last.then_inc(sem("split_used"), 1)
                    last.then_inc(sem("split_used"), 1)

                def act_transposes(a):
                    pe.wait_ge(sem("act_ready"), a)
                    for j in range(4):
                        last = nc.tensor.transpose(ps[:, 2, j * P:(j + 1) * P], act_out[:, j * P:(j + 1) * P], ident[:])
                    last.then_inc(sem("actT_done"), 1)

                def down(a, m, shift, first, end):
                    pe.wait_ge(sem("actT_ready"), a)
                    for i in range(2):
                        w_hi, w_lo = split_tile(m + i, D, shift)
                        for half in range(2):
                            for j in range(2):
                                t = slice((2 * i + j) * P, (2 * i + j + 1) * P)
                                last = split_product(ps[:, 4 + half, :], aT_hi[:, t], aT_lo[:, t],
                                                     w_hi[:, j, half * BANK:(half + 1) * BANK],
                                                     w_lo[:, j, half * BANK:(half + 1) * BANK],
                                                     first and i == 0 and j == 0, end and i == 1 and j == 1)
                        if i == 0:
                            last.then_inc(sem("split_used"), 1)
                    last.then_inc(sem("split_used"), 1)

                def gate_first(e, gathers):
                    pe.wait_ge(sem("xe_ready"), gathers)
                    pe.wait_ge(sem("silu_done"), NF + NFE * e)
                    hidden(0, FFN_TILES, MOE_TILES * e)

                def expert(e, gathers, last_one):
                    a0 = NF + NFE * e
                    s0 = MOE_TILES * e
                    M = FFN_TILES
                    pe.wait_ge(sem("act_ready"), a0)
                    hidden(1, M + 2, s0)
                    pe.wait_ge(sem("added"), 4 * e + 1)
                    for c in range(C):
                        last = nc.tensor.transpose(ps[:, 3, c * P:(c + 1) * P], disp[:, c, :], ident[:])
                    last.then_inc(sem("dispatchT_done"), 1)

                    def step(f, shift, first):
                        pe.wait_ge(sem("silu_done"), a0 + f)
                        hidden(0, M + 4, shift)
                        act_transposes(a0 + f)
                        if first and not last_one:
                            gather(gathers + 1)
                        hidden(1, M + 6, shift)
                        down(a0 + f, M + 8, shift, first, False)

                    step(1, s0, True)
                    with pe.Fori(2, NFE) as f:
                        step(f, s0 + 6 * (f - 1), False)
                    act_transposes(a0 + NFE)
                    down(a0 + NFE, M + MOE_TILES - 2, s0, False, True)
                    if not last_one:
                        gate_first(e + 1, gathers + 1)
                    pe.wait_ge(sem("dispatchT_ready"), e + 1)
                    pe.wait_ge(sem("y_ready"), e + 1)
                    for c in range(C):
                        t = slice(c * P, (c + 1) * P)
                        for half in range(2):
                            o = ps[:, ADD_BANKS[2 * c + half], :]
                            d = slice(half * BANK, (half + 1) * BANK)
                            nc.tensor.matmul(o, dispT[:, t], y_hi[:, d], start=True, stop=False)
                            nc.tensor.matmul(o, dispT[:, t], y_lo[:, d], start=False, stop=True).then_inc(
                                sem("combined"), 1)

                def one_pass(base, gathers):
                    gather(gathers + 1)
                    gate_first(base, gathers + 1)
                    with pe.Fori(0, NE - 1) as e:
                        expert(e + base, e + gathers + 1, False)
                    expert(base + NE - 1, gathers + NE, True)

                one_pass(0, 0)
                pe.wait_ge(sem("routed"), 1)
                busiest = pe.value_load(most[0:1, 0:1])
                with pe.If(busiest > P):
                    pe.wait_ge(sem("added"), 4 * NE + 1)
                    one_pass(NE, NE)

            mixer(0)
            dense()
            mixer(1)
            experts()

        @block.scalar
        def _(act):
            emptied = [0]
            cols = [0]

            def from_batch(moves):
                act.wait_ge(sem("transposed"), emptied[0] + 1)
                for dst, src, scale in moves(ps[:, 4 + emptied[0] % 4, :]):
                    last = nc.scalar.activation(dst, src, ACT.Copy, scale=scale)
                emptied[0] += 1
                last.then_inc(sem("transposed_used"), 1)

            def pairs(dst, q, gain=None):
                def moves(b):
                    if gain is None:
                        return [(dst[:, q:q + 2, :], b.rearrange("p (k t) -> p k t", k=2), 1.0)]
                    return [(dst[:, q + i, :], b[:, i * SEQ:(i + 1) * SEQ], gain(q + i)) for i in range(2)]
                return moves

            split_tiles = [0]

            def weights_high(l, count=1):
                for _ in range(count):
                    m = split_tiles[0]
                    split_tiles[0] += 1
                    i = SPLIT[m - l * len(SPLIT)]
                    n = BASE[l] + i
                    act.wait_ge(full[n % R], 16 * (n // R + 1))
                    if m - l * len(SPLIT) >= 2:
                        act.wait_ge(*mixer_use(l, SPLIT[m - l * len(SPLIT) - 2]))
                    nc.scalar.activation(hi_m[:, m % 2, :], ring[:, n % R, :], ACT.Copy).then_inc(
                        sem("mixer_hi_ready"), 1)

            def take_columns(dst):
                act.wait_ge(sem("columns_done"), cols[0] + 1)
                pair = 2 * (cols[0] % 2)
                last = nc.scalar.activation(dst, ps[:, pair:pair + 2, 0:dst.shape[2]], ACT.Copy)
                cols[0] += 1
                last.then_inc(sem("columns_used"), 1)

            def sum_squares(slot, src, done):
                for c in range(C):
                    last = nc.scalar.activation(junk(c), src[:, c, :], ACT.Square,
                                                accum_out=ss[:, slot + c:slot + c + 1])
                last.then_inc(sem(done), 1)

            def junk(c):
                return z[:, c, 0:D]

            def load_layer(l):
                s = lparams[l]
                act.dma_start(sp16[:, 0, :], a_re[l].rearrange("(j g) p -> j (g p)", g=2)).then_inc(s, 16)
                act.dma_start(sp16[:, 1, :], a_im[l].rearrange("(j g) p -> j (g p)", g=2)).then_inc(s, 16)
                act.dma_start(dt16[:], log_dt[l].rearrange("(j g) -> j g", g=2)).then_inc(s, 16)
                for r, w in enumerate((b_re, b_im)):
                    act.dma_start(b_raw[:, r], w[l].rearrange("(j g) p c -> (g p) j c", g=2)).then_inc(s, 16)
                for r, w in enumerate((c_re, c_im)):
                    for half in range(2):
                        act.dma_start(c_raw[:, r, :, half * STATE:(half + 1) * STATE],
                                       w[l].rearrange("(q g) c p -> (g c) q p", q=4)).then_inc(s, 16)

            def mixer(l):
                if l > 0:
                    act.wait_ge(sem("x_ready"), l)
                load_layer(l)
                if l == 0:
                    act.wait_ge(sem("mem_loaded"), 16)
                    sum_squares(0, h, "mem_squared")
                    weights_high(0, 2)
                    act.wait_ge(sem("mem_gain_loaded"), 16)
                    for q in range(0, KD, 2):
                        act.wait_ge(sem("transposed"), emptied[0] + 1)
                        b = ps[:, 4 + emptied[0] % 4, :]
                        for i in range(2):
                            nc.scalar.activation(xT_hi[:, q + i, :], b[:, i * SEQ:(i + 1) * SEQ], ACT.Copy,
                                                 scale=gains[:, 1, 0, q + i:q + i + 1])
                        nc.scalar.activation(memT[:, q:q + 2, :], b.rearrange("p (k t) -> p k t", k=2),
                                             ACT.Copy).then_inc(sem("transposed_used"), 1)
                        emptied[0] += 1
                    act.wait_ge(sem("x_loaded"), 16)
                    act.wait_ge(sem("mem_squared"), 1)
                    sum_squares(2, x, "x_squared")
                    weights_high(l)
                    act.wait_ge(params, 16 * (3 * L - 1 + 5 * L))
                else:
                    sum_squares(2, x, "x_squared")
                    weights_high(l)
                act.wait_ge(lparams[l], 16 * 9)
                nc.scalar.activation(dt16[:], dt16[:], ACT.Exp).then_inc(sem("dt_ready"), 1)
                weights_high(l)
                act.wait_ge(sem("angle_ready"), l + 1)
                nc.scalar.activation(sp16[:, 6, :], sp16[:, 2, :], ACT.Exp)
                nc.scalar.activation(sp16[:, 5, :], sp16[:, 9, :], ACT.Sin, scale=-1.0, bias=half_pi[0:NJ, :])
                nc.scalar.activation(sp16[:, 8, :], sp16[:, 4, :], ACT.Sin).then_inc(sem("step_ready"), 1)
                if l == 0:
                    act.wait_ge(sem("rope_angle_ready"), 1)
                    nc.scalar.activation(rope[:, 1], ang[:], ACT.Sin)
                    nc.scalar.activation(rope[:, 0], turns[:], ACT.Sin, scale=-1.0,
                                         bias=half_pi[:]).then_inc(sem("rope_ready"), 1)
                take_columns(kv[:, :, 0:BANK])
                take_columns(kv[:, :, BANK:2 * BANK])
                from_batch(lambda b: [(spT[:, 0:6, :], b[:, 0:6 * NJ].rearrange("p (i j) -> p i j", i=6), 1.0)])
                for q in range(0, KD, 2):
                    from_batch(pairs(hT, q, lambda k: gains[:, 0, l, k:k + 1]))
                take_columns(z[:, :, 0:BANK])
                for r in range(2):
                    from_batch(lambda b: [(bT[:, :, r, :], b.rearrange("p (q s) -> p q s", q=4), 1.0)])
                for r in range(2):
                    def moves(b):
                        v = b.rearrange("p (j g c) -> p j g c", g=2, c=GCH)
                        return [(cT[g * STATE:(g + 1) * STATE, :, r, g * GCH:(g + 1) * GCH],
                                 v[g * STATE:(g + 1) * STATE, :, g, :], 1.0 - 2.0 * r) for g in range(2)]
                    if r == 0:
                        act.wait_ge(sem("cT_zero"), l + 1)
                    from_batch(moves)
                for q in range(0, KS, 2):
                    from_batch(pairs(uT, q))
                act.wait_ge(sem("phase_ready"), l + 1)
                nc.scalar.activation(flat(sintab), flat(sintab), ACT.Sin, scale=TWO_PI)
                nc.scalar.activation(flat(costab), flat(costab), ACT.Sin, scale=-TWO_PI,
                                     bias=half_pi[:]).then_inc(sem("rotation_ready"), 1)
                take_columns(z[:, :, BANK:2 * BANK])
                def head_squares(src, o, dim, heads, sums, scrap):
                    act.wait_ge(sem("columns_used"), cols[0])
                    for c in range(C):
                        for hd in range(heads):
                            last = nc.scalar.activation(scrap(c, hd), src[:, c, o + hd * dim:o + (hd + 1) * dim],
                                                        ACT.Square, accum_out=sums(c, hd))
                    return last

                for n in range(2, SSM_COLS):
                    take_columns(z[:, :, n * BANK:(n + 1) * BANK])
                    for i in range(2):
                        if n == SQUARES_AT[i]:
                            last = head_squares(z, Q0 + i * AW, HD, HEADS,
                                                lambda c, hd: rqk[:, c, i * HEADS + hd:i * HEADS + hd + 1],
                                                lambda c, hd: hi_m[:, c, (i * HEADS + hd) * HD:(i * HEADS + hd + 1) * HD])
                            if i == 1:
                                last.then_inc(sem("qk_squared"), 1)
                    for i, (src, o) in enumerate(((z, MQ0), (kv, 0))):
                        if n == SQUARES_AT[2 + i]:
                            last = head_squares(src, o, XD, XH, lambda c, hd: rm[:, i, c, hd:hd + 1],
                                                lambda c, hd: xT_hi[:, XH * i + hd, c * XD:(c + 1) * XD])
                            if i == 0:
                                last.then_inc(sem("mqk_squared"), 1)
                act.wait_ge(sem("y_used"), KS * (l + 1))
                nc.scalar.activation(flat(gT), flat(gT), ACT.Gelu_apprx_tanh).then_inc(sem("gelu_ready"), 1)
                take_columns(z[:, :, SSM_COLS * BANK:(SSM_COLS + 1) * BANK])
                act.wait_ge(sem("qk_squared"), l + 1)
                act.wait_ge(sem("mqk_squared"), l + 1)
                nc.scalar.activation(flat(xT_hi), flat(hT), ACT.Copy).then_inc(sem("input_hi_ready"), 1)
                weights_high(l, 2)
                for qk in range(2):
                    for i in range(0, HEADS // 2, 2):
                        from_batch(pairs(qkT[:, qk], i))
                for dst, g in ((qmT, 0), (kmT, 1)):
                    for i in range(0, XH, 2):
                        from_batch(pairs(dst, i, lambda k: gmq[:, l, g:g + 1]))
                for s in range(UNITS + 2):
                    if 1 <= s <= UNITS:
                        w = (4 if s > ATT_UNITS else NG * ((s - 1) // SLOTS + 1)) * P
                        act.wait_ge(sem("slot_done"), (UNITS + 2) * l + s + 1)
                        nc.scalar.activation(pT[:, 0:w], flat_banks(6, 2)[:, 0:w], ACT.Copy).then_inc(
                            sem("probsT_ready"), 1)
                    if s < ATT_UNITS:
                        w = NG * (s // SLOTS + 1) * P
                        act.wait_ge(sem("max_ready"), UNITS * l + s + 1)
                        nc.scalar.activation(pr[:, s % 2, 0:w], sc[:, s % 2, 0:w], ACT.Exp, scale=-1.0,
                                             bias=stat[:, s, 0:1], accum_out=stat[:, s, 1:2]).then_inc(
                                                 sem("probs_ready"), 1)
                    elif s < UNITS:
                        c, hd = (s - ATT_UNITS) // 2, (s - ATT_UNITS) % 2 * 2
                        act.wait_ge(sem("max_ready"), UNITS * l + s + 1)
                        for i in range(2):
                            last = nc.scalar.activation(
                                pr[:, s % 2, i * MEM:(i + 1) * MEM], ps[:, 4, i * MEM:(i + 1) * MEM], ACT.Exp,
                                scale=XD ** -0.5, bias=rm[:, 0, c, hd + i:hd + i + 1],
                                accum_out=rm[:, 1, c, hd + i:hd + i + 1])
                        last.then_inc(sem("probs_ready"), 1)
                    if s < AHEAD:
                        weights_high(l)
                    if s < len(FILL):
                        t, i = FILL[s]
                        if t == "glu" and i == 1:
                            act.wait_ge(sem("columns_done"), cols[0] + 2)
                            pair = 2 * ((cols[0] + 1) % 2)
                            nc.scalar.activation(sig, ps[:, pair:pair + 2, :], ACT.Sigmoid).then_inc(
                                sem("glu_gate_ready"), 1)
                            act.wait_ge(sem("columns_used"), cols[0])
                            for c in range(C):
                                last = nc.scalar.activation(z[:, c, GATE0:GATE0 + D], z[:, c, GATE0:GATE0 + D],
                                                            ACT.Sigmoid)
                            last.then_inc(sem("ssm_gate_ready"), 1)
                            cols[0] += 2
                        elif t == "transposes":
                            act.wait_ge(sem("columns_done"), cols[0] + 1)
                            pair = 2 * (cols[0] % 2)
                            nc.scalar.activation(flat(soT), flat_banks(pair, 2), ACT.Copy).then_inc(
                                sem("columns_used"), 1)
                            cols[0] += 1
                        elif t == "branch":
                            cols[0] += 1
                        elif t == IN_FULL:
                            take_columns(z[:, :, IN_FULL * BANK:COLS])
                        elif t not in ("glu", "none") and i == 1:
                            take_columns(z[:, :, t * BANK:(t + 1) * BANK])
                for c in range(C):
                    last = nc.scalar.activation(z[:, c, GATE0 + D:COLS], z[:, c, GATE0 + D:COLS], ACT.Sigmoid)
                last.then_inc(sem("gates_ready"), 1)
                from_batch(pairs(oT, 0))
                for q in range(0, XH, 2):
                    from_batch(pairs(omT, q))
                cols[0] += 4
                weights_high(l, 2)
                for q in range(0, KD, 2):
                    act.wait_ge(sem("transposed"), emptied[0] + 1)
                    b = ps[:, 4 + emptied[0] % 4, :]
                    nc.scalar.activation(xT_hi[:, q:q + 2, :], b.rearrange("p (k t) -> p k t", k=2),
                                         ACT.Copy).then_inc(sem("xT_hi_ready"), 1)
                    emptied[0] += 1
                weights_high(l, 2)
                cols[0] += 2
                act.wait_ge(sem("columns_used"), COL_TILES * (l + 1))
                sum_squares(2, x, "x_squared")

            def flat_banks(b, n):
                return ps[:, b:b + n, :].rearrange("p b n -> p (b n)")

            def hi_part(src, src_full, m, shift, after=True):
                act.wait_ge(*src_full)
                if after:
                    act.wait_ge(sem("split_used"), m - H + 1 + shift)
                nc.scalar.activation(hi[:, m % H, :], src, ACT.Copy).then_inc(sem("hi_ready"), 1)

            def dense():
                def split(m, shift, after=True):
                    n = MIX_TILES + m
                    hi_part(ring[:, n % R, :], (full[n % R], 16 * (n // R + 1 + shift)), m, 3 * shift, after)

                act.wait_ge(sem("h_ready"), 3)
                split(0, 0, False)
                split(1, 0, False)
                for q in range(0, KD, 2):
                    def moves(b):
                        return [(hT_hi[:, q + i, :], b[:, i * SEQ:(i + 1) * SEQ], gains[:, 2, 0, q + i:q + i + 1])
                                for i in range(2)]
                    act.wait_ge(sem("transposed"), emptied[0] + 1)
                    for dst, src, scale in moves(ps[:, 4 + emptied[0] % 4, :]):
                        last = nc.scalar.activation(dst, src, ACT.Copy, scale=scale)
                    last.then_inc(sem("hT_hi_ready"), 1)
                    emptied[0] += 1

                def silu(f, gate_done):
                    act.wait_ge(sem("split_used"), gate_done)
                    nc.scalar.activation(gate_act[:], ps[:, 0, :], ACT.Silu).then_inc(sem("silu_done"), 1)

                def act_hi(f):
                    act.wait_ge(sem("actT_done"), f)
                    nc.scalar.activation(aT_hi[:], ps[:, 2, :], ACT.Copy).then_inc(sem("aT_hi_ready"), 1)

                def step(f, s, wait_act):
                    split(2, s)
                    split(3, s)
                    if wait_act:
                        act.wait_ge(sem("split_used"), 3 * f - 1)
                    act_hi(f)
                    split(4, s)
                    act.wait_ge(sem("act_ready"), f)
                    silu(f, 3 * f)

                for k in range(KD):
                    last = nc.scalar.activation(xT_hi[:, k, :], memT[:, k, :], ACT.Copy, scale=gains[:, 1, 1, k:k + 1])
                last.then_inc(sem("memory_hi_ready"), 1)
                silu(0, 1)
                split(2, 0, False)
                split(3, 0)
                act_hi(1)
                split(4, 0)
                act.wait_ge(sem("act_ready"), 1)
                silu(1, 3)
                with act.Fori(2, NF) as f:
                    step(f, f - 1, True)
                act.wait_ge(sem("split_used"), 3 * NF - 1)
                act_hi(NF)
                split(FFN_TILES - 1, 0)
                for i in range(2):
                    act.wait_ge(sem("split_used"), FFN_TILES - 2 + i)
                    weights_high(1)

            def experts():
                def split(c, M, s, turn):
                    hi_part(ring_e[:, c % RM, :], (full_e[c % RM], 16 * (turn + 1)), M, s)

                act.wait_ge(sem("h_ready"), 2 * L + 1)
                for i in range(2):
                    split(i, FFN_TILES + i, 0, 0)
                for q in range(0, KD, 2):
                    from_batch(pairs(hT, q, lambda k: gains[:, 2, 1, k:k + 1]))
                split(2, FFN_TILES + 2, 0, 0)
                act.wait_ge(sem("logits_ready"), 1)
                nc.scalar.activation(lg[:].rearrange("p c e -> p (c e)"), lg[:].rearrange("p c e -> p (c e)"),
                                     ACT.Exp).then_inc(sem("routes_exp"), 1)

                def gathered_high(count):
                    act.wait_ge(sem("xe_scaled"), count)
                    nc.scalar.activation(xe_hi[:], xe[:], ACT.Copy).then_inc(sem("xe_hi_ready"), 1)

                def expert(e, gathers, last_one):
                    a0 = NF + NFE * e
                    t0 = NFE * e
                    s0 = MOE_TILES * e
                    M = FFN_TILES

                    def silu(a, gate_done):
                        act.wait_ge(sem("split_used"), gate_done)
                        act.wait_ge(sem("act_ready"), a)
                        nc.scalar.activation(gate_act[:], ps[:, 0, :], ACT.Silu).then_inc(sem("silu_done"), 1)

                    def act_hi(a, down_done):
                        act.wait_ge(sem("actT_done"), a)
                        act.wait_ge(sem("split_used"), down_done)
                        nc.scalar.activation(aT_hi[:], ps[:, 2, :], ACT.Copy).then_inc(sem("aT_hi_ready"), 1)

                    split(3, M + 3, s0, t0)
                    silu(a0, M + s0 + 2)

                    def step(f, s, turn):
                        for i in range(4):
                            split(4 + i, M + 4 + i, s, turn + (4 + i) // RM)
                        act_hi(a0 + f, M + s + 4)
                        split(8, M + 8, s, turn + 1)
                        silu(a0 + f, M + s + 6)
                        split(9, M + 9, s, turn + 1)

                    with act.Fori(1, NFE) as f:
                        step(f, s0 + 6 * (f - 1), t0 + f - 1)
                    split(4, M + MOE_TILES - 2, s0, t0 + NFE - 1)
                    if not last_one:
                        act.wait_ge(sem("split_used"), M + s0 + MOE_TILES - 4)
                        gathered_high(gathers + 1)
                    split(5, M + MOE_TILES - 1, s0, t0 + NFE - 1)
                    act_hi(a0 + NFE, M + s0 + MOE_TILES - 4)
                    if not last_one:
                        for i in range(2):
                            split(i, M + i, s0 + MOE_TILES, t0 + NFE)
                    act.wait_ge(sem("added"), 4 * e + 1)
                    act.wait_ge(sem("split_used"), M + s0 + MOE_TILES)
                    nc.scalar.activation(y_hi[:], flat_banks(4, 2), ACT.Copy).then_inc(sem("y_hi_ready"), 1)
                    if not last_one:
                        split(2, M + 2, s0 + MOE_TILES, t0 + NFE)

                def one_pass(base, gathers):
                    if base:
                        for i in range(3):
                            split(i, FFN_TILES + i, MOE_TILES * base, NFE * base)
                    gathered_high(gathers + 1)
                    with act.Fori(0, NE - 1) as e:
                        expert(e + base, e + gathers + 1, False)
                    expert(base + NE - 1, gathers + NE, True)

                one_pass(0, 0)
                act.wait_ge(sem("routed"), 1)
                busiest = act.value_load(most[0:1, 0:1])
                with act.If(busiest > P):
                    one_pass(NE, NE)

            mixer(0)
            dense()
            mixer(1)
            experts()

        @block.vector
        def _(dve):
            done = sem("vector_chain")
            n = [0]
            V = nc.vector

            def chain(ins):
                n[0] += 1
                ins.then_inc(done, 1)
                dve.wait_ge(done, n[0])

            def reduce_angle(r, k, a):
                chain(V.tensor_scalar(k, a, 1 / TWO_PI, ROUND, ALU.mult, ALU.add))
                chain(V.tensor_scalar(k, k, ROUND, None, ALU.subtract))
                chain(V.scalar_tensor_tensor(out=r, in0=k, scalar=-PI_A, in1=a, op0=ALU.mult, op1=ALU.add))
                chain(V.scalar_tensor_tensor(out=r, in0=k, scalar=-PI_B, in1=r, op0=ALU.mult, op1=ALU.add))
                chain(V.scalar_tensor_tensor(out=r, in0=k, scalar=-PI_C, in1=r, op0=ALU.mult, op1=ALU.add))
                chain(V.tensor_scalar(r, r, 3.1415925, -3.1415925, ALU.min, ALU.max))
                return V.scalar_tensor_tensor(out=k, in0=r, scalar=-1.0, in1=r, op0=ALU.mult, op1=ALU.max)

            split_tiles = [0]

            def weights_low(l, count=1):
                for _ in range(count):
                    m = split_tiles[0]
                    split_tiles[0] += 1
                    n = BASE[l] + SPLIT[m - l * len(SPLIT)]
                    dve.wait_ge(sem("mixer_hi_ready"), m + 1)
                    V.tensor_tensor(ring_lo[:, n % R, :], ring[:, n % R, :], hi_m[:, m % 2, :].bitcast(F32),
                                    ALU.subtract).then_inc(sem("mixer_lo_ready"), 1)

            operands = [0]

            def operand_low(batch):
                for q in range(0, KD, 2):
                    operands[0] += 1
                    dve.wait_ge(sem("xT_hi_ready"), operands[0])
                    b = ps[:, 4 + (batch + q // 2) % 4, :]
                    V.tensor_tensor(xT_lo[:, q:q + 2, :], b.rearrange("p (k t) -> p k t", k=2),
                                    xT_hi[:, q:q + 2, :].bitcast(F32), ALU.subtract).then_inc(
                                        sem("transposed_used"), 1)

            def memory_low(l, q):
                for k in (q, q + 1):
                    last = V.scalar_tensor_tensor(out=xT_lo[:, k, :], in0=memT[:, k, :], scalar=gains[:, 1, l, k:k + 1],
                                                  in1=xT_hi[:, k, :].bitcast(F32), op0=ALU.mult, op1=ALU.subtract)
                return last

            def scale_rows(dst, src, r0):
                for c in range(C):
                    last = V.tensor_scalar(dst[:, c, :], src[:, c, :], rs[:, r0 + c:r0 + c + 1], None, ALU.mult)
                return last

            def setup():
                dve.wait_ge(sem("mem_rs"), 1)
                scale_rows(h, h, 0).then_inc(sem("h_ready"), 1)

            def constants():
                dve.wait_ge(sem("consts_ready"), 1)
                V.tensor_copy(ramp[:], ramp_i[:])
                for c in range(C):
                    for i, g in enumerate((1, 2)):
                        chain(V.tensor_scalar(grid_i[:, i, :], dist_i[:, c, :], DIL[g] - 1, None, ALU.bitwise_and))
                        last = V.tensor_scalar(gmask(c, g), grid_i[:, i, 0:(c + 1) * P], 0, NEG, ALU.is_gt, ALU.mult)
                last.then_inc(sem("grid_ready"), 1)
                dve.wait_ge(sem("mem_gain_loaded"), 16)
                weights_low(0)
                for q in range(0, KD, 2):
                    dve.wait_ge(sem("transposed_used"), q // 2 + 1)
                    last = memory_low(0, q)
                last.then_inc(sem("memT_scaled"), 1)
                weights_low(0)
                dve.wait_ge(sem("pos_loaded"), 16)
                chain(V.tensor_copy(pos[:], pos_i[:]))
                for c in range(C):
                    last = V.tensor_scalar(turns[:, c, :], invf[:], pos[:, c:c + 1], None, ALU.mult)
                chain(last)
                chain(V.tensor_copy(ang[:], turns[:]))
                reduce_angle(ang[:], turns[:], ang[:]).then_inc(sem("rope_angle_ready"), 1)
                weights_low(0)

            def ssm_setup(l):
                s = sp16
                if l > 0:
                    dve.wait_ge(sem("x_ready"), l)
                    weights_low(l)
                dve.wait_ge(lparams[l], 16 * 9)
                dve.wait_ge(sem("dt_ready"), l + 1)
                dt = spread(dt16[:], 2, STATE)
                for i in range(2):
                    last = V.tensor_tensor(s[:, 2 + i, :].rearrange("j (g p) -> j g p", g=2),
                                           s[:, i, :].rearrange("j (g p) -> j g p", g=2), dt, ALU.mult)
                chain(last)
                weights_low(l)
                reduce_angle(s[:, 4, :], s[:, 9, :], s[:, 3, :]).then_inc(sem("angle_ready"), 1)
                chain(V.tensor_scalar(s[:, 10, :], s[:, 4, :], 1 / TWO_PI, None, ALU.mult))
                chain(V.tensor_scalar(s[:, 11, :], s[:, 10, :], ROUND_FINE, None, ALU.add))
                chain(V.tensor_scalar(s[:, 11, :], s[:, 11, :], ROUND_FINE, None, ALU.subtract))
                dve.wait_ge(sem("step_ready"), l + 1)
                V.tensor_tensor(s[:, 8, :], s[:, 8, :], s[:, 6, :], ALU.mult)
                chain(V.tensor_tensor(s[:, 5, :], s[:, 5, :], s[:, 6, :], ALU.mult))
                chain(V.tensor_scalar(s[:, 5, :], s[:, 5, :], 1.0, None, ALU.subtract))
                V.tensor_tensor(s[:, 2, :], s[:, 5, :], s[:, 0, :], ALU.mult)
                V.tensor_tensor(s[:, 9, :], s[:, 8, :], s[:, 1, :], ALU.mult)
                V.tensor_tensor(s[:, 3, :], s[:, 8, :], s[:, 0, :], ALU.mult)
                chain(V.tensor_tensor(s[:, 7, :], s[:, 5, :], s[:, 1, :], ALU.mult))
                V.tensor_tensor(s[:, 2, :], s[:, 2, :], s[:, 9, :], ALU.add)
                chain(V.tensor_tensor(s[:, 3, :], s[:, 3, :], s[:, 7, :], ALU.subtract))
                V.tensor_tensor(s[:, 0, :], s[:, 0, :], s[:, 0, :], ALU.mult)
                chain(V.tensor_tensor(s[:, 1, :], s[:, 1, :], s[:, 1, :], ALU.mult))
                chain(V.tensor_tensor(s[:, 0, :], s[:, 0, :], s[:, 1, :], ALU.add))
                chain(V.reciprocal(s[:, 0, :], s[:, 0, :]))
                V.tensor_tensor(s[:, 2, :], s[:, 2, :], s[:, 0, :], ALU.mult)
                V.tensor_tensor(s[:, 3, :], s[:, 3, :], s[:, 0, :], ALU.mult).then_inc(sem("ssm_params"), 1)
                dve.wait_ge(sem("x_rs"), 2 * l + 1)
                if l == 0:
                    dve.wait_ge(sem("transposed"), 4)
                scale_rows(h, x, 2).then_inc(sem("h_ready"), 1)
                V.memset(b_bar, 0.0)
                V.memset(cT[:], 0.0).then_inc(sem("cT_zero"), 1)
                dve.wait_ge(sem("transposed_used"), batches_to(l, "ssm"))
                f_re, f_im = spread(spT[:, 4, :], 2, GCH), spread(spT[:, 5, :], 2, GCH)
                for r, (p, q, op) in enumerate(((f_re, f_im, ALU.subtract), (f_im, f_re, ALU.add))):
                    V.tensor_tensor(b_tmp, b_raw[:, 0], p, ALU.mult)
                    chain(V.tensor_tensor(b_tmp2, b_raw[:, 1], q, ALU.mult))
                    for g in range(2):
                        rows = slice(g * STATE, (g + 1) * STATE)
                        last = V.tensor_tensor(b_bar[rows, r, :, g * GCH:(g + 1) * GCH], b_tmp[rows], b_tmp2[rows], op)
                    chain(last)
                last = V.memset(stat[:, 0, 3:4], 0.0)
                last.then_inc(sem("b_bar_ready"), 1)
                if l == 0:
                    dve.wait_ge(sem("rope_ready"), 1)
                for j in range(NJ):
                    last = V.tensor_scalar(costab[:, j, :], ramp[:], spT[:, 2, j:j + 1], ROUND, ALU.mult, ALU.add)
                chain(last)
                chain(V.tensor_scalar(flat(costab), flat(costab), ROUND, None, ALU.subtract))
                for j in range(NJ):
                    last = V.scalar_tensor_tensor(out=sintab[:, j, :], in0=ramp[:], scalar=spT[:, 3, j:j + 1],
                                                  in1=costab[:, j, :], op0=ALU.mult, op1=ALU.subtract)
                V.tensor_tensor(spT[:, 6, :], spT[:, 2, :], spT[:, 3, :], ALU.subtract)
                chain(last)
                chain(V.memset(stat[:, 0, 3:4], 0.0))
                for j in range(NJ):
                    last = V.scalar_tensor_tensor(out=sintab[:, j, :], in0=ramp[:], scalar=spT[:, 6, j:j + 1],
                                                  in1=sintab[:, j, :], op0=ALU.mult, op1=ALU.add)
                chain(last)
                chain(V.tensor_scalar(flat(sintab), flat(sintab), 0.4999999, -0.4999999, ALU.min, ALU.max))
                V.scalar_tensor_tensor(out=flat(costab), in0=flat(sintab), scalar=-1.0, in1=flat(sintab),
                                       op0=ALU.mult, op1=ALU.max).then_inc(sem("phase_ready"), 1)

            def ssm(l):
                dve.wait_ge(sem("rotation_ready"), l + 1)
                for v in range(NJ // 2):
                    j = 2 * v
                    cos, sin = costab[:, j:j + 2, :], sintab[:, j:j + 2, :]
                    bu = ps[:, 4:6, :].rearrange("p j (r t) -> p j r t", r=2)
                    dve.wait_ge(sem("bu_done"), NJ // 2 * l + v + 1)
                    V.tensor_tensor(wa[:], bu, spread(cos, 2, 2), ALU.mult)
                    V.tensor_tensor(wb[:, :, 0, :], bu[:, :, 1, :], sin, ALU.mult)
                    last = V.tensor_tensor(wb[:, :, 1, :], bu[:, :, 0, :], sin, ALU.mult)
                    last.then_inc(sem("bu_used"), 1)
                    dve.wait_ge(sem("bu_used"), NJ // 2 * l + v + 1)
                    V.tensor_tensor(wv[:, :, 0, :], wa[:, :, 0, :], wb[:, :, 0, :], ALU.add)
                    chain(V.tensor_tensor(wv[:, :, 1, :], wa[:, :, 1, :], wb[:, :, 1, :], ALU.subtract))
                    for i in range(2):
                        for r in range(2):
                            last = V.tensor_tensor_scan(wp[:, i, r, :], spT[:, 0, j + i:j + i + 1].to_broadcast([P, SEQ]),
                                                        wv[:, i, r, :], 0.0, ALU.mult, ALU.add)
                    chain(last)
                    V.tensor_tensor(wa[:], wp[:], spread(cos, 2, 2), ALU.mult)
                    chain(V.tensor_tensor(wb[:], wp[:], spread(sin, 2, 2), ALU.mult))
                    V.tensor_tensor(wv[:, :, 0, :], wa[:, :, 0, :], wb[:, :, 1, :], ALU.subtract)
                    V.tensor_tensor(wv[:, :, 1, :], wa[:, :, 1, :], wb[:, :, 0, :], ALU.add).then_inc(
                        sem("states_ready"), 1)
                    if v % 2 == 1:
                        q = v // 2
                        dve.wait_ge(sem("y_done"), NJ // 2 * l + v + 1)
                        if q == 0:
                            dve.wait_ge(params, 16 * (3 * L - 1 + 5 * L))
                        last = V.scalar_tensor_tensor(out=gT[:, q, :], in0=uT[:, q, :], scalar=dsk[:, l, q:q + 1],
                                                      in1=ps[:, 6, q % 2 * SEQ:(q % 2 + 1) * SEQ], op0=ALU.mult,
                                                      op1=ALU.add)
                        last.then_inc(sem("y_used"), 1)

            def attention_inputs(l):
                if l == 0:
                    dve.wait_ge(sem("rope_ready"), 1)
                for qk in range(2):
                    for r in range(2):
                        for half in range(2):
                            g = gqk[:, l, qk, half * 32:(half + 1) * 32]
                            last = V.tensor_tensor(rgain[:, qk, r, :, half * 32:(half + 1) * 32], rope[:, r],
                                                   spread(g, 1, C), ALU.mult)
                chain(last)
                dve.wait_ge(sem("columns_used"), COL_TILES * l + 2 + SSM_COLS - 1)
                qk = z[:, :, Q0:Q0 + 2 * AW]
                by_head = qk.rearrange("p c (h d) -> p c h d", d=HD)
                mq = z[:, :, MQ0:MQ0 + XW]
                mk = kv[:, :, 0:XW]
                for t, r in ((t1, 0), (t2, 1)):
                    for i in range(2):
                        for c in range(C):
                            w = slice(i * AW, (i + 1) * AW)
                            last = V.tensor_tensor(t[:, c, w].rearrange("p (h d) -> p h d", d=HD),
                                                   qk[:, c, w].rearrange("p (h d) -> p h d", d=HD),
                                                   spread(rgain[:, i, r, c, :], 1, HEADS), ALU.mult)
                chain(last)
                a = t1[:].rearrange("p c (h d) -> p c h d", d=HD)
                b = t2[:].rearrange("p c (h d) -> p c h d", d=HD)
                lo_, hi_ = slice(0, HD // 2), slice(HD // 2, HD)
                V.tensor_tensor(by_head[:, :, :, lo_], a[:, :, :, lo_], b[:, :, :, hi_], ALU.subtract)
                chain(V.tensor_tensor(by_head[:, :, :, hi_], b[:, :, :, lo_], a[:, :, :, hi_], ALU.add))
                dve.wait_ge(sem("qk_rs"), l + 1)
                V.tensor_tensor(by_head, by_head, spread(rqk2[:], 3, HD), ALU.mult).then_inc(sem("qk_ready"), 1)
                dve.wait_ge(sem("mqk_rs"), l + 1)
                for i, t in enumerate((mq, mk)):
                    v = t.rearrange("p c (h d) -> p c h d", d=XD)
                    last = V.tensor_tensor(v, v, spread(rm2[:, i], 3, XD), ALU.mult)
                last.then_inc(sem("mqk_ready"), 1)
                dve.wait_ge(sem("input_hi_ready"), l + 1)
                dve.wait_ge(*mixer_use(l, SPLIT[KV_TILES] - 1))
                V.tensor_tensor(xT_lo[:], hT[:], xT_hi[:].bitcast(F32), ALU.subtract).then_inc(
                    sem("input_lo_ready"), 1)
                weights_low(l)

            def attention(l):
                def take(u):
                    if u >= ATT_UNITS:
                        c, hd = (u - ATT_UNITS) // 2, (u - ATT_UNITS) % 2 * 2
                        chain(V.reciprocal(rm2[:, 1, c, hd:hd + 2], rm[:, 1, c, hd:hd + 2]))
                        return V.tensor_tensor(omem[:, c, hd * XD:(hd + 2) * XD].rearrange("p (h d) -> p h d", d=XD),
                                               ps[:, 5, 2 * P:BANK].rearrange("p (h d) -> p h d", d=XD),
                                               spread(rm2[:, 1, c, hd:hd + 2], 2, XD), ALU.mult)
                    c, s = u // SLOTS, u % SLOTS
                    chain(V.reciprocal(stat[:, u, 2:3], stat[:, u, 1:2]))
                    return V.tensor_scalar(oatt[:, c, s * HD:(s + 1) * HD], ps[:, 5, 2 * P:2 * P + HD],
                                           stat[:, u, 2:3], None, ALU.mult)

                if l == 0:
                    dve.wait_ge(sem("mask_ready"), 1)
                for s in range(UNITS + 2):
                    dve.wait_ge(sem("slot_done"), (UNITS + 2) * l + s + 1)
                    if s >= 2:
                        last = take(s - 2)
                    if s < ATT_UNITS:
                        c = s // SLOTS
                        w = NG * (c + 1) * P
                        if s >= 2:
                            dve.wait_ge(sem("probs_ready"), UNITS * l + s - 1)
                        last = V.scalar_tensor_tensor(
                            out=sc[:, s % 2, 0:w], in0=ps[:, 4:6, :].rearrange("p b n -> p (b n)")[:, 0:w],
                            scalar=-HD ** -0.5, in1=mask[:, c * NG * P:c * NG * P + w], op0=ALU.mult, op1=ALU.subtract)
                        last.then_inc(sem("slot_used"), 1)
                        dve.wait_ge(sem("slot_used"), (UNITS + 2) * l + s + 1)
                        V.tensor_reduce(stat[:, s, 0:1], sc[:, s % 2, 0:w], AX.X, ALU.min).then_inc(sem("max_ready"), 1)
                    elif s < UNITS:
                        c, hd = (s - ATT_UNITS) // 2, (s - ATT_UNITS) % 2 * 2
                        last = V.tensor_reduce(rm2[:, 0, c, hd:hd + 2], ps[:, 4, :].rearrange("p (h m) -> p h m", m=MEM),
                                               AX.X, ALU.max)
                        last.then_inc(sem("slot_used"), 1)
                        dve.wait_ge(sem("slot_used"), (UNITS + 2) * l + s + 1)
                        V.tensor_scalar(rm[:, 0, c, hd:hd + 2], rm2[:, 0, c, hd:hd + 2], -XD ** -0.5, None,
                                        ALU.mult).then_inc(sem("max_ready"), 1)
                    else:
                        last.then_inc(sem("slot_used"), 1)
                    if s <= AHEAD:
                        weights_low(l)
                    if s == GLU_AT:
                        glu(l)
                    elif s >= 1 and s <= len(FILL) and FILL[s - 1][0] == "transposes":
                        cols[0] += 1
                    elif s >= 1 and s <= len(FILL) and FILL[s - 1][0] == "branch":
                        if FILL[s - 1][1] == 0:
                            dve.wait_ge(sem("ssm_gate_ready"), l + 1)
                        gated(0, FILL[s - 1][1], l)

            def glu(l):
                dve.wait_ge(sem("glu_gate_ready"), l + 1)
                pair = 2 * (cols[0] % 2)
                last = V.tensor_tensor(sout, ps[:, pair:pair + 2, :], sig, ALU.mult)
                last.then_inc(sem("columns_used"), 2)
                cols[0] += 2

            cols = [0]
            CT = 2 + IN_FULL + 1

            def gated(b, half, l):
                dve.wait_ge(sem("columns_done"), cols[0] + 1)
                pair = 2 * (cols[0] % 2)
                o = slice(half * BANK, (half + 1) * BANK)
                g = z[:, :, GATE0 + b * D + half * BANK:GATE0 + b * D + (half + 1) * BANK]
                if b == 0:
                    V.tensor_tensor(merged[:, :, o], ps[:, pair:pair + 2, :], g, ALU.mult).then_inc(
                        sem("columns_used"), 1)
                else:
                    V.tensor_tensor(g, ps[:, pair:pair + 2, :], g, ALU.mult).then_inc(sem("columns_used"), 1)
                dve.wait_ge(sem("columns_used"), cols[0] + 1)
                cols[0] += 1
                if b > 0:
                    last = V.tensor_tensor(merged[:, :, o], merged[:, :, o], g, ALU.add)
                    if b == 2 and half == 1:
                        last.then_inc(sem("merged_ready"), 1)
                    else:
                        chain(last)

            def merge(l):
                dve.wait_ge(sem("gates_ready"), l + 1)
                for b in range(1, 3):
                    if b == 2:
                        weights_low(l)
                    for half in range(2):
                        gated(b, half, l)
                operand_low(batches_to(l, "mem_out"))
                weights_low(l, 3)
                for half in range(2):
                    dve.wait_ge(sem("columns_done"), cols[0] + 1)
                    pair = 2 * (cols[0] % 2)
                    o = slice(half * BANK, (half + 1) * BANK)
                    last = V.tensor_tensor(x[:, :, o], ps[:, pair:pair + 2, :], x[:, :, o], ALU.add)
                    last.then_inc(sem("columns_used"), 1)
                    cols[0] += 1
                dve.wait_ge(sem("x_rs"), 2 * l + 2)
                scale_rows(h, x, 2).then_inc(sem("h_ready"), 1)

            def lo_part(src, m, shift):
                dve.wait_ge(sem("hi_ready"), m + 1 + shift)
                last = V.tensor_tensor(lo[:, m % H, :], src, hi[:, m % H, :].bitcast(F32), ALU.subtract)
                last.then_inc(sem("lo_ready"), 1)

            def act_low(a):
                dve.wait_ge(sem("aT_hi_ready"), a)
                V.tensor_tensor(aT_lo[:], ps[:, 2, :], aT_hi[:].bitcast(F32), ALU.subtract).then_inc(
                    sem("actT_ready"), 1)

            def act_product(a, up_done):
                dve.wait_ge(sem("split_used"), up_done)
                dve.wait_ge(sem("silu_done"), a)
                V.tensor_tensor(act_out[:], ps[:, 1, :], gate_act[:], ALU.mult).then_inc(sem("act_ready"), 1)

            def dense():
                def split(m, shift):
                    n_ = MIX_TILES + m
                    lo_part(ring[:, n_ % R, :], m, 3 * shift)

                split(0, 0)
                for q in range(0, KD, 2):
                    dve.wait_ge(sem("hT_hi_ready"), q // 2 + 1)
                    for i in range(2):
                        b = ps[:, 4 + (batches_to(0, "merged") + q // 2) % 4, i * SEQ:(i + 1) * SEQ]
                        last = V.scalar_tensor_tensor(out=hT_lo[:, q + i, :], in0=b, scalar=gains[:, 2, 0, q + i:q + i + 1],
                                                      in1=hT_hi[:, q + i, :].bitcast(F32), op0=ALU.mult,
                                                      op1=ALU.subtract)
                    last.then_inc(sem("transposed_used"), 1)

                split(1, 0)
                dve.wait_ge(sem("memory_hi_ready"), 1)
                for q in range(0, KD, 2):
                    last = memory_low(1, q)
                last.then_inc(sem("memT_scaled"), 1)
                act_product(1, 2)

                def step(f, s):
                    split(2, s)
                    split(3, s)
                    act_low(f)
                    split(4, s)
                    act_product(f + 1, 3 * f + 1)
                with dve.Fori(1, NF) as f:
                    step(f, f - 1)
                act_low(NF)
                split(FFN_TILES - 1, 0)
                weights_low(1, 2)
                dve.wait_ge(sem("split_used"), FFN_TILES)
                for c in range(C):
                    last = V.tensor_tensor(x[:, c, :], ps[:, 4 + 2 * c:6 + 2 * c, :].rearrange("p b n -> p (b n)"),
                                           x[:, c, :], ALU.add)
                last.then_inc(sem("x_ready"), 1)
                dve.wait_ge(sem("x_ready"), 1)

            def route():
                for c in range(1):
                    V.memset(slot_of[:], -1.0)
                V.memset(tie[:], 0.0)
                chain(V.memset(rstat[:], 0.0))
                for e in range(1, NE):
                    last = V.memset(tie[:, e, 0:e], 1.0)
                for i in range(3):
                    lo_part(ring_e[:, i, :], FFN_TILES + i, 0)
                dve.wait_ge(sem("logits_done"), 1)
                chain(V.tensor_copy(lg[:], ps[:, 3, 0:C * NE].rearrange("p (c e) -> p c e", c=C)))
                mine = spread(lg[:], 3, NE)
                other = spread(lg[:], 2, NE)
                for c in range(C):
                    V.tensor_tensor(cmp_[:, 0, c], other[:, c], mine[:, c], ALU.is_gt)
                    chain(V.tensor_tensor(cmp_[:, 1, c], other[:, c], mine[:, c], ALU.is_equal))
                    chain(V.tensor_tensor(cmp_[:, 1, c], cmp_[:, 1, c], tie[:], ALU.mult))
                    chain(V.tensor_tensor(cmp_[:, 0, c], cmp_[:, 0, c], cmp_[:, 1, c], ALU.add))
                chain(V.tensor_reduce(sel[:], cmp_[:, 0], AX.X, ALU.add))
                last = V.tensor_scalar(sel[:], sel[:], 2.0, None, ALU.is_lt)
                last.then_inc(sem("selected"), 1)
                dve.wait_ge(sem("selected"), 1)
                chain(V.tensor_reduce(rstat[:, 0:2], lg[:], AX.X, ALU.max))
                V.tensor_tensor(lg[:], lg[:], spread(rstat[:, 0:2], 2, NE), ALU.subtract).then_inc(
                    sem("logits_ready"), 1)
                dve.wait_ge(sem("routes_exp"), 1)
                chain(V.tensor_tensor(gate[:], lg[:], sel[:], ALU.mult))
                chain(V.tensor_reduce(rstat[:, 2:4], gate[:], AX.X, ALU.add))
                chain(V.reciprocal(rstat[:, 2:4], rstat[:, 2:4]))
                chain(V.tensor_tensor(gate[:], gate[:], spread(rstat[:, 2:4], 2, NE), ALU.mult))
                dve.wait_ge(sem("places_done"), 1)
                where = slot_of[:, :, 0:NE]
                chain(V.tensor_scalar(where, ps[:, 3, 0:C * NE].rearrange("p (c e) -> p c e", c=C), 1.0, None, ALU.add))
                chain(V.tensor_tensor(where, where, sel[:], ALU.mult))
                chain(V.tensor_scalar(where, where, 1.0, None, ALU.subtract))
                chain(V.tensor_reduce(rstat[:, 4:5], ps[:, 3, 2 * NE:3 * NE], AX.X, ALU.max))
                last = V.tensor_copy(most[:], rstat[:, 4:5])
                last.then_inc(sem("routed"), 1)
                V.memset(rstat[:, 5:6], 0.0).then_inc(sem("added"), 1)

            def experts():
                route()

                def dispatch(e):
                    for c in range(C):
                        last = V.tensor_scalar(disp[:, c, :], ramp[:, 0:P], slot_of[:, c, bass.ds(e, 1)], None,
                                               ALU.is_equal)
                    last.then_inc(sem("dispatch_ready"), 1)

                def scale_gathered(count):
                    dve.wait_ge(sem("gathered"), count)
                    V.tensor_tensor(xe[:], ps[:, 6:8, :].rearrange("p b (k t) -> p (b k) t", t=P),
                                    spread(gains[:, 2, 1, :], 2, P), ALU.mult).then_inc(sem("xe_scaled"), 1)

                def gathered_low(count):
                    dve.wait_ge(sem("xe_hi_ready"), count)
                    V.tensor_tensor(xe_lo[:], xe[:], xe_hi[:].bitcast(F32), ALU.subtract).then_inc(
                        sem("xe_ready"), 1)

                def split(c, M, s):
                    lo_part(ring_e[:, c % RM, :], M, s)

                def add_rows(e_here, e):
                    dve.wait_ge(sem("added"), 4 * e + 1)
                    for c in range(C):
                        for half in range(2):
                            i = 2 * c + half
                            o = slice(half * BANK, (half + 1) * BANK)
                            dve.wait_ge(sem("combined"), 4 * e + i + 1)
                            V.scalar_tensor_tensor(x[:, c, o], ps[:, ADD_BANKS[i], :],
                                                   gate[:, c, bass.ds(e_here, 1)], x[:, c, o], ALU.mult,
                                                   ALU.add).then_inc(sem("added"), 1)

                def expert(e_here, e, gathers, first_one, last_one):
                    a0 = NF + NFE * e
                    s0 = MOE_TILES * e
                    M = FFN_TILES
                    split(3, M + 3, s0)
                    if not first_one:
                        add_rows(e_here - 1, e - 1)
                    for i in range(4, 6):
                        split(i, M + i, s0)
                    act_product(a0 + 1, M + s0 + 4)
                    dve.wait_ge(sem("dispatchT_done"), e + 1)
                    V.tensor_copy(dispT[:], ps[:, 3, 0:C * P]).then_inc(sem("dispatchT_ready"), 1)
                    if not last_one:
                        dve.wait_ge(sem("gathered"), gathers)
                        dispatch(e_here + 1)

                    def step(f, s, first=False):
                        for i in range(2 if first else 0, 4):
                            split(4 + i, M + 4 + i, s)
                        act_low(a0 + f)
                        split(8, M + 8, s)
                        if first and not last_one:
                            scale_gathered(gathers + 1)
                        split(9, M + 9, s)
                        act_product(a0 + f + 1, M + s + 8)

                    step(1, s0, True)
                    with dve.Fori(2, NFE) as f:
                        step(f, s0 + 6 * (f - 1))
                    split(4, M + MOE_TILES - 2, s0)
                    if not last_one:
                        gathered_low(gathers + 1)
                    split(5, M + MOE_TILES - 1, s0)
                    act_low(a0 + NFE)
                    if not last_one:
                        for i in range(2):
                            split(i, M + i, s0 + MOE_TILES)
                    dve.wait_ge(sem("y_hi_ready"), e + 1)
                    V.tensor_tensor(y_lo[:], ps[:, 4:6, :].rearrange("p b n -> p (b n)"), y_hi[:].bitcast(F32),
                                    ALU.subtract).then_inc(sem("y_ready"), 1)
                    if last_one:
                        add_rows(e_here, e)
                    else:
                        split(2, M + 2, s0 + MOE_TILES)

                def one_pass(base, gathers):
                    dispatch(0)
                    if base:
                        for i in range(3):
                            split(i, FFN_TILES + i, MOE_TILES * base)
                    scale_gathered(gathers + 1)
                    gathered_low(gathers + 1)
                    expert(0, base, gathers + 1, True, False)
                    with dve.Fori(1, NE - 1) as e:
                        expert(e, e + base, e + gathers + 1, False, False)
                    expert(NE - 1, base + NE - 1, gathers + NE, False, True)

                dve.wait_ge(sem("routed"), 1)
                one_pass(0, 0)
                busiest = dve.value_load(most[0:1, 0:1])
                with dve.If(busiest > P):
                    V.tensor_scalar(slot_of[:], slot_of[:], float(P), None, ALU.subtract).then_inc(sem("slots_moved"), 1)
                    dve.wait_ge(sem("slots_moved"), 1)
                    one_pass(NE, NE)
                V.memset(rstat[:, 0:1], 0.0).then_inc(sem("x_final"), 1)

            setup()
            constants()
            for l in range(L):
                ssm_setup(l)
                ssm(l)
                attention_inputs(l)
                cols[0] += CT
                attention(l)
                merge(l)
                if l == 0:
                    dense()
            experts()


_INS = ['x', 'mem', 'positions', 'norm_mix', 'w_in', 'ssm_a_re', 'ssm_a_im', 'ssm_log_dt', 'ssm_b_re', 'ssm_b_im',
        'ssm_c_re', 'ssm_c_im', 'ssm_d', 'ssm_w_glu', 'w_ssm_out', 'att_q_norm', 'att_k_norm', 'w_att_out',
        'norm_mem', 'w_mem_kv', 'mem_q_norm', 'mem_k_norm', 'w_mem_out', 'w_o', 'norm_ffn', 'ffn_w_gate',
        'ffn_w_up', 'ffn_w_down', 'moe_w_router', 'moe_w_gate', 'moe_w_up', 'moe_w_down']


def kernel(**inputs):
    import numpy as _np
    import concourse.bacc as _bacc
    from concourse import mybir as _mybir
    from concourse.bass_utils import run_bass_kernel_spmd as _run

    nc = _bacc.Bacc("TRN2", target_bir_lowering=False, num_devices=1)
    arrays, args = {}, []
    for name in _INS:
        a = _np.ascontiguousarray(inputs[name])
        arrays[f"in_{name}"] = a
        args.append(nc.dram_tensor(f"in_{name}", a.shape, _mybir.dt.from_np(a.dtype), kind="ExternalInput").ap())
    shape = inputs["x"].shape
    args.append(nc.dram_tensor("out", shape, _mybir.dt.float32, kind="ExternalOutput").ap())
    decoder_trunk(nc, *args)
    r = _run(nc, [arrays], core_ids=[0])
    return r.results[0]["out"]
```
